# Optimizing a Trainium2 kernel written in Bass

```python
import math
import jax, jax.numpy as jnp
from jax import lax
import numpy as np

D_MODEL = 1024
BATCH = 1
SEQ = 1024
DEPTH = 1
DEC_BATCH = 8
DEC_SEQ = 8
PAST_LEN = 4096
PAGE_SIZE = 128

N_HEADS = 8
N_KV = 2
REP = N_HEADS // N_KV
HEAD_DIM = 64
Q_WIDTH = N_HEADS * HEAD_DIM
KV_WIDTH = N_KV * HEAD_DIM
WINDOW = 128
ATT_BLOCK = 128
W_BUF = min(WINDOW, PAST_LEN)
N_BUCKETS = 32
MAX_DISTANCE = 128
C_GROUPS = 4
C_CHUNK = 128
C_WIDTH = 512
C_GDIM = C_WIDTH // C_GROUPS
PLE_DIM = 256
PEER_HEADS = 8
N_KEYS = 128
N_EXPERTS = N_KEYS * N_KEYS
PEER_TOPK = 16
PEER_DKEY = 256
PEER_DHALF = PEER_DKEY // 2
PEER_BLOCK = 128
IN_WIDTH = Q_WIDTH + 2 * KV_WIDTH + 2 * C_WIDTH + 2 * D_MODEL
ALPHA = (2.0 * DEPTH) ** 0.25
BETA = (8.0 * DEPTH) ** -0.25
LN_EPS = 1e-5
NEG = -1e30

kernel_name = 'hybrid_swa_sink_gmlp_peer_step'

def layer_norm(x, g, b):
    xf = x.astype(jnp.float32)
    mu = xf.mean(-1, keepdims=True)
    var = jnp.mean(jnp.square(xf - mu), -1, keepdims=True)
    return ((xf - mu) * lax.rsqrt(var + LN_EPS)).astype(x.dtype) * g + b

def split_in(z):
    idx = np.cumsum([Q_WIDTH, KV_WIDTH, KV_WIDTH, C_WIDTH, C_WIDTH, D_MODEL]).tolist()
    return jnp.split(z, idx, axis=-1)

def t5_bias(dist, table):
    n = jnp.maximum(dist, 0)
    max_exact = N_BUCKETS // 2
    nf = jnp.maximum(n, 1).astype(jnp.float32)
    large = max_exact + (jnp.log(nf / max_exact) / math.log(MAX_DISTANCE / max_exact)
                         * (N_BUCKETS - max_exact)).astype(jnp.int32)
    large = jnp.minimum(large, N_BUCKETS - 1)
    bucket = jnp.where(n < max_exact, n, large)
    return jnp.moveaxis(table[bucket], -1, 0)

def prompt_band_pattern(table):
    nb = SEQ // ATT_BLOCK
    qi = jnp.arange(ATT_BLOCK)[:, None]
    kj = jnp.arange(2 * ATT_BLOCK)[None, :]
    dist = qi - kj + ATT_BLOCK
    kpos = jnp.arange(nb)[:, None, None] * ATT_BLOCK - ATT_BLOCK + kj[None]
    mask = (dist >= 0) & (dist < WINDOW) & (kpos >= 0)
    return t5_bias(dist, table), mask

def sample_band_pattern(table, n_new):
    qi = jnp.arange(n_new)[:, None]
    kj = jnp.arange(W_BUF + n_new)[None, :]
    dist = qi - (kj - W_BUF)
    mask = (dist >= 0) & (dist < WINDOW)
    return t5_bias(dist, table), mask

def banded_attention(q, k, v, mask, bias, sinks):
    s = jnp.einsum('bnqgrd,bnkgd->bngrqk', q, k).astype(jnp.float32) * (HEAD_DIM ** -0.5)
    s = s + bias.astype(jnp.float32).reshape(N_KV, REP, *bias.shape[1:])[None, None]
    s = jnp.where(mask[None, :, None, None], s, NEG)
    sink = sinks.astype(jnp.float32).reshape(N_KV, REP)[None, None, :, :, None]
    m = jnp.maximum(s.max(-1), sink)
    e = jnp.exp(s - m[..., None])
    w = e / (e.sum(-1) + jnp.exp(sink - m))[..., None]
    return jnp.einsum('bngrqk,bnkgd->bnqgrd', w.astype(v.dtype), v)

def shift_block(t):
    return jnp.pad(t, ((0, 0), (1, 0), (0, 0), (0, 0), (0, 0)))[:, :-1]

def attn_prompt(q, k, v, sinks, bias, mask):
    B, T = q.shape[:2]
    nb = T // ATT_BLOCK
    qb = q.reshape(B, nb, ATT_BLOCK, N_KV, REP, HEAD_DIM)
    kb = k.reshape(B, nb, ATT_BLOCK, N_KV, HEAD_DIM)
    vb = v.reshape(B, nb, ATT_BLOCK, N_KV, HEAD_DIM)
    kk = jnp.concatenate([shift_block(kb), kb], axis=2)
    vv = jnp.concatenate([shift_block(vb), vb], axis=2)
    o = banded_attention(qb, kk, vv, mask, bias, sinks)
    return o.reshape(B, T, Q_WIDTH)

def attn_sample(q, k, v, k_cache, v_cache, sinks, bias, mask):
    Bd, S = q.shape[:2]
    k_all = jnp.concatenate([k_cache, k.reshape(Bd, S, N_KV, HEAD_DIM)], axis=1)
    v_all = jnp.concatenate([v_cache, v.reshape(Bd, S, N_KV, HEAD_DIM)], axis=1)
    o = banded_attention(q.reshape(Bd, 1, S, N_KV, REP, HEAD_DIM), k_all[:, None], v_all[:, None],
                         mask[None], bias, sinks)
    return o.reshape(Bd, S, Q_WIDTH), k_all[:, -W_BUF:], v_all[:, -W_BUF:]

def chunk_prompt(u, v, ws, bs):
    B, T = v.shape[:2]
    nc = T // C_CHUNK
    vb = v.reshape(B, nc, C_CHUNK, C_GROUPS, C_GDIM)
    wm = ws * jnp.tril(jnp.ones((C_CHUNK, C_CHUNK), ws.dtype))
    s = jnp.einsum('gts,bcsgd->bctgd', wm, vb) + bs.T[:, :, None]
    return u * s.reshape(B, T, C_WIDTH)

def chunk_sample(u, v, ws, bs):
    Bd, S = v.shape[:2]
    wm = (ws * jnp.tril(jnp.ones((C_CHUNK, C_CHUNK), ws.dtype)))[:, :S, :S]
    s = jnp.einsum('gts,bsgd->btgd', wm, v.reshape(Bd, S, C_GROUPS, C_GDIM)) + bs[:, :S].T[:, :, None]
    return u * s.reshape(Bd, S, C_WIDTH)

def peer_ffn(x, wq, subkeys, u_tab, v_tab):
    shp = x.shape
    xf = x.reshape(-1, D_MODEL)
    T = xf.shape[0]
    nblk = -(-T // PEER_BLOCK)
    xp = jnp.pad(xf, ((0, nblk * PEER_BLOCK - T), (0, 0))).reshape(nblk, PEER_BLOCK, D_MODEL)

    def block(xb):
        q = (xb @ wq).reshape(PEER_BLOCK, PEER_HEADS, 2, PEER_DHALF)
        s = jnp.einsum('thcd,hcnd->thcn', q, subkeys).astype(jnp.float32)
        sv, si = lax.top_k(s, PEER_TOPK)
        cand = (sv[:, :, 0, :, None] + sv[:, :, 1, None, :]).reshape(PEER_BLOCK, PEER_HEADS, PEER_TOPK * PEER_TOPK)
        fv, fi = lax.top_k(cand, PEER_TOPK)
        i1 = jnp.take_along_axis(si[:, :, 0], fi // PEER_TOPK, axis=-1)
        i2 = jnp.take_along_axis(si[:, :, 1], fi % PEER_TOPK, axis=-1)
        e = i1 * N_KEYS + i2
        g = jax.nn.softmax(fv, axis=-1)
        a = jax.nn.gelu(jnp.einsum('thkd,td->thk', u_tab[e], xb))
        return jnp.einsum('thk,thkd->td', (g * a).astype(v_tab.dtype), v_tab[e])

    y = lax.map(block, xp).reshape(-1, D_MODEL)[:T]
    return y.reshape(shp)

def finish_layer(x, p, ya, yc, ga, gc, wa, wc, wo, l1g, l1b, pwq, psk, pu, pv, wpg, wpp, l2g, l2b):
    mix = jax.nn.sigmoid(ga) * (ya @ wa) + jax.nn.sigmoid(gc) * (yc @ wc)
    x1 = layer_norm(ALPHA * x + mix @ wo, l1g, l1b)
    f = peer_ffn(x1, pwq, psk, pu, pv)
    e = jax.nn.sigmoid(x1 @ wpg) * (p @ wpp)
    return layer_norm(ALPHA * x1 + f + e, l2g, l2b)

def setup_inputs(seed: int = 0) -> dict:
    key = jax.random.key(seed)
    ks = list(jax.random.split(key, 28))

    def nrm(shape, scale):
        return jax.random.normal(ks.pop(), shape, jnp.float32) * scale

    L = DEPTH
    return {
        'x_prompt': nrm((BATCH, SEQ, D_MODEL), 1.0),
        'x_sample': nrm((DEC_BATCH, DEC_SEQ, D_MODEL), 1.0),
        'cache_k_win': nrm((L, DEC_BATCH, W_BUF, N_KV, HEAD_DIM), 1.0),
        'cache_v_win': nrm((L, DEC_BATCH, W_BUF, N_KV, HEAD_DIM), 1.0),
        'p_prompt': nrm((L, BATCH, SEQ, PLE_DIM), 1.0),
        'p_sample': nrm((L, DEC_BATCH, DEC_SEQ, PLE_DIM), 1.0),
        'rel_bias_table': nrm((N_BUCKETS, N_HEADS), 0.5),
        'w_in': nrm((L, D_MODEL, IN_WIDTH), D_MODEL ** -0.5),
        'attn_sinks': nrm((L, N_HEADS), 1.0),
        'w_att_out': nrm((L, Q_WIDTH, D_MODEL), Q_WIDTH ** -0.5),
        'c_ln_g': 1.0 + nrm((L, C_WIDTH), 0.05),
        'c_ln_b': nrm((L, C_WIDTH), 0.05),
        'c_ws': nrm((L, C_GROUPS, C_CHUNK, C_CHUNK), C_CHUNK ** -0.5),
        'c_bs': 1.0 + nrm((L, C_GROUPS, C_CHUNK), 0.1),
        'w_chunk_out': nrm((L, C_WIDTH, D_MODEL), C_WIDTH ** -0.5),
        'w_o': nrm((L, D_MODEL, D_MODEL), BETA * D_MODEL ** -0.5),
        'ln1_g': 1.0 + nrm((L, D_MODEL), 0.05),
        'ln1_b': nrm((L, D_MODEL), 0.05),
        'peer_wq': nrm((L, D_MODEL, PEER_HEADS * PEER_DKEY), D_MODEL ** -0.5),
        'peer_subkeys': nrm((L, PEER_HEADS, 2, N_KEYS, PEER_DHALF), PEER_DHALF ** -0.5),
        'peer_u': nrm((L, N_EXPERTS, D_MODEL), D_MODEL ** -0.5),
        'peer_v': nrm((L, N_EXPERTS, D_MODEL), BETA),
        'w_ple_gate': nrm((L, D_MODEL, D_MODEL), D_MODEL ** -0.5),
        'w_ple_proj': nrm((L, PLE_DIM, D_MODEL), BETA * PLE_DIM ** -0.5),
        'ln2_g': 1.0 + nrm((L, D_MODEL), 0.05),
        'ln2_b': nrm((L, D_MODEL), 0.05),
    }

def reference(x_prompt, x_sample, cache_k_win, cache_v_win, p_prompt, p_sample, rel_bias_table,
              w_in, attn_sinks, w_att_out, c_ln_g, c_ln_b, c_ws, c_bs, w_chunk_out, w_o,
              ln1_g, ln1_b, peer_wq, peer_subkeys, peer_u, peer_v, w_ple_gate, w_ple_proj,
              ln2_g, ln2_b):
    bias_p, mask_p = prompt_band_pattern(rel_bias_table)
    bias_s, mask_s = sample_band_pattern(rel_bias_table, x_sample.shape[1])
    xp, xs = x_prompt, x_sample
    kp_l, vp_l, ks_l, vs_l, cs_l = [], [], [], [], []
    for i in range(DEPTH):
        shared = (w_att_out[i], w_chunk_out[i], w_o[i], ln1_g[i], ln1_b[i], peer_wq[i],
                  peer_subkeys[i], peer_u[i], peer_v[i], w_ple_gate[i], w_ple_proj[i],
                  ln2_g[i], ln2_b[i])
        q, k, v, cu, cv, ga, gc = split_in(xp @ w_in[i])
        cv = layer_norm(cv, c_ln_g[i], c_ln_b[i])
        ya = attn_prompt(q, k, v, attn_sinks[i], bias_p, mask_p)
        yc = chunk_prompt(cu, cv, c_ws[i], c_bs[i])
        kp_l.append(k.reshape(k.shape[0], k.shape[1], N_KV, HEAD_DIM)[:, -W_BUF:])
        vp_l.append(v.reshape(v.shape[0], v.shape[1], N_KV, HEAD_DIM)[:, -W_BUF:])
        xp = finish_layer(xp, p_prompt[i], ya, yc, ga, gc, *shared)
        q, k, v, cu, cv, ga, gc = split_in(xs @ w_in[i])
        cv = layer_norm(cv, c_ln_g[i], c_ln_b[i])
        ya, k_new, v_new = attn_sample(q, k, v, cache_k_win[i], cache_v_win[i], attn_sinks[i], bias_s, mask_s)
        yc = chunk_sample(cu, cv, c_ws[i], c_bs[i])
        ks_l.append(k_new)
        vs_l.append(v_new)
        cs_l.append(cv)
        xs = finish_layer(xs, p_sample[i], ya, yc, ga, gc, *shared)
    return (xp, xs, jnp.stack(kp_l), jnp.stack(vp_l), jnp.stack(ks_l), jnp.stack(vs_l), jnp.stack(cs_l))


_drawn_inputs = setup_inputs


def setup_inputs(seed=0):
    import zlib

    import numpy as np

    out = dict(_drawn_inputs(seed))
    spreads = {}
    factors = {'attn_sinks': 8.0}
    for name, (base, spread) in spreads.items():
        noise = np.random.default_rng([zlib.crc32(name.encode()), seed]).standard_normal(out[name].shape)
        drawn = base * np.exp(spread * noise) if base else spread * noise
        out[name] = __import__('jax').numpy.asarray(drawn.astype(out[name].dtype))
    for name, factor in factors.items():
        out[name] = (out[name] * factor).astype(out[name].dtype)
    return out
```

```python
import math
from contextlib import ExitStack

import numpy as np

import concourse.bass as bass
from concourse import mybir

F32 = mybir.dt.float32
F16 = mybir.dt.float16
U32 = mybir.dt.uint32
ALU = mybir.AluOpType
ACT = mybir.ActivationFunctionType
X = mybir.AxisListType.X

P = 128
D = 1024
KT = D // P
PROMPT, SAMPLE = 1024, 64
T = PROMPT + SAMPLE
NB = PROMPT // P
SEQS, NEW = 8, 8
HEADS, GROUPS, REP, HD = 8, 2, 4, 64
QW, KVW, CW = 512, 128, 512
CG = 4
IN_W = QW + 2 * KVW + 2 * CW + 2 * D
PLE = 256
PH, HALVES, KEYS, TOPK = 8, 2, 128, 16
HK = PH * TOPK
NEG = -1e30
LOWEST = -3.0e38
ALPHA = 2.0 ** 0.25
EPS = 1e-5
BUCKETS, MAX_DISTANCE = 32, 128
TOEP = 384
ZK, ZKV, ZU, ZV, ZG, ZW = 512, 640, 896, 1408, 1920, 3968

SU, SV, SH, SG = 64.0, 16.0, 64.0, 32768.0


def over_blocks(eng, body):
    with eng.Fori(0, NB // 2) as i:
        body(i * 2, 0)
        body(i * 2 + 1, 1)
    body(NB, 0)


def rows_of(n):
    return SAMPLE if isinstance(n, int) and n == NB else P


class Space:

    def __init__(self, nc, stack, stage):
        self.nc, self.stack, self.stage = nc, stack, stage

    def sb(self, name, shape, dt=F32):
        return self.stack.enter_context(self.nc.sbuf_tensor(f"{self.stage}_{name}", shape, dt))

    def psum(self, name, shape, dt=F32):
        return self.stack.enter_context(self.nc.psum_tensor(f"{self.stage}_{name}", shape, dt))

    def sem(self, name):
        return self.stack.enter_context(self.nc.semaphore(f"{self.stage}_{name}"))

    def sems(self, name, n):
        return [self.sem(f"{name}{i}") for i in range(n)]


def layer_norm_stats(dve, src, rows, stats, mv, var_ready, rstd_ready, count):
    for c, part in enumerate(src):
        dve.bn_stats(stats[:rows, c, :], part)
    dve.drain()
    dve.bn_aggr(mv[:rows, :], stats[:rows, 0:len(src), :])
    dve.drain()
    dve.tensor_scalar(mv[:rows, 1:2], mv[:rows, 1:2], EPS, None, ALU.add).then_inc(var_ready, 1)
    dve.wait_ge(rstd_ready, count)


def inverse_deviation(pool, rows, mv, power, rstd, var_ready, rstd_ready, count):
    pool.wait_ge(var_ready, count)
    pool.tensor_tensor(rstd[:rows, :], mv[:rows, 1:2], power[:rows, :], ALU.pow).then_inc(rstd_ready, 1)


def bias_stage(nc, a):
    with ExitStack() as stack:
        s = Space(nc, stack, "bias")
        table = s.sb("table", [BUCKETS, HEADS])
        onehot = s.sb("onehot", [BUCKETS, TOEP])
        outside = s.sb("outside", [HEADS, TOEP])
        rev = s.sb("rev", [HEADS, TOEP])
        zero = s.sb("zero", [P, ZW])
        ps = s.psum("ps", [HEADS, TOEP])
        loaded, product, made, stored = s.sem("loaded"), s.sem("product"), s.sem("made"), s.sem("stored")
        zeroed = s.sem("zeroed")
        with nc.Block() as block:

            @block.sync
            def _(sp):
                sp.dma_start(table[:], a.rel_bias_table).then_inc(loaded, 16)
                sp.dma_start(onehot[:], a.c_bucket).then_inc(loaded, 16)
                sp.dma_start(outside[:], a.c_outside).then_inc(loaded, 16)
                sp.wait_ge(made, 1)
                sp.dma_start(a.rev, rev[:].unsqueeze(1).broadcast_to([HEADS, P, TOEP])).then_inc(stored, 16)
                sp.wait_ge(zeroed, 1)
                sp.dma_start(a.z[0], zero[:]).then_inc(stored, 16)
                sp.wait_ge(stored, 32)

            @block.tensor
            def _(pe):
                pe.wait_ge(loaded, 48)
                pe.matmul(ps[:], table[:], onehot[:], start=True, stop=True).then_inc(product, 1)

            @block.vector
            def _(dve):
                dve.wait_ge(loaded, 48)
                dve.wait_ge(product, 1)
                dve.tensor_tensor(rev[:], ps[:], outside[:], ALU.add).then_inc(made, 1)

            @block.gpsimd
            def _(pool):
                pool.memset(zero[:], 0.0).then_inc(zeroed, 1)


def project_stage(nc, a):
    with ExitStack() as stack:
        s = Space(nc, stack, "project")
        w = s.sb("w", [P, KT, IN_W])
        xt = s.sb("xt", [P, 2, KT, P])
        z = s.sb("z", [P, 2, ZW])
        gain = s.sb("gain", [P, CW])
        shift = s.sb("shift", [P, CW])
        stats, mv, rstd = s.sb("stats", [P, 1, 6]), s.sb("mv", [P, 2]), s.sb("rstd", [P, 1])
        power = s.sb("power", [P, 1])
        ps = s.psum("ps", [P, 8, 512])
        w_cols = [(0, 512), (512, 768), (768, 1280), (1280, 1792)] + [(1792 + 512 * j, 2304 + 512 * j) for j in range(4)]
        w_loaded = s.sems("w_loaded", 8)
        const_loaded = s.sem("const_loaded")
        x_loaded = s.sems("x_loaded", 2)
        bank_full = s.sems("bank_full", 8)
        bank_read = s.sems("bank_read", 8)
        z_act, z_dve = s.sem("z_act"), s.sem("z_dve")
        z_stored = s.sems("z_stored", 2)
        var_ready, rstd_ready = s.sem("var_ready"), s.sem("rstd_ready")
        with nc.Block() as block:

            @block.sync
            def _(sp):
                sp.dma_start(xt[:, 0], a.xt_blocks[0]).then_inc(x_loaded[0], 16)
                for j, (c0, c1) in enumerate(w_cols):
                    sp.dma_start(w[:, :, c0:c1], a.w_in[:, :, c0:c1]).then_inc(w_loaded[j], 16)
                sp.dma_start(gain[:], a.c_ln_g).then_inc(const_loaded, 16)
                sp.dma_start(shift[:], a.c_ln_b).then_inc(const_loaded, 16)

                def load(n, slot):
                    sp.dma_start(xt[:, slot], a.xt_blocks[bass.ds(n, 1)]).then_inc(x_loaded[slot], 16)

                def store(n, slot):
                    sp.wait_ge(z_act, n + 1)
                    sp.wait_ge(z_dve, n + 1)
                    sp.dma_start(a.z[bass.ds(n + 1, 1)], z[:, slot]).then_inc(z_stored[slot], 16)

                with sp.Fori(0, NB // 2) as i:
                    for slot in range(2):
                        n = i * 2 + slot
                        sp.wait_ge(bank_full[7], n + 1)
                        load(n + 1, 1 - slot)
                        store(n, slot)
                store(NB, 0)
                sp.wait_ge(z_stored[0], 16 * (NB // 2 + 2))
                sp.wait_ge(z_stored[1], 16 * (NB // 2 + 1))

            @block.tensor
            def _(pe):
                pe.sem_inc(bank_full[7], 1)

                def body(n, slot):
                    r = rows_of(n)
                    pe.wait_ge(x_loaded[slot], (n - slot) * 8 + 16)
                    for bank in range(8):
                        pe.wait_ge(bank_read[bank], n + 1)
                        pe.wait_ge(w_loaded[bank], 16)
                        q_tiles = [(j * P, j * P) for j in range(4)]
                        for o, c in (q_tiles, [(0, QW)])[bank] if bank < 2 else ():
                            for k in range(KT):
                                mm = pe.matmul(ps[:, bank, o:o + r], w[:, k, c:c + P], xt[:, slot, k, :r],
                                               start=k == 0, stop=k == KT - 1)
                        c0, c1 = w_cols[bank]
                        o = 0 if bank > 1 else P
                        if bank:
                            for k in range(KT):
                                mm = pe.matmul(ps[:r, bank, o:o + c1 - c0], xt[:, slot, k, :r], w[:, k, c0:c1],
                                               start=k == 0, stop=k == KT - 1)
                        mm.then_inc(bank_full[bank], 1)

                over_blocks(pe, body)

            @block.scalar
            def _(act):
                for bank in (0, 2, 4, 5, 6, 7):
                    act.sem_inc(bank_read[bank], 1)

                def body(n, slot):
                    r = rows_of(n)
                    act.wait_ge(z_stored[slot], (n - slot) * 8 + 16)
                    act.wait_ge(bank_full[0], n + 1)
                    act.activation(z[:, slot, 0:QW].rearrange("p (j t) -> p j t", j=4)[:, :, :r],
                                   ps[:, 0, :].rearrange("p (j t) -> p j t", j=4)[:, :, :r],
                                   ACT.Copy).then_inc(bank_read[0], 1)
                    act.wait_ge(bank_full[2], n + 1)
                    act.activation(z[:r, slot, ZU:ZV], ps[:r, 2, :], ACT.Copy).then_inc(bank_read[2], 1)
                    for j in range(4):
                        if j == 3:
                            act.wait_ge(bank_full[7], n + 2)
                        else:
                            act.wait_ge(bank_full[4 + j], n + 1)
                        act.activation(z[:r, slot, ZG + 512 * j:ZG + 512 * j + 512], ps[:r, 4 + j, :],
                                       ACT.Tanh, scale=0.5).then_inc(bank_read[4 + j], 1)
                    act.drain().then_inc(z_act, 1)

                over_blocks(act, body)

            @block.gpsimd
            def _(pool):
                pool.memset(power[:], -0.5)
                pool.memset(z[:], 0.0)
                pool.drain()
                pool.sem_inc(z_stored[0], 16)
                pool.sem_inc(z_stored[1], 16)
                over_blocks(pool, lambda n, slot: inverse_deviation(pool, rows_of(n), mv, power, rstd, var_ready, rstd_ready, n + 1))

            @block.vector
            def _(dve):
                for bank in (1, 3):
                    dve.sem_inc(bank_read[bank], 1)
                dve.wait_ge(const_loaded, 32)

                def body(n, slot):
                    r = rows_of(n)
                    dve.wait_ge(z_stored[slot], (n - slot) * 8 + 16)
                    dve.wait_ge(bank_full[1], n + 1)
                    dve.tensor_copy(z[:, slot, ZK:ZK + r], ps[:, 1, 0:r])
                    dve.tensor_copy(z[:r, slot, ZKV:ZU], ps[:r, 1, P:P + 2 * KVW]).then_inc(bank_read[1], 1)
                    dve.wait_ge(bank_full[3], n + 1)
                    layer_norm_stats(dve, [ps[:r, 3, :]], r, stats, mv, var_ready, rstd_ready, n + 1)
                    out = z[:r, slot, ZV:ZG]
                    dve.tensor_scalar(out, ps[:r, 3, :], mv[:r, 0:1], rstd[:r, :], ALU.subtract,
                                      ALU.mult).then_inc(bank_read[3], 1)
                    dve.drain()
                    dve.tensor_tensor(out, out, gain[:r, :], ALU.mult)
                    dve.drain()
                    dve.tensor_tensor(out, out, shift[:r, :], ALU.add)
                    dve.drain().then_inc(z_dve, 1)

                over_blocks(dve, body)


def mix_prompt_stage(nc, a):
    with ExitStack() as stack:
        s = Space(nc, stack, "mix")
        za = s.sb("za", [P, 2, ZG])
        prev = s.sb("prev", [P, 2, 3 * P])
        bias = s.sb("bias", [P, HEADS, 2 * P])
        sink = s.sb("sink", [P, HEADS])
        ident = s.sb("ident", [P, P])
        ws = s.sb("ws", [P, CG, P])
        tril = s.sb("tril", [P, P])
        bs = s.sb("bs", [P, CG])
        sc = s.sb("sc", [P, HEADS, 2 * P])
        m, negm, total, esink, dsink = (s.sb(x, [P, HEADS]) for x in ("m", "negm", "total", "esink", "dsink"))
        prT = s.sb("prT", [P, 2 * HEADS, P])
        yc = s.sb("yc", [P, CW])
        yt = s.sb("yt", [P, 2, 8, P])
        ps = s.psum("ps", [P, 8, 512])
        const_loaded, ws_ready = s.sem("const_loaded"), s.sem("ws_ready")
        loaded = s.sems("loaded", 2)
        left_loaded = s.sem("left_loaded")
        biased = s.sem("biased")
        scores_full = s.sem("scores_full")
        maxed = s.sem("maxed")
        exped = s.sem("exped")
        normed = s.sem("normed")
        gm_full, yc_ready, ycT_full, ycT_read = (s.sem(x) for x in ("gm_full", "yc_ready", "ycT_full", "ycT_read"))
        prT_full, prT_read = s.sems("prT_full", 4), s.sems("prT_read", 4)
        ya_full, ya_read = s.sem("ya_full"), s.sem("ya_read")
        y_stored = s.sems("y_stored", 2)

        with nc.Block() as block:

            def toeplitz(k0):
                return bass.AP(a.rev.tensor, k0 + P - 1, [[TOEP - 1, P], [P * TOEP, HEADS], [1, P]])

            @block.sync
            def _(sp):
                def load(n, slot):
                    sp.dma_start(za[:, slot], a.z[bass.ds(n + 1, 1), :, 0:ZG]).then_inc(loaded[slot], 16)
                    sp.dma_start(prev[:, slot, 0:3 * P], a.z[bass.ds(n, 1), :, ZK:ZK + 3 * P]).then_inc(loaded[slot], 16)

                load(0, 0)
                for dst, src in ((ident, a.c_ident), (ws, a.wsT), (tril, a.c_tril), (bs, a.bsT), (sink, a.sink_rows),
                                 (bias[:, :, P:2 * P], toeplitz(P))):
                    sp.dma_start(dst[:], src).then_inc(const_loaded, 16)
                with sp.Fori(0, NB // 2) as i:
                    for slot in range(2):
                        n = i * 2 + slot
                        if slot == 0:
                            sp.wait_ge(y_stored[1], i * 16 + 16)
                            load(n + 1, 1)
                        else:
                            sp.wait_ge(y_stored[0], i * 16 + 32)
                            load(n + 1, 0)
                        sp.wait_ge(biased, n + 1)
                        sp.dma_start(bias[:, :, 0:P], toeplitz(0)).then_inc(left_loaded, 16)
                        sp.wait_ge(ya_read, n + 2)
                        sp.wait_ge(ycT_read, n + 2)
                        sp.dma_start(a.yT[bass.ds(n, 1)], yt[:, slot]).then_inc(y_stored[slot], 16)
                sp.dma_start(a.k_prompt, a.z[NB, :, ZKV:ZKV + KVW]).then_inc(const_loaded, 16)
                sp.dma_start(a.v_prompt, a.z[NB, :, ZKV + KVW:ZU]).then_inc(const_loaded, 16)
                sp.wait_ge(const_loaded, 8 * 16)
                for slot in range(2):
                    sp.wait_ge(y_stored[slot], 16 * (NB // 2 + 1))
                sp.wait_ge(loaded[0], 32 * (NB // 2 + 1))
                sp.wait_ge(left_loaded, 16 * (NB + 1))

            @block.tensor
            def _(pe):
                pe.wait_ge(const_loaded, 6 * 16)

                def body(n, slot):
                    pe.wait_ge(loaded[slot], (n - slot) * 16 + 32)
                    pe.wait_ge(ya_read, n + 1)
                    for h in range(HEADS):
                        g, r = divmod(h, REP)
                        lo = g * HD
                        for half in range(2):
                            kT = prev[lo:lo + HD, slot, 0:P] if half == 0 else za[lo:lo + HD, slot, ZK:ZK + P]
                            mm = pe.matmul(ps[:, h // 2, (h % 2) * 256 + half * P:(h % 2) * 256 + half * P + P],
                                           za[lo:lo + HD, slot, r * P:(r + 1) * P], kT, start=True, stop=True)
                    mm.then_inc(scores_full, 1)
                    pe.wait_ge(ws_ready, 1)
                    pe.wait_ge(prT_read[0], n + 1)
                    for g in range(CG):
                        mm = pe.matmul(ps[:, 4, g * P:(g + 1) * P], ws[:, g, :],
                                       za[:, slot, ZV + g * P:ZV + (g + 1) * P], start=True, stop=True)
                    mm.then_inc(gm_full, 1)
                    pe.wait_ge(yc_ready, n + 1)
                    pe.wait_ge(prT_read[1], n + 1)
                    for g in range(CG):
                        mm = pe.transpose(ps[:, 5, g * P:(g + 1) * P], yc[:, g * P:(g + 1) * P], ident[:])
                    mm.then_inc(ycT_full, 1)
                    pe.wait_ge(normed, n + 1)
                    for q in range(4):
                        if q == 1:
                            pe.wait_ge(ycT_read, n + 2)
                        pe.wait_ge(prT_read[q], n + 1)
                        for j in range(4):
                            h, half = 2 * q + j // 2, j % 2
                            mm = pe.transpose(ps[:, 4 + q, j * P:(j + 1) * P], sc[:, h, half * P:(half + 1) * P], ident[:])
                        mm.then_inc(prT_full[q], 1)
                    for h in range(HEADS):
                        g, r = divmod(h, REP)
                        lo = g * HD
                        if h % 2 == 0:
                            pe.wait_ge(prT_read[h // 2], n + 2)
                        pe.matmul(ps[lo:lo + HD, 0, r * P:(r + 1) * P], prev[:, slot, 2 * P + lo:2 * P + lo + HD],
                                  prT[:, 2 * h, :], start=True, stop=False)
                        mm = pe.matmul(ps[lo:lo + HD, 0, r * P:(r + 1) * P],
                                       za[:, slot, ZKV + KVW + lo:ZKV + KVW + lo + HD],
                                       prT[:, 2 * h + 1, :], start=False, stop=True)
                    mm.then_inc(ya_full, 1)

                with pe.Fori(0, NB // 2) as i:
                    body(i * 2, 0)
                    body(i * 2 + 1, 1)

            @block.scalar
            def _(act):
                act.sem_inc(ya_read, 1)
                act.sem_inc(prT_read[0], 1)
                act.sem_inc(prT_read[1], 1)
                act.sem_inc(y_stored[0], 16)
                act.sem_inc(y_stored[1], 16)

                def body(n, slot):
                    act.wait_ge(maxed, n + 1)
                    for h in range(HEADS):
                        act.activation(sc[:, h, :], sc[:, h, :], ACT.Exp, bias=negm[:, h:h + 1],
                                       accum_out=total[:, h:h + 1])
                    act.activation(esink[:], dsink[:], ACT.Exp)
                    act.drain().then_inc(exped, 1)
                    act.wait_ge(y_stored[slot], (n - slot) * 8 + 16)
                    for q in (0, 1):
                        act.wait_ge(prT_full[q], n + 1)
                        act.activation(prT[:, 4 * q:4 * q + 4, :], ps[:, 4 + q, :].rearrange("p (j t) -> p j t", j=4),
                                       ACT.Copy).then_inc(prT_read[q], 1)
                    act.wait_ge(ya_full, n + 1)
                    act.activation(yt[:, slot, 0:4, :], ps[:, 0, :].rearrange("p (j t) -> p j t", j=4),
                                   ACT.Copy).then_inc(ya_read, 1)

                with act.Fori(0, NB // 2) as i:
                    body(i * 2, 0)
                    body(i * 2 + 1, 1)

            @block.gpsimd
            def _(pool):
                pool.memset(bias[:, :, 0:P], NEG)
                pool.drain()
                pool.sem_inc(left_loaded, 16)

            @block.vector
            def _(dve):
                dve.sem_inc(prT_read[2], 1)
                dve.sem_inc(prT_read[3], 1)
                dve.sem_inc(ycT_read, 1)
                dve.wait_ge(const_loaded, 6 * 16)
                for g in range(CG):
                    last = dve.tensor_tensor(ws[:, g, :], ws[:, g, :], tril[:], ALU.mult)
                last.then_inc(ws_ready, 1)

                def body(n, slot):
                    dve.wait_ge(left_loaded, n * 16 + 16)
                    dve.wait_ge(scores_full, n + 1)
                    for q in range(4):
                        dve.scalar_tensor_tensor(sc[:, 2 * q:2 * q + 2, :], ps[:, q, :].rearrange("p (h k) -> p h k", h=2),
                                                 HD ** -0.5, bias[:, 2 * q:2 * q + 2, :], ALU.mult, ALU.add)
                    dve.drain().then_inc(biased, 1)
                    dve.tensor_reduce(m[:], sc[:], X, ALU.max)
                    dve.drain()
                    dve.tensor_tensor(m[:], m[:], sink[:], ALU.max)
                    dve.drain()
                    dve.tensor_scalar(negm[:], m[:], -1.0, None, ALU.mult)
                    dve.tensor_tensor(dsink[:], sink[:], m[:], ALU.subtract)
                    dve.drain().then_inc(maxed, 1)
                    dve.wait_ge(gm_full, n + 1)
                    for g in range(CG):
                        cols = slice(g * P, (g + 1) * P)
                        dve.scalar_tensor_tensor(yc[:, cols], ps[:, 4, cols], bs[:, g:g + 1],
                                                 za[:, slot, ZU + g * P:ZU + (g + 1) * P], ALU.add, ALU.mult)
                    dve.drain().then_inc(yc_ready, 1)
                    dve.wait_ge(ycT_full, n + 1)
                    dve.wait_ge(y_stored[slot], (n - slot) * 8 + 16)
                    dve.tensor_copy(yt[:, slot, 4:8, :], ps[:, 5, :].rearrange("p (j t) -> p j t", j=4)).then_inc(ycT_read, 1)
                    dve.wait_ge(exped, n + 1)
                    dve.tensor_tensor(total[:], total[:], esink[:], ALU.add)
                    dve.drain()
                    dve.reciprocal(total[:], total[:])
                    dve.drain()
                    dve.tensor_tensor(sc[:], sc[:], total[:].unsqueeze(2).broadcast_to([P, HEADS, 2 * P]), ALU.mult)
                    dve.drain().then_inc(normed, 1)
                    for q in (2, 3):
                        dve.wait_ge(prT_full[q], n + 1)
                        dve.tensor_copy(prT[:, 4 * q:4 * q + 4, :],
                                        ps[:, 4 + q, :].rearrange("p (j t) -> p j t", j=4)).then_inc(prT_read[q], 1)

                with dve.Fori(0, NB // 2) as i:
                    body(i * 2, 0)
                    body(i * 2 + 1, 1)


def mix_sample_stage(nc, a):
    S4 = SEQS // 4
    KA = P + NEW
    with ExitStack() as stack:
        s = Space(nc, stack, "smix")
        za = s.sb("za", [P, ZG])
        qs = s.sb("qs", [P, SEQS, REP, NEW])
        ckT = s.sb("ckT", [P, SEQS, P])
        cv = s.sb("cv", [P, SEQS, P])
        vnew = s.sb("vnew", [NEW, SEQS, P])
        bias = s.sb("bias", [P, GROUPS, KA])
        sink = s.sb("sink", [P, S4, GROUPS])
        ident = s.sb("ident", [P, P])
        ws = s.sb("ws", [SAMPLE, CG, SAMPLE])
        tril = s.sb("tril", [P, P])
        bs = s.sb("bs", [SAMPLE, CG])
        sc = s.sb("sc", [P, S4, GROUPS, KA])
        m, negm, total, esink, dsink = (s.sb(x, [P, S4, GROUPS]) for x in ("m", "negm", "total", "esink", "dsink"))
        prT = s.sb("prT", [P, S4 * GROUPS, P])
        prN = s.sb("prN", [NEW, S4 * GROUPS, P])
        yc = s.sb("yc", [SAMPLE, CW])
        yt = s.sb("yt", [P, 8, P])
        ps = s.psum("ps", [P, 8, 512])
        loaded, ws_ready, outs, q_ready = (s.sem(x) for x in ("loaded", "ws_ready", "outs", "q_ready"))
        names = ("scores_full", "maxed", "exped", "normed", "gm_full", "yc_ready", "ycT_full", "prT_full", "prT_read",
                 "ya_full", "y_act", "y_dve")
        scores_full, maxed, exped, normed, gm_full, yc_ready, ycT_full, prT_full, prT_read, ya_full, y_act, y_dve = map(s.sem, names)
        with nc.Block() as block:

            @block.sync
            def _(sp):
                sp.dma_start(za[:], a.z[NB + 1, :, 0:ZG]).then_inc(loaded, 16)
                sp.dma_start(ckT[:], a.cache_kT).then_inc(loaded, 16)
                sp.dma_start(cv[:], a.cache_v).then_inc(loaded, 16)
                sp.dma_start(vnew[:], a.z[NB + 1, 0:SAMPLE, ZKV + KVW:ZU].rearrange("(s j) c -> j s c", j=NEW)).then_inc(loaded, 16)
                sp.dma_start(ident[:], a.c_ident).then_inc(loaded, 16)
                sp.dma_start(tril[:], a.c_tril).then_inc(loaded, 16)
                sp.dma_start(bs[:], a.bs_sample).then_inc(loaded, 16)
                sp.dma_start(sink[:], a.sink_sample).then_inc(loaded, 16)
                sp.dma_start(ws[:], a.ws_sample).then_inc(loaded, 16)
                for q in range(4):
                    for r in range(REP):
                        row = q * 32 + r * NEW
                        sp.dma_start(bias[row:row + NEW, :, :],
                                     bass.AP(a.rev.tensor, r * P * TOEP + P - 1,
                                             [[TOEP - 1, NEW], [REP * P * TOEP, GROUPS], [1, KA]])).then_inc(loaded, 16)
                for win, cache, c0 in ((a.k_sample, a.cache_k_rows, ZKV), (a.v_sample, a.cache_v_rows, ZKV + KVW)):
                    sp.dma_start(win[:, 0:P - NEW, :], cache[:, NEW:P, :]).then_inc(outs, 16)
                    sp.dma_start(win[:, P - NEW:P, :],
                                 a.z[NB + 1, 0:SAMPLE, c0:c0 + KVW].rearrange("(s j) c -> s j c", j=NEW)).then_inc(outs, 16)
                sp.dma_start(a.chunk_v, a.z[NB + 1, 0:SAMPLE, ZV:ZG]).then_inc(outs, 16)
                sp.wait_ge(y_act, 1)
                sp.wait_ge(y_dve, 2)
                sp.dma_start(a.yT[NB], yt[:]).then_inc(outs, 16)
                sp.wait_ge(outs, 6 * 16)

            n_loads = 9 + 16

            @block.tensor
            def _(pe):
                pe.wait_ge(loaded, 16 * n_loads)
                pe.wait_ge(q_ready, 1)
                for b in range(SEQS):
                    quad, hi = b % 4, b // 4
                    for g in range(GROUPS):
                        rows = slice(g * HD, (g + 1) * HD)
                        q = qs[rows, b].rearrange("p r j -> p (r j)")
                        out = ps[quad * 32:(quad + 1) * 32, hi * GROUPS + g, :]
                        pe.matmul(out[:, 0:P], q, ckT[rows, b, :], start=True, stop=True)
                        mm = pe.matmul(out[:, P:KA], q, za[rows, ZK + b * NEW:ZK + (b + 1) * NEW],
                                       start=True, stop=True)
                mm.then_inc(scores_full, 1)
                pe.wait_ge(ws_ready, 1)
                for g in range(CG):
                    mm = pe.matmul(ps[0:SAMPLE, 4, g * P:(g + 1) * P], ws[:, g, :],
                                   za[0:SAMPLE, ZV + g * P:ZV + (g + 1) * P], start=True, stop=True)
                mm.then_inc(gm_full, 1)
                pe.wait_ge(yc_ready, 1)
                for g in range(CG):
                    mm = pe.transpose(ps[:, 5, g * P:g * P + SAMPLE], yc[:, g * P:(g + 1) * P], ident[0:SAMPLE, 0:SAMPLE])
                mm.then_inc(ycT_full, 1)
                pe.wait_ge(normed, 1)
                for j in range(S4 * GROUPS):
                    pr = sc[:, j // GROUPS, j % GROUPS, :]
                    pe.transpose(ps[:, 6, j * P:(j + 1) * P], pr[:, 0:P], ident[:])
                    mm = pe.transpose(ps[0:NEW, 7, j * P:(j + 1) * P], pr[:, P:KA], ident[:])
                mm.then_inc(prT_full, 1)
                pe.wait_ge(prT_read, 1)
                for b in range(SEQS):
                    quad, hi = b % 4, b // 4
                    for g in range(GROUPS):
                        out = ps[g * HD:(g + 1) * HD, 0, 0:REP * SAMPLE].rearrange("p (r t) -> p r t", r=REP)[:, :, b * NEW:(b + 1) * NEW]
                        j = hi * GROUPS + g
                        cols = slice(quad * 32, quad * 32 + 32)
                        pe.matmul(out, cv[:, b, g * HD:(g + 1) * HD], prT[:, j, cols].rearrange("p (r t) -> p r t", r=REP), start=True, stop=False)
                        mm = pe.matmul(out, vnew[:, b, g * HD:(g + 1) * HD], prN[:, j, cols].rearrange("p (r t) -> p r t", r=REP), start=False, stop=True)
                mm.then_inc(ya_full, 1)

            @block.scalar
            def _(act):
                act.wait_ge(loaded, 16 * n_loads)
                for r in range(REP):
                    act.activation(qs[:, :, r, :], za[:, r * P:r * P + SAMPLE].rearrange("p (s j) -> p s j", j=NEW), ACT.Copy)
                act.drain().then_inc(q_ready, 1)
                act.wait_ge(maxed, 1)
                for b in range(S4):
                    for g in range(GROUPS):
                        act.activation(sc[:, b, g, :], sc[:, b, g, :], ACT.Exp, bias=negm[:, b, g:g + 1],
                                       accum_out=total[:, b, g:g + 1])
                act.activation(esink[:], dsink[:], ACT.Exp)
                act.drain().then_inc(exped, 1)
                act.wait_ge(prT_full, 1)
                act.activation(prT[:], ps[:, 6, :].rearrange("p (j t) -> p j t", j=4), ACT.Copy)
                act.activation(prN[:], ps[0:NEW, 7, :].rearrange("p (j t) -> p j t", j=4), ACT.Copy)
                act.drain().then_inc(prT_read, 1)
                act.wait_ge(y_dve, 1)
                act.wait_ge(ya_full, 1)
                act.activation(yt[:, 0:4, 0:SAMPLE], ps[:, 0, 0:REP * SAMPLE].rearrange("p (r t) -> p r t", r=REP),
                               ACT.Copy).then_inc(y_act, 1)

            @block.vector
            def _(dve):
                dve.memset(yt[:], 0.0)
                dve.drain().then_inc(y_dve, 1)
                dve.wait_ge(loaded, 16 * n_loads)
                for g in range(CG):
                    last = dve.tensor_tensor(ws[:, g, :], ws[:, g, :], tril[0:SAMPLE, 0:SAMPLE], ALU.mult)
                last.then_inc(ws_ready, 1)
                dve.wait_ge(scores_full, 1)
                for b in range(S4):
                    dve.scalar_tensor_tensor(sc[:, b], ps[:, GROUPS * b:GROUPS * b + GROUPS, 0:KA],
                                             HD ** -0.5, bias[:], ALU.mult, ALU.add)
                dve.drain()
                dve.tensor_reduce(m[:], sc[:], X, ALU.max)
                dve.drain()
                dve.tensor_tensor(m[:], m[:], sink[:], ALU.max)
                dve.drain()
                dve.tensor_scalar(negm[:], m[:], -1.0, None, ALU.mult)
                dve.tensor_tensor(dsink[:], sink[:], m[:], ALU.subtract)
                dve.drain().then_inc(maxed, 1)
                dve.wait_ge(gm_full, 1)
                for g in range(CG):
                    cols = slice(g * P, (g + 1) * P)
                    dve.scalar_tensor_tensor(yc[:, cols], ps[0:SAMPLE, 4, cols], bs[:, g:g + 1],
                                             za[0:SAMPLE, ZU + g * P:ZU + (g + 1) * P], ALU.add, ALU.mult)
                dve.drain().then_inc(yc_ready, 1)
                dve.wait_ge(exped, 1)
                dve.tensor_tensor(total[:], total[:], esink[:], ALU.add)
                dve.drain()
                dve.reciprocal(total[:], total[:])
                dve.drain()
                for b in range(S4):
                    for g in range(GROUPS):
                        dve.tensor_scalar(sc[:, b, g, :], sc[:, b, g, :], total[:, b, g:g + 1], None, ALU.mult)
                dve.drain().then_inc(normed, 1)
                dve.wait_ge(ycT_full, 1)
                dve.tensor_copy(yt[:, 4:8, 0:SAMPLE],
                                ps[:, 5, :].rearrange("p (j t) -> p j t", j=4)[:, :, 0:SAMPLE]).then_inc(y_dve, 1)


def merge_stage(nc, a):
    with ExitStack() as stack:
        s = Space(nc, stack, "merge")
        wa, wc = s.sb("wa", [P, 4, D]), s.sb("wc", [P, 4, D])
        wo, wpg, wpp = s.sb("wo", [P, KT, D]), s.sb("wpg", [P, KT, D]), s.sb("wpp", [P, 2, D])
        gain, shift, ident = s.sb("gain", [P, D]), s.sb("shift", [P, D]), s.sb("ident", [P, P])
        yt, gates = s.sb("yt", [P, 2, 8, P]), s.sb("gates", [P, 2, 2 * D])
        x, pt = s.sb("x", [P, 2, D]), s.sb("pt", [P, 2, 2, P])
        t1, t2, mt, x1 = s.sb("t1", [P, D]), s.sb("t2", [P, D]), s.sb("mt", [P, KT, P]), s.sb("x1", [P, D])
        x1t, xh, xl = s.sb("x1t", [P, KT, P]), s.sb("xh", [P, KT, P], F16), s.sb("xl", [P, KT, P], F16)
        tg, base = s.sb("tg", [P, D]), s.sb("base", [P, D])
        stats, mv, rstd = s.sb("stats", [P, 2, 6]), s.sb("mv", [P, 2]), s.sb("rstd", [P, 1])
        power = s.sb("power", [P, 1])
        ps = s.psum("ps", [P, 8, 512])
        w_loaded = {k: s.sem(f"w_loaded_{k}") for k in ("wa", "wc", "wo", "wpg", "wpp", "const")}
        loaded = s.sems("loaded", 2)
        (ac_full, ac_read, mix_ready, mixT_full, mixT_read, o_full, o_read, x_scaled, x1_ready, x1T_full, x1T_read,
         xl_ready, gate_full, gate_act, base_ready) = (s.sem(k) for k in (
             "ac_full", "ac_read", "mix_ready", "mixT_full", "mixT_read", "o_full", "o_read", "x_scaled", "x1_ready",
             "x1T_full", "x1T_read", "xl_ready", "gate_full", "gate_act", "base_ready"))
        stored = s.sem("stored")
        var_ready, rstd_ready = s.sem("var_ready"), s.sem("rstd_ready")

        with nc.Block() as block:

            @block.sync
            def _(sp):
                def load(n, slot):
                    for dst, src in ((yt, a.yT[bass.ds(n, 1)]), (gates, a.z[bass.ds(n + 1, 1), :, ZG:ZW]),
                                     (x, a.x_blocks[bass.ds(n, 1)]), (pt, a.pt_blocks[bass.ds(n, 1)])):
                        sp.dma_start(dst[:, slot], src).then_inc(loaded[slot], 16)

                load(0, 0)
                for k, dst, src in (("wa", wa, a.wa), ("wc", wc, a.wc), ("const", ident, a.c_ident), ("wo", wo, a.wo),
                                    ("const", gain, a.ln1_g), ("const", shift, a.ln1_b), ("wpg", wpg, a.wpg), ("wpp", wpp, a.wpp)):
                    sp.dma_start(dst[:], src).then_inc(w_loaded[k], 16)

                def store(n):
                    sp.wait_ge(x1T_read, n + 1)
                    sp.wait_ge(xl_ready, n + 1)
                    cols = bass.ds(n * P, P)
                    sp.dma_start(a.x1T[bass.ds(n, 1)], x1t[:]).then_inc(stored, 16)
                    sp.dma_start(a.xh[:, :, cols], xh[:]).then_inc(stored, 16)
                    sp.dma_start(a.xl[:, :, cols], xl[:]).then_inc(stored, 16)
                    sp.wait_ge(base_ready, n + 2)
                    sp.dma_start(a.base[bass.ds(n, 1)], base[:]).then_inc(stored, 16)

                with sp.Fori(0, NB // 2) as i:
                    for slot in range(2):
                        n = i * 2 + slot
                        sp.wait_ge(stored, n * 64 + 64)
                        load(n + 1, 1 - slot)
                        store(n)
                store(NB)
                sp.wait_ge(stored, (NB + 2) * 64)

            @block.tensor
            def _(pe):
                pe.wait_ge(w_loaded["const"], 48)

                def product(bank, lhs, w, kt):
                    for c in range(2):
                        for k in range(kt):
                            mm = pe.matmul(ps[:, bank + c, :], lhs[:, k, :], w[:, k, c * 512:(c + 1) * 512],
                                           start=k == 0, stop=k == kt - 1)
                    return mm

                def transposes(bank, src):
                    for k in range(KT):
                        mm = pe.transpose(ps[:, bank + k // 4, (k % 4) * P:(k % 4 + 1) * P], src[:, k * P:(k + 1) * P], ident[:])
                    return mm

                def body(n, slot):
                    pe.wait_ge(loaded[slot], (n - slot) * 32 + 64)
                    pe.wait_ge(base_ready, n + 1)
                    for k in ("wa", "wc"):
                        pe.wait_ge(w_loaded[k], 16)
                    product(0, yt[:, slot, 0:4], wa, 4)
                    product(2, yt[:, slot, 4:8], wc, 4).then_inc(ac_full, 1)
                    pe.wait_ge(mix_ready, n + 1)
                    transposes(4, t1).then_inc(mixT_full, 1)
                    pe.wait_ge(mixT_read, n + 1)
                    pe.wait_ge(w_loaded["wo"], 16)
                    product(6, mt, wo, KT).then_inc(o_full, 1)
                    for k in ("wpg", "wpp"):
                        pe.wait_ge(w_loaded[k], 16)
                    product(2, pt[:, slot], wpp, 2)
                    pe.wait_ge(x1_ready, n + 1)
                    transposes(4, x1).then_inc(x1T_full, 1)
                    pe.wait_ge(x1T_read, n + 1)
                    product(0, x1t, wpg, KT).then_inc(gate_full, 1)

                over_blocks(pe, body)

            def two(bank):
                return ps[:, bank:bank + 2, :]

            def halves(t):
                return t.rearrange("p (c n) -> p c n", c=2)

            @block.scalar
            def _(act):
                act.sem_inc(stored, 64)

                def body(n, slot):
                    act.wait_ge(loaded[slot], (n - slot) * 32 + 64)
                    act.activation(x[:, slot], x[:, slot], ACT.Copy, scale=ALPHA).then_inc(x_scaled, 1)
                    act.wait_ge(mixT_full, n + 1)
                    act.activation(mt[:].rearrange("p (c k) t -> p c (k t)", c=2), two(4), ACT.Copy).then_inc(mixT_read, 1)
                    act.wait_ge(x1T_full, n + 1)
                    act.wait_ge(stored, n * 64 + 64)
                    act.activation(x1t[:].rearrange("p (c k) t -> p c (k t)", c=2), two(4), ACT.Copy)
                    act.activation(xh[:].rearrange("p (c k) t -> p c (k t)", c=2), two(4), ACT.Copy)
                    act.drain().then_inc(x1T_read, 1)
                    act.wait_ge(gate_full, n + 1)
                    act.activation(halves(tg[:]), two(0), ACT.Tanh, scale=0.5).then_inc(gate_act, 1)

                over_blocks(act, body)

            @block.gpsimd
            def _(pool):
                pool.memset(power[:], -0.5)
                pool.drain()
                over_blocks(pool, lambda n, slot: inverse_deviation(pool, P, mv, power, rstd, var_ready, rstd_ready, n + 1))

            @block.vector
            def _(dve):
                dve.wait_ge(w_loaded["const"], 48)

                def body(n, slot):
                    dve.wait_ge(loaded[slot], (n - slot) * 32 + 64)
                    dve.wait_ge(ac_full, n + 1)
                    dve.scalar_tensor_tensor(halves(t1[:]), halves(gates[:, slot, 0:D]), 1.0, two(0), ALU.add, ALU.mult)
                    dve.scalar_tensor_tensor(halves(t2[:]), halves(gates[:, slot, D:2 * D]), 1.0, two(2), ALU.add, ALU.mult)
                    dve.drain()
                    dve.tensor_tensor(t1[:], t1[:], t2[:], ALU.add)
                    dve.drain().then_inc(mix_ready, 1)
                    dve.wait_ge(x_scaled, n + 1)
                    dve.wait_ge(o_full, n + 1)
                    dve.scalar_tensor_tensor(halves(x1[:]), two(6), 0.5, halves(x[:, slot]), ALU.mult, ALU.add)
                    dve.drain()
                    layer_norm_stats(dve, [x1[:, 0:512], x1[:, 512:1024]], P, stats, mv, var_ready, rstd_ready, n + 1)
                    dve.tensor_scalar(x1[:], x1[:], mv[:, 0:1], rstd[:, :], ALU.subtract, ALU.mult)
                    dve.drain()
                    dve.tensor_tensor(x1[:], x1[:], gain[:], ALU.mult)
                    dve.drain()
                    dve.tensor_tensor(x1[:], x1[:], shift[:], ALU.add)
                    dve.drain().then_inc(x1_ready, 1)
                    dve.wait_ge(x1T_read, n + 1)
                    dve.tensor_tensor(xl[:], x1t[:], xh[:], ALU.subtract).then_inc(xl_ready, 1)
                    dve.wait_ge(gate_act, n + 1)
                    dve.scalar_tensor_tensor(halves(t2[:]), halves(tg[:]), 1.0, two(2), ALU.add, ALU.mult)
                    dve.wait_ge(stored, n * 64 + 64)
                    dve.tensor_scalar(base[:], x1[:], ALPHA, None, ALU.mult)
                    dve.drain()
                    dve.scalar_tensor_tensor(base[:], t2[:], 0.5, base[:], ALU.mult, ALU.add)
                    dve.drain().then_inc(base_ready, 1)

                dve.sem_inc(base_ready, 1)
                over_blocks(dve, body)


def route_stage(nc, a):
    BT = 8
    with ExitStack() as stack:
        s = Space(nc, stack, "route")
        wq, sub = s.sb("wq", [P, KT, 2 * PH * P]), s.sb("sub", [P, 2 * PH, KEYS])
        ident, iota, iota16 = s.sb("ident", [P, P]), s.sb("iota", [P, KEYS], F16), s.sb("iota16", [P, TOPK])
        x1t, qt = s.sb("x1t", [P, KT, P]), s.sb("qt", [P, 2 * PH, P])
        sc = s.sb("sc", [P, 2, 2 * PH, KEYS])
        rest = s.sb("rest", [P, 2 * PH * KEYS])
        pair = s.sb("pair", [P, PH, TOPK * TOPK])
        sv, si = s.sb("sv", [P, 2 * PH, TOPK]), s.sb("si", [P, 2 * PH, TOPK], U32)
        sif = s.sb("sif", [P, PH, 2, TOPK])
        fv, fi = s.sb("fv", [P, PH, TOPK]), s.sb("fi", [P, PH, TOPK], U32)
        half_u = s.sb("half_u", [P, 2, PH, TOPK], U32)
        half_f = s.sb("half_f", [P, 2, PH, TOPK])
        pick = s.sb("pick", [P, 3, PH, TOPK])
        gsum = s.sb("gsum", [P, PH])
        col = s.sb("col", [P, 2, P])
        gh16, gl = s.sb("gh16", [P, P], F16), s.sb("gl", [P, P])
        gh, gt = s.sb("gh", [P, P]), s.sb("gt", [P, P])
        now = s.sb("now", [P, 2, 4, BT])
        hot_c = s.sb("hot_c", [P, 2, BT, KEYS], F16)
        hot_h, hot_l = s.sb("hot_h", [P, 2, BT, KEYS], F16), s.sb("hot_l", [P, 2, BT, KEYS], F16)
        gbuf = s.sb("gbuf", [P, KEYS, P])
        ps = s.psum("ps", [P, 8, 512])
        power, scrap = s.sb("one", [P, 1]), s.sb("scrap", [P, 1])
        w_loaded, const_loaded, x_loaded = s.sem("w_loaded"), s.sem("const_loaded"), s.sem("x_loaded")
        q_full, q_read, s_full, s_read = (s.sem(k) for k in ("q_full", "q_read", "s_full", "s_read"))
        sc_used, exp_in, exp_out, picked = (s.sem(k) for k in ("sc_used", "exp_in", "exp_out", "picked"))
        pickT_full = s.sem("pickT_full")
        now_ready, rows_ready, cols_ready = s.sem("now_ready"), s.sem("rows_ready"), s.sem("cols_ready")
        g_full, g_read, g_stored = s.sem("g_full"), s.sem("g_read"), s.sem("g_stored")
        block_done = s.sem("block_done")
        batches = P // BT

        def over_batches(eng, n, body):
            with eng.Fori(0, rows_of(n) // BT // 2) as j:
                body(j * 2, 0)
                body(j * 2 + 1, 1)

        with nc.Block() as block:

            @block.sync
            def _(sp):
                sp.dma_start(x1t[:], a.x1T[0]).then_inc(x_loaded, 16)
                sp.dma_start(wq[:], a.wq).then_inc(w_loaded, 16)
                for dst, src in ((sub, a.subT), (ident, a.c_ident), (iota, a.c_iota), (iota16, a.c_iota16)):
                    sp.dma_start(dst[:], src).then_inc(const_loaded, 16)

                def body(n, slot):
                    if not (isinstance(n, int) and n == NB):
                        sp.wait_ge(q_full, n * 4 + 4)
                        sp.dma_start(x1t[:], a.x1T[bass.ds(n + 1, 1)]).then_inc(x_loaded, 16)
                    sp.wait_ge(block_done, n + 1)
                    r = rows_of(n)
                    sp.dma_start(a.g[:, :, bass.ds(n * P, r)].rearrange("i p t -> p i t"), gbuf[:, :, 0:r]).then_inc(g_stored, 16)

                over_blocks(sp, body)
                sp.wait_ge(g_stored, 16 * (NB + 2))

            @block.tensor
            def _(pe):
                pe.sem_inc(g_full, 4)
                pe.wait_ge(w_loaded, 16)
                pe.wait_ge(const_loaded, 64)

                def scores(n):
                    pe.wait_ge(x_loaded, n * 16 + 16)
                    for j in range(4):
                        pe.wait_ge(q_read, n * 4 + j + 1)
                        for t in range(4):
                            c = (4 * j + t) * P
                            for k in range(KT):
                                mm = pe.matmul(ps[:, j % 2, t * P:(t + 1) * P], wq[:, k, c:c + P], x1t[:, k, :],
                                               start=k == 0, stop=k == KT - 1)
                        mm.then_inc(q_full, 1)
                    for j in range(4):
                        pe.wait_ge(q_read, n * 4 + j + 3)
                        pe.wait_ge(s_read, n * 4 + j + 1)
                        for t in range(4):
                            hc = 4 * j + t
                            mm = pe.matmul(ps[:, 2, t * P:(t + 1) * P], qt[:, hc, :], sub[:, hc, :], start=True, stop=True)
                        mm.then_inc(s_full, 1)

                scores(0)

                def body(n, slot):
                    if not (isinstance(n, int) and n == NB):
                        scores(n + 1)
                    pe.wait_ge(picked, n + 1)
                    for j in range(3):
                        mm = pe.transpose(ps[:, 3, j * P:(j + 1) * P], pick[:, j].rearrange("p h k -> p (h k)"), ident[:])
                    mm.then_inc(pickT_full, 1)

                    def batch(b, half):
                        pe.wait_ge(rows_ready, n * batches + b + 1)
                        pe.wait_ge(cols_ready, n * batches + b + 3)
                        for q in range(BT // 4):
                            pe.wait_ge(g_read, (n * batches + b) * 2 + q + 1)
                            for t in range(4):
                                o = ps[:, 4 + 2 * half + q, t * P:(t + 1) * P]
                                tt = 4 * q + t
                                pe.matmul(o, hot_c[:, half, tt, :], hot_h[:, half, tt, :], start=True, stop=False)
                                mm = pe.matmul(o, hot_c[:, half, tt, :], hot_l[:, half, tt, :], start=False, stop=True)
                            mm.then_inc(g_full, 1)
                    over_batches(pe, n, batch)

                over_blocks(pe, body)

            @block.scalar
            def _(act):
                act.sem_inc(q_read, 2)
                act.sem_inc(s_read, 1)
                act.sem_inc(g_read, 4)
                act.sem_inc(g_stored, 16)
                act.sem_inc(sc_used, 2)

                def scores(n, slot):
                    for j in range(4):
                        act.wait_ge(q_full, n * 4 + j + 1)
                        act.activation(qt[:, 4 * j:4 * j + 4, :], ps[:, j % 2, :].rearrange("p (t n) -> p t n", t=4),
                                       ACT.Copy).then_inc(q_read, 1)
                    act.wait_ge(sc_used, n + 1)
                    for j in range(4):
                        act.wait_ge(s_full, n * 4 + j + 1)
                        act.activation(sc[:, slot, 4 * j:4 * j + 4, :], ps[:, 2, :].rearrange("p (t n) -> p t n", t=4),
                                       ACT.Copy).then_inc(s_read, 1)

                scores(0, 0)

                def body(n, slot):
                    if not (isinstance(n, int) and n == NB):
                        scores(n + 1, 1 - slot)
                    act.wait_ge(exp_in, n + 1)
                    act.activation(pick[:, 2], pick[:, 2], ACT.Exp).then_inc(exp_out, 1)
                    act.wait_ge(g_stored, n * 16 + 16)

                    def batch(b, half):
                        for q in range(BT // 4):
                            act.wait_ge(g_full, (n * batches + b) * 2 + q + 5)
                            act.wait_ge(const_loaded, 64)
                            act.activation(gbuf[:, :, bass.ds(b * BT + 4 * q, 4)],
                                           ps[:, 4 + 2 * half + q, :].rearrange("p (t i) -> p i t", t=4),
                                           ACT.Copy).then_inc(g_read, 1)
                    over_batches(act, n, batch)
                    act.drain().then_inc(block_done, 1)

                over_blocks(act, body)

            @block.gpsimd
            def _(pool):
                pool.memset(power[:], 1.0)
                pool.drain()
                pool.sem_inc(cols_ready, 2)
                pool.wait_ge(const_loaded, 64)

                def body(n, slot):
                    def batch(b, half):
                        pool.wait_ge(now_ready, n * batches + b + 1)
                        pool.wait_ge(g_full, (n * batches + b) * 2 + 2)
                        pool.tensor_tensor(scrap[:], power[:], power[:], ALU.mult)
                        for t in range(BT):
                            pool.tensor_scalar(hot_c[:, half, t, :], iota[:], now[:, half, 3, t:t + 1], None, ALU.is_equal)
                        pool.drain().then_inc(cols_ready, 1)
                    over_batches(pool, n, batch)

                over_blocks(pool, body)

            @block.vector
            def _(dve):
                dve.wait_ge(const_loaded, 64)

                def top16(scores, rest, values, indices):
                    n = len(scores)
                    for j in range(n):
                        dve.max(values[j][:, 0:8], scores[j])
                    dve.drain()
                    for j in range(n):
                        dve.max_index(indices[j][:, 0:8], values[j][:, 0:8], scores[j])
                        dve.match_replace(rest[j], values[j][:, 0:8], scores[j], LOWEST)
                    dve.drain()
                    for j in range(n):
                        dve.max(values[j][:, 8:16], rest[j])
                    dve.drain()
                    for j in range(n):
                        dve.max_index(indices[j][:, 8:16], values[j][:, 8:16], rest[j])

                def body(n, slot):
                    dve.wait_ge(s_read, n * 4 + 5)
                    dve.memset(gsum[:], 0.0)
                    hc = range(2 * PH)
                    top16([sc[:, slot, j, :] for j in hc], [rest[:, j * KEYS:(j + 1) * KEYS] for j in hc],
                          [sv[:, j, :] for j in hc], [si[:, j, :] for j in hc])
                    dve.drain().then_inc(sc_used, 1)
                    half = sv[:].rearrange("p (h c) k -> p h c k", c=2)
                    pairs = pair[:].rearrange("p h (i j) -> p h i j", i=TOPK)
                    dve.tensor_tensor(pairs, half[:, :, 0].unsqueeze(3).broadcast_to([P, PH, TOPK, TOPK]),
                                      half[:, :, 1].unsqueeze(2).broadcast_to([P, PH, TOPK, TOPK]), ALU.add)
                    dve.tensor_copy(sif[:].rearrange("p h c k -> p (h c k)"), si[:].rearrange("p h k -> p (h k)"))
                    dve.drain()
                    top16([pair[:, h, :] for h in range(PH)], [rest[:, h * 256:(h + 1) * 256] for h in range(PH)],
                          [fv[:, h, :] for h in range(PH)], [fi[:, h, :] for h in range(PH)])
                    dve.drain()
                    dve.tensor_tensor(pick[:, 2], fv[:], fv[:, :, 0:1].broadcast_to([P, PH, TOPK]), ALU.subtract)
                    dve.tensor_scalar(half_u[:, 0], fi[:], 4, None, ALU.logical_shift_right)
                    dve.tensor_scalar(half_u[:, 1], fi[:], TOPK - 1, None, ALU.bitwise_and)
                    dve.drain().then_inc(exp_in, 1)
                    dve.tensor_copy(half_f[:].rearrange("p c h k -> p (c h k)"), half_u[:].rearrange("p c h k -> p (c h k)"))
                    dve.drain()
                    for c in range(2):
                        dve.tensor_tensor(pairs, half_f[:, c].unsqueeze(3).broadcast_to([P, PH, TOPK, TOPK]),
                                          iota16[:].unsqueeze(1).unsqueeze(1).broadcast_to([P, PH, TOPK, TOPK]), ALU.is_equal)
                        dve.drain()
                        dve.tensor_tensor(pairs, pairs, sif[:, :, c].unsqueeze(2).broadcast_to([P, PH, TOPK, TOPK]), ALU.mult)
                        dve.drain()
                        dve.tensor_reduce(pick[:, c], pairs, X, ALU.add)
                        dve.drain()
                    dve.wait_ge(exp_out, n + 1)
                    dve.tensor_reduce(gsum[:], pick[:, 2], X, ALU.add)
                    dve.drain()
                    dve.reciprocal(gsum[:], gsum[:])
                    dve.drain()
                    dve.tensor_tensor(pick[:, 2], pick[:, 2], gsum[:].unsqueeze(2).broadcast_to([P, PH, TOPK]), ALU.mult)
                    dve.drain().then_inc(picked, 1)
                    dve.wait_ge(pickT_full, n + 1)
                    dve.tensor_copy(col[:], ps[:, 3, 0:2 * P].rearrange("p (c t) -> p c t", c=2))
                    dve.tensor_scalar(gt[:], ps[:, 3, 2 * P:3 * P], SG, None, ALU.mult)
                    dve.drain()
                    dve.tensor_copy(gh16[:], gt[:])
                    dve.drain()
                    dve.tensor_copy(gh[:], gh16[:])
                    dve.tensor_tensor(gl[:], gt[:], gh16[:], ALU.subtract)
                    dve.drain()

                    def batch(b, half):
                        dve.wait_ge(cols_ready, n * batches + b + 1)
                        dve.wait_ge(g_full, (n * batches + b) * 2 + 2)
                        dve.wait_ge(const_loaded, 64)
                        for j, src in enumerate((col[:, 0], gh, gl, col[:, 1])):
                            dve.tensor_copy(now[:, half, j, :], src[:, bass.ds(b * BT, BT)])
                        dve.drain().then_inc(now_ready, 1)
                        for t in range(BT):
                            for j, hot in ((1, hot_h), (2, hot_l)):
                                dve.tensor_scalar(hot[:, half, t, :], iota[:], now[:, half, 0, t:t + 1],
                                                  now[:, half, j, t:t + 1], ALU.is_equal, ALU.mult)
                        dve.drain().then_inc(rows_ready, 1)
                    over_batches(dve, n, batch)

                over_blocks(dve, body)


def experts_stage(nc, a):
    ROWS = 4
    TURNS = KEYS // ROWS
    CHUNKS = [(0, 384), (384, 768), (768, T)]
    NC = len(CHUNKS)
    YB = 3
    TB = [(b * P, min((b + 1) * P, T)) for b in range(NB + 1)]
    with ExitStack() as stack:
        s = Space(nc, stack, "experts")
        xh, xl = s.sb("xh", [P, KT, T], F16), s.sb("xl", [P, KT, T], F16)
        y = s.sb("y", [P, NB + 1, D])
        ut, uh, ul = s.sb("ut", [P, 2, D]), s.sb("uh", [P, 2, KT, P], F16), s.sb("ul", [P, 2, KT, P], F16)
        vt = s.sb("vt", [P, 2, D])
        vh, vl = s.sb("vh", [P, ROWS, D], F16), s.sb("vl", [P, ROWS, D], F16)
        g = s.sb("g", [P, 2, T])
        act_a = s.sb("act_a", [P, NC, 384])
        hf = s.sb("hf", [P, 384])
        hh, hl = s.sb("hh", [P, ROWS, T], F16), s.sb("hl", [P, ROWS, T], F16)
        gain, shift = s.sb("gain", [P, D]), s.sb("shift", [P, D])
        stats, mv, rstd = s.sb("stats", [P, 2, 6]), s.sb("mv", [P, 2]), s.sb("rstd", [P, 1])
        power = s.sb("power", [P, 1])
        ps = s.psum("ps", [P, 8, 512])
        const_loaded = s.sem("const_loaded")
        u_loaded, v_loaded, g_loaded = s.sems("u_loaded", 2), s.sems("v_loaded", 2), s.sems("g_loaded", 2)
        u_high, u_ready, v_high, v_ready = (s.sem(k) for k in ("u_high", "u_ready", "v_high", "v_ready"))
        a_full, a_read, h_temp, h_ready = (s.sem(k) for k in ("a_full", "a_read", "h_temp", "h_ready"))
        y_full, y_read, turn_done = s.sem("y_full"), s.sem("y_read"), s.sem("turn_done")
        y_ready, y_stored = s.sem("y_ready"), s.sem("y_stored")
        var_ready, rstd_ready = s.sem("var_ready"), s.sem("rstd_ready")
        n_const = 4 + 1

        def over_turns(eng, body):
            with eng.Fori(0, TURNS - 1) as i:
                body(i, False)
            body(TURNS - 1, True)

        with nc.Block() as block:

            @block.sync
            def _(sp):
                def load_u(e, slot):
                    sp.dma_start(ut[:, slot], a.uT[bass.ds(e, 1)]).then_inc(u_loaded[slot], 16)

                def load_vg(e, slot):
                    sp.dma_start(g[:, slot], a.g[bass.ds(e, 1), :, 0:T]).then_inc(g_loaded[slot], 16)
                    sp.dma_start(vt[:, slot], a.v[bass.ds(e, 1)]).then_inc(v_loaded[slot], 16)

                load_u(0, 0)
                sp.dma_start(xh[:], a.xh[:, :, 0:T]).then_inc(const_loaded, 16)
                sp.dma_start(xl[:], a.xl[:, :, 0:T]).then_inc(const_loaded, 16)
                load_u(1, 1)
                load_vg(0, 0)
                load_vg(1, 1)
                sp.dma_start(y[:], a.base.rearrange("b p d -> p b d")).then_inc(const_loaded, 16)
                sp.dma_start(gain[:], a.ln2_g).then_inc(const_loaded, 16)
                sp.dma_start(shift[:], a.ln2_b).then_inc(const_loaded, 16)

                def body(i, last):
                    for m in range(ROWS):
                        if last and m >= ROWS - 2:
                            continue
                        e = i * ROWS + m
                        sp.wait_ge(u_ready, e + 1)
                        load_u(e + 2, m % 2)
                        sp.wait_ge(h_temp, e * NC + 2 * NC)
                        sp.wait_ge(v_ready, e + 1)
                        load_vg(e + 2, m % 2)

                over_turns(sp, body)
                for b, (t0, t1) in enumerate(TB):
                    sp.wait_ge(y_ready, b + 1)
                    out = a.y_prompt[t0:t1, :] if b < NB else a.y_sample
                    sp.dma_start(out, y[0:t1 - t0, b, :]).then_inc(y_stored, 16)
                sp.wait_ge(y_stored, 16 * (NB + 1))

            @block.tensor
            def _(pe):
                pe.sem_inc(turn_done, 1)
                pe.wait_ge(const_loaded, 16 * n_const)

                def body(i, last):
                    for m in range(ROWS):
                        e, slot = i * ROWS + m, m % 2
                        pe.wait_ge(u_ready, e + 1)
                        for c, (t0, t1) in enumerate(CHUNKS):
                            bank = (m * NC + c) % 4
                            pe.wait_ge(a_read, e * NC + c + 1)
                            for k in range(KT):
                                for j, (w, x) in enumerate(((uh, xh), (uh, xl), (ul, xh))):
                                    mm = pe.matmul(ps[:, bank, 0:t1 - t0], w[:, slot, k, :], x[:, k, t0:t1],
                                                   start=k == 0 and j == 0, stop=k == KT - 1 and j == 2)
                            mm.then_inc(a_full, 1)
                    pe.wait_ge(v_ready, i * ROWS + ROWS)
                    for b, (t0, t1) in enumerate(TB):
                        pe.wait_ge(h_ready, i * (ROWS * NC) + (ROWS - 1) * NC + b // 3 + 1)
                        for d in range(2):
                            q = b * 2 + d
                            pe.wait_ge(y_read, i * (2 * len(TB)) + q + 1)
                            for m in range(ROWS):
                                for j, (h, v) in enumerate(((hh, vh), (hh, vl), (hl, vh))):
                                    mm = pe.matmul(ps[0:t1 - t0, 4 + q % YB, :], h[:, m, t0:t1], v[:, m, d * 512:(d + 1) * 512],
                                                   start=m == 0 and j == 0, stop=m == ROWS - 1 and j == 2)
                            mm.then_inc(y_full, 1)
                    pe.drain().then_inc(turn_done, 1)

                over_turns(pe, body)

            @block.scalar
            def _(act):
                act.sem_inc(a_read, 4)

                def high_u(e, slot, count):
                    act.wait_ge(u_loaded[slot], count)
                    act.activation(uh[:, slot].rearrange("p k t -> p (k t)"), ut[:, slot], ACT.Copy, scale=SU).then_inc(u_high, 1)

                high_u(0, 0, 16)
                high_u(1, 1, 16)

                def body(i, last):
                    for m in range(ROWS):
                        e, slot = i * ROWS + m, m % 2
                        for c, (t0, t1) in enumerate(CHUNKS):
                            act.wait_ge(h_temp, e * NC + c + 1)
                            act.wait_ge(a_full, e * NC + c + 1)
                            act.activation(act_a[:, c, 0:t1 - t0], ps[:, (m * NC + c) % 4, 0:t1 - t0],
                                           ACT.Gelu_apprx_tanh, scale=1.0 / SU).then_inc(a_read, 1)
                        if not (last and m >= ROWS - 2):
                            high_u(e + 2, slot, (i * 2 + m // 2) * 16 + 32)
                        if m == 0:
                            act.wait_ge(turn_done, i + 1)
                        act.wait_ge(v_loaded[slot], (i * 2 + m // 2) * 16 + 16)
                        act.activation(vh[:, m], vt[:, slot], ACT.Copy, scale=SV).then_inc(v_high, 1)

                over_turns(act, body)

            @block.gpsimd
            def _(pool):
                pool.memset(power[:], -0.5)
                pool.drain()
                for b, (t0, t1) in enumerate(TB):
                    inverse_deviation(pool, t1 - t0, mv, power, rstd, var_ready, rstd_ready, b + 1)

            @block.vector
            def _(dve):
                dve.sem_inc(h_temp, NC)
                dve.sem_inc(y_read, YB)
                dve.wait_ge(const_loaded, 16 * n_const)

                def low_u(e, slot):
                    dve.wait_ge(u_high, e + 1)
                    dve.scalar_tensor_tensor(ul[:, slot].rearrange("p k t -> p (k t)"), ut[:, slot], SU,
                                             uh[:, slot].rearrange("p k t -> p (k t)"), ALU.mult, ALU.subtract).then_inc(u_ready, 1)

                low_u(0, 0)
                low_u(1, 1)

                def body(i, last):
                    dve.wait_ge(turn_done, i + 1)
                    for m in range(ROWS):
                        e, slot = i * ROWS + m, m % 2
                        dve.wait_ge(g_loaded[slot], (i * 2 + m // 2) * 16 + 16)
                        for c, (t0, t1) in enumerate(CHUNKS):
                            w = t1 - t0
                            dve.wait_ge(a_read, e * NC + c + 5)
                            dve.scalar_tensor_tensor(hf[:, 0:w], g[:, slot, t0:t1], SH / SG, act_a[:, c, 0:w], ALU.mult, ALU.mult)
                            dve.drain().then_inc(h_temp, 1)
                            dve.tensor_copy(hh[:, m, t0:t1], hf[:, 0:w])
                            dve.drain()
                            dve.tensor_tensor(hl[:, m, t0:t1], hf[:, 0:w], hh[:, m, t0:t1], ALU.subtract)
                            dve.drain().then_inc(h_ready, 1)
                        if not (last and m >= ROWS - 2):
                            low_u(e + 2, slot)
                        dve.wait_ge(v_high, e + 1)
                        dve.scalar_tensor_tensor(vl[:, m], vt[:, slot], SV, vh[:, m], ALU.mult, ALU.subtract).then_inc(v_ready, 1)
                    for b, (t0, t1) in enumerate(TB):
                        for d in range(2):
                            q = b * 2 + d
                            r = t1 - t0
                            dve.wait_ge(y_full, i * (2 * len(TB)) + q + 1)
                            part = y[0:r, b, d * 512:(d + 1) * 512]
                            dve.scalar_tensor_tensor(part, ps[0:r, 4 + q % YB, :], 1.0 / (SH * SV), part, ALU.mult,
                                                     ALU.add).then_inc(y_read, 1)

                over_turns(dve, body)
                dve.drain()
                for b, (t0, t1) in enumerate(TB):
                    r = t1 - t0
                    row = y[0:r, b, :]
                    layer_norm_stats(dve, [row[:, 0:512], row[:, 512:1024]], r, stats, mv, var_ready, rstd_ready, b + 1)
                    dve.tensor_scalar(row, row, mv[:r, 0:1], rstd[:r, :], ALU.subtract, ALU.mult)
                    dve.drain()
                    dve.tensor_tensor(row, row, gain[:r, :], ALU.mult)
                    dve.drain()
                    dve.tensor_tensor(row, row, shift[:r, :], ALU.add)
                    dve.drain().then_inc(y_ready, 1)


def build(nc, a):
    bias_stage(nc, a)
    project_stage(nc, a)
    mix_prompt_stage(nc, a)
    mix_sample_stage(nc, a)
    merge_stage(nc, a)
    route_stage(nc, a)
    experts_stage(nc, a)


class Arrays:
    pass


def shape_constants():
    dist = 2 * P - 1 - np.arange(TOEP)
    inside = (dist >= 0) & (dist < P)
    n = np.maximum(dist, 0)
    exact = BUCKETS // 2
    large = exact + (np.log(np.maximum(n, 1) / exact) / math.log(MAX_DISTANCE / exact) * (BUCKETS - exact)).astype(np.int32)
    bucket = np.where(n < exact, n, np.minimum(large, BUCKETS - 1))
    onehot = ((np.arange(BUCKETS)[:, None] == bucket[None]) & inside[None]).astype(np.float32)
    outside = np.broadcast_to(np.where(inside, 0.0, NEG).astype(np.float32), (HEADS, TOEP))
    return {
        "c_bucket": onehot,
        "c_outside": np.ascontiguousarray(outside),
        "c_ident": np.eye(P, dtype=np.float32),
        "c_tril": np.triu(np.ones((P, P), np.float32)),
        "c_iota": np.broadcast_to(np.arange(KEYS, dtype=np.float16), (P, KEYS)).copy(),
        "c_iota16": np.broadcast_to(np.arange(TOPK, dtype=np.float32), (P, TOPK)).copy(),
    }


def laid_out(x_prompt, x_sample, cache_k_win, cache_v_win, p_prompt, p_sample, rel_bias_table, w_in, attn_sinks,
             w_att_out, c_ln_g, c_ln_b, c_ws, c_bs, w_chunk_out, w_o, ln1_g, ln1_b, peer_wq, peer_subkeys, peer_u,
             peer_v, w_ple_gate, w_ple_proj, ln2_g, ln2_b):
    def blocks(prompt, sample):
        w = prompt.shape[-1]
        rows = np.zeros(((NB + 1) * P, w), np.float32)
        rows[:PROMPT] = prompt.reshape(PROMPT, w)
        rows[PROMPT:T] = sample.reshape(SAMPLE, w)
        return rows.reshape(NB + 1, P, w)

    def by_feature(b):
        return b.reshape(NB + 1, P, -1, P).transpose(0, 3, 2, 1)

    def k_tiles(w):
        return w.reshape(-1, P, w.shape[-1]).transpose(1, 0, 2)

    def rows(v):
        return np.broadcast_to(v.reshape(1, -1), (P, v.size))

    heads = [g * REP + r for r in range(REP) for g in range(GROUPS)]
    q_cols = np.concatenate([np.arange(h * HD, (h + 1) * HD) for h in heads])
    w = w_in[0]
    x = blocks(x_prompt, x_sample)
    ws_sample = np.zeros((SAMPLE, CG, SAMPLE), np.float32)
    for b in range(SEQS):
        seq = slice(b * NEW, (b + 1) * NEW)
        ws_sample[seq, :, seq] = c_ws[0][:, :NEW, :NEW].transpose(2, 0, 1)
    sinks = attn_sinks[0].reshape(1, GROUPS, REP, 1, 1).transpose(0, 2, 3, 4, 1)
    sink_sample = np.broadcast_to(sinks, (4, REP, NEW, SEQS // 4, GROUPS)).reshape(P, SEQS // 4, GROUPS)
    return {
        "ws_sample": ws_sample,
        "sink_sample": sink_sample,
        "bs_sample": np.tile(c_bs[0][:, :NEW].T, (SEQS, 1)),
        "x_blocks": x,
        "xt_blocks": by_feature(x),
        "pt_blocks": by_feature(blocks(p_prompt[0], p_sample[0])),
        "rel_bias_table": rel_bias_table,
        "w_in": k_tiles(np.concatenate([w[:, q_cols], w[:, QW:]], axis=1)),
        "sink_rows": rows(attn_sinks),
        "wa": k_tiles(w_att_out[0][q_cols]),
        "wc": k_tiles(w_chunk_out[0]),
        "wo": k_tiles(w_o[0]),
        "wpg": k_tiles(w_ple_gate[0]),
        "wpp": k_tiles(w_ple_proj[0]),
        "wq": k_tiles(peer_wq[0]),
        "subT": peer_subkeys[0].reshape(2 * PH, KEYS, P).transpose(2, 0, 1),
        "uT": peer_u[0].reshape(KEYS, KEYS, KT, P).transpose(0, 3, 2, 1),
        "v": peer_v[0].reshape(KEYS, KEYS, D),
        "c_ln_g": rows(c_ln_g), "c_ln_b": rows(c_ln_b),
        "ln1_g": rows(ln1_g), "ln1_b": rows(ln1_b), "ln2_g": rows(ln2_g), "ln2_b": rows(ln2_b),
        "wsT": c_ws[0].transpose(2, 0, 1),
        "bsT": c_bs[0].T,
        "cache_kT": cache_k_win[0].transpose(2, 3, 0, 1).reshape(KVW, SEQS, P),
        "cache_v": cache_v_win[0].reshape(SEQS, P, KVW).transpose(1, 0, 2),
        "cache_k_rows": cache_k_win[0].reshape(SEQS, P, KVW),
        "cache_v_rows": cache_v_win[0].reshape(SEQS, P, KVW),
    }


OUTPUTS = {
    "y_prompt": (PROMPT, D), "y_sample": (SAMPLE, D), "k_prompt": (P, KVW), "v_prompt": (P, KVW),
    "k_sample": (SEQS, P, KVW), "v_sample": (SEQS, P, KVW), "chunk_v": (SAMPLE, CW),
}
SCRATCH = {
    "rev": ((HEADS, P, TOEP), F32),
    "z": ((NB + 2, P, ZW), F32),
    "yT": ((NB + 1, P, 8, P), F32),
    "x1T": ((NB + 1, P, KT, P), F32),
    "xh": ((P, KT, (NB + 1) * P), F16), "xl": ((P, KT, (NB + 1) * P), F16),
    "base": ((NB + 1, P, D), F32),
    "g": ((KEYS, KEYS, (NB + 1) * P), F32),
}
SHAPES = {
    "y_prompt": (1, PROMPT, D), "y_sample": (SEQS, NEW, D),
    "k_prompt": (1, 1, P, GROUPS, HD), "v_prompt": (1, 1, P, GROUPS, HD),
    "k_sample": (1, SEQS, P, GROUPS, HD), "v_sample": (1, SEQS, P, GROUPS, HD),
    "chunk_v": (1, SEQS, NEW, CW),
}


def kernel(**inputs):
    import concourse.bacc as bacc
    from concourse.bass_utils import run_bass_kernel_spmd

    nc = bacc.Bacc("TRN2", target_bir_lowering=False, num_devices=1)
    arrays = {**shape_constants(), **laid_out(**{k: np.asarray(v) for k, v in inputs.items()})}
    arrays = {f"in_{k}": np.ascontiguousarray(v) for k, v in arrays.items()}
    a = Arrays()
    for k, v in arrays.items():
        a.__dict__[k[3:]] = nc.dram_tensor(k, v.shape, mybir.dt.from_np(v.dtype), kind="ExternalInput").ap()
    for k, shape in OUTPUTS.items():
        a.__dict__[k] = nc.dram_tensor(f"out_{k}", shape, F32, kind="ExternalOutput").ap()
    for k, (shape, dt) in SCRATCH.items():
        a.__dict__[k] = nc.dram_tensor(f"scratch_{k}", shape, dt, kind="Internal").ap()
    build(nc, a)
    r = run_bass_kernel_spmd(nc, [arrays], core_ids=[0])
    return tuple(r.results[0][f"out_{k}"].reshape(SHAPES[k]) for k in OUTPUTS)
```

```python
import math
from contextlib import ExitStack

import numpy as np

import concourse.bass as bass
from concourse import mybir

F32 = mybir.dt.float32
F16 = mybir.dt.float16
U32 = mybir.dt.uint32
ALU = mybir.AluOpType
ACT = mybir.ActivationFunctionType
X = mybir.AxisListType.X

P = 128
D = 1024
KT = D // P
PROMPT, SAMPLE = 1024, 64
T = PROMPT + SAMPLE
NB = PROMPT // P
SEQS, NEW = 8, 8
HEADS, GROUPS, REP, HD = 8, 2, 4, 64
QW, KVW, CW = 512, 128, 512
CG = 4
IN_W = QW + 2 * KVW + 2 * CW + 2 * D
PLE = 256
PH, HALVES, KEYS, TOPK = 8, 2, 128, 16
HK = PH * TOPK
BT = 8
NEG = -1e30
LOWEST = -3.0e38
ALPHA = 2.0 ** 0.25
EPS = 1e-5
BUCKETS, MAX_DISTANCE = 32, 128
TOEP = 384
ZK, ZKV, ZU, ZV, ZG, ZW = 512, 640, 896, 1408, 1920, 3968

SW, SU, SV, SH, SG = 64.0, 64.0, 16.0, 64.0, 32768.0


def over_blocks(eng, body):
    with eng.Fori(0, NB // 2) as i:
        body(i * 2, 0)
        body(i * 2 + 1, 1)
    body(NB, 0)


def rows_of(n):
    return SAMPLE if isinstance(n, int) and n == NB else P


class Space:

    def __init__(self, nc, stack, stage):
        self.nc, self.stack, self.stage = nc, stack, stage
        self.taken = []
        stack.callback(self.clear)

    def sb(self, name, shape, dt=F32):
        return self.stack.enter_context(self.nc.sbuf_tensor(f"{self.stage}_{name}", shape, dt))

    def psum(self, name, shape, dt=F32):
        return self.stack.enter_context(self.nc.psum_tensor(f"{self.stage}_{name}", shape, dt))

    def sem(self, name):
        self.taken.append(self.nc.alloc_semaphore(f"{self.stage}_{name}"))
        return self.taken[-1]

    def sems(self, name, n):
        return [self.sem(f"{name}{i}") for i in range(n)]

    def clear(self):
        self.nc.all_engine_barrier()
        self.nc.clear_and_free_semaphores(self.taken)
        self.nc.all_engine_barrier()


def layer_norm_stats(dve, src, rows, stats, mv, var_ready, rstd_ready, count, eps=EPS):
    for c, part in enumerate(src):
        dve.bn_stats(stats[:rows, c, :], part)
    dve.drain()
    dve.bn_aggr(mv[:rows, :], stats[:rows, 0:len(src), :])
    dve.drain()
    dve.tensor_scalar(mv[:rows, 1:2], mv[:rows, 1:2], eps, None, ALU.add).then_inc(var_ready, 1)
    dve.wait_ge(rstd_ready, count)


def inverse_deviation(pool, rows, mv, power, rstd, var_ready, rstd_ready, count):
    pool.wait_ge(var_ready, count)
    pool.tensor_tensor(rstd[:rows, :], mv[:rows, 1:2], power[:rows, :], ALU.pow).then_inc(rstd_ready, 1)


def bias_stage(nc, a):
    with ExitStack() as stack:
        s = Space(nc, stack, "bias")
        table = s.sb("table", [BUCKETS, HEADS])
        onehot = s.sb("onehot", [BUCKETS, TOEP])
        outside = s.sb("outside", [HEADS, TOEP])
        rev = s.sb("rev", [HEADS, TOEP])
        zero = s.sb("zero", [P, ZW])
        ps = s.psum("ps", [HEADS, TOEP])
        loaded, product, made, stored = s.sem("loaded"), s.sem("product"), s.sem("made"), s.sem("stored")
        zeroed = s.sem("zeroed")
        with nc.Block() as block:

            @block.sync
            def _(sp):
                sp.dma_start(table[:], a.rel_bias_table).then_inc(loaded, 16)
                sp.dma_start(onehot[:], a.c_bucket).then_inc(loaded, 16)
                sp.dma_start(outside[:], a.c_outside).then_inc(loaded, 16)
                sp.wait_ge(made, 1)
                sp.dma_start(a.rev, rev[:].unsqueeze(1).broadcast_to([HEADS, P, TOEP])).then_inc(stored, 16)
                sp.wait_ge(zeroed, 1)
                sp.dma_start(a.z[0], zero[:]).then_inc(stored, 16)
                sp.wait_ge(stored, 32)

            @block.tensor
            def _(pe):
                pe.wait_ge(loaded, 48)
                pe.matmul(ps[:], table[:], onehot[:], start=True, stop=True).then_inc(product, 1)

            @block.vector
            def _(dve):
                dve.wait_ge(loaded, 48)
                dve.wait_ge(product, 1)
                dve.tensor_tensor(rev[:], ps[:], outside[:], ALU.add).then_inc(made, 1)

            @block.gpsimd
            def _(pool):
                pool.memset(zero[:], 0.0).then_inc(zeroed, 1)


def project_stage(nc, a):
    PIECE = 256
    PIECES = IN_W // PIECE
    with ExitStack() as stack:
        s = Space(nc, stack, "project")
        piece = s.sb("piece", [P, 2, KT, PIECE])
        wh, wl = s.sb("wh", [P, KT, IN_W], F16), s.sb("wl", [P, KT, IN_W], F16)
        xt = s.sb("xt", [P, 2, KT, P])
        xh, xl = s.sb("xh", [P, 2, KT, P], F16), s.sb("xl", [P, 2, KT, P], F16)
        z = s.sb("z", [P, 2, ZW])
        gain = s.sb("gain", [P, CW])
        shift = s.sb("shift", [P, CW])
        stats, mv, rstd = s.sb("stats", [P, 1, 6]), s.sb("mv", [P, 2]), s.sb("rstd", [P, 1])
        power = s.sb("power", [P, 1])
        ps = s.psum("ps", [P, 8, 512])
        w_cols = [(0, 512), (512, 768), (768, 1280), (1280, 1792)] + [(1792 + 512 * j, 2304 + 512 * j) for j in range(4)]
        w_loaded = s.sems("w_loaded", 2)
        w_high, w_ready = s.sem("w_high"), s.sem("w_ready")
        x_high, x_ready = s.sem("x_high"), s.sem("x_ready")
        const_loaded = s.sem("const_loaded")
        x_loaded = s.sems("x_loaded", 2)
        bank_full = s.sems("bank_full", 8)
        bank_read = s.sems("bank_read", 8)
        z_act, z_dve = s.sem("z_act"), s.sem("z_dve")
        z_stored = s.sems("z_stored", 2)
        var_ready, rstd_ready = s.sem("var_ready"), s.sem("rstd_ready")
        with nc.Block() as block:

            @block.sync
            def _(sp):
                sp.dma_start(xt[:, 0], a.xt_blocks[0]).then_inc(x_loaded[0], 16)
                for j in range(PIECES):
                    if j > 1:
                        sp.wait_ge(w_ready, j - 1)
                    sp.dma_start(piece[:, j % 2], a.w_in[:, :, j * PIECE:(j + 1) * PIECE]).then_inc(w_loaded[j % 2], 16)
                sp.dma_start(gain[:], a.c_ln_g).then_inc(const_loaded, 16)
                sp.dma_start(shift[:], a.c_ln_b).then_inc(const_loaded, 16)

                def load(n, slot):
                    sp.dma_start(xt[:, slot], a.xt_blocks[bass.ds(n, 1)]).then_inc(x_loaded[slot], 16)

                def store(n, slot):
                    sp.wait_ge(z_act, n + 1)
                    sp.wait_ge(z_dve, n + 1)
                    sp.dma_start(a.z[bass.ds(n + 1, 1)], z[:, slot]).then_inc(z_stored[slot], 16)

                with sp.Fori(0, NB // 2) as i:
                    for slot in range(2):
                        n = i * 2 + slot
                        sp.wait_ge(bank_full[7], n + 1)
                        load(n + 1, 1 - slot)
                        store(n, slot)
                store(NB, 0)
                sp.wait_ge(z_stored[0], 16 * (NB // 2 + 2))
                sp.wait_ge(z_stored[1], 16 * (NB // 2 + 1))

            @block.tensor
            def _(pe):
                pe.sem_inc(bank_full[7], 1)

                def body(n, slot):
                    r = rows_of(n)
                    pe.wait_ge(x_ready, n + 1)
                    for bank in range(8):
                        pe.wait_ge(bank_read[bank], n + 1)
                        pe.wait_ge(w_ready, w_cols[bank][1] // PIECE)
                        q_tiles = [(j * P, j * P) for j in range(4)]
                        for o, c in (q_tiles, [(0, QW)])[bank] if bank < 2 else ():
                            for k in range(KT):
                                for j, (w, x) in enumerate(((wh, xh), (wh, xl), (wl, xh))):
                                    mm = pe.matmul(ps[:, bank, o:o + r], w[:, k, c:c + P], x[:, slot, k, :r],
                                                   start=k == 0 and j == 0, stop=k == KT - 1 and j == 2)
                        c0, c1 = w_cols[bank]
                        o = 0 if bank > 1 else P
                        if bank:
                            for k in range(KT):
                                for j, (x, w) in enumerate(((xh, wh), (xh, wl), (xl, wh))):
                                    mm = pe.matmul(ps[:r, bank, o:o + c1 - c0], x[:, slot, k, :r], w[:, k, c0:c1],
                                                   start=k == 0 and j == 0, stop=k == KT - 1 and j == 2)
                        mm.then_inc(bank_full[bank], 1)

                over_blocks(pe, body)

            @block.scalar
            def _(act):
                for bank in (0, 2, 4, 5, 6, 7):
                    act.sem_inc(bank_read[bank], 1)

                def high_x(n, slot):
                    act.wait_ge(x_loaded[slot], (n - slot) * 8 + 16)
                    act.activation(xh[:, slot], xt[:, slot], ACT.Copy).then_inc(x_high, 1)

                high_x(0, 0)
                for j in range(PIECES):
                    act.wait_ge(w_loaded[j % 2], 16 * (j // 2 + 1))
                    act.activation(wh[:, :, j * PIECE:(j + 1) * PIECE], piece[:, j % 2], ACT.Copy, scale=SW).then_inc(w_high, 1)

                def body(n, slot):
                    r = rows_of(n)
                    if not (isinstance(n, int) and n == NB):
                        high_x(n + 1, 1 - slot)
                    act.wait_ge(z_stored[slot], (n - slot) * 8 + 16)
                    act.wait_ge(bank_full[0], n + 1)
                    act.activation(z[:, slot, 0:QW].rearrange("p (j t) -> p j t", j=4)[:, :, :r],
                                   ps[:, 0, :].rearrange("p (j t) -> p j t", j=4)[:, :, :r],
                                   ACT.Copy, scale=1.0 / SW).then_inc(bank_read[0], 1)
                    act.wait_ge(bank_full[2], n + 1)
                    act.activation(z[:r, slot, ZU:ZV], ps[:r, 2, :], ACT.Copy, scale=1.0 / SW).then_inc(bank_read[2], 1)
                    for j in range(4):
                        if j == 3:
                            act.wait_ge(bank_full[7], n + 2)
                        else:
                            act.wait_ge(bank_full[4 + j], n + 1)
                        act.activation(z[:r, slot, ZG + 512 * j:ZG + 512 * j + 512], ps[:r, 4 + j, :],
                                       ACT.Tanh, scale=0.5 / SW).then_inc(bank_read[4 + j], 1)
                    act.drain().then_inc(z_act, 1)

                over_blocks(act, body)

            @block.gpsimd
            def _(pool):
                pool.memset(power[:], -0.5)
                pool.memset(z[:], 0.0)
                pool.drain()
                pool.sem_inc(z_stored[0], 16)
                pool.sem_inc(z_stored[1], 16)
                over_blocks(pool, lambda n, slot: inverse_deviation(pool, rows_of(n), mv, power, rstd, var_ready, rstd_ready, n + 1))

            @block.vector
            def _(dve):
                for bank in (1, 3):
                    dve.sem_inc(bank_read[bank], 1)

                def low_x(n, slot):
                    dve.wait_ge(x_high, n + 1)
                    dve.tensor_tensor(xl[:, slot], xt[:, slot], xh[:, slot], ALU.subtract).then_inc(x_ready, 1)

                low_x(0, 0)
                for j in range(PIECES):
                    cols = slice(j * PIECE, (j + 1) * PIECE)
                    dve.wait_ge(w_high, j + 1)
                    dve.scalar_tensor_tensor(wl[:, :, cols], piece[:, j % 2], SW, wh[:, :, cols], ALU.mult,
                                             ALU.subtract).then_inc(w_ready, 1)
                dve.wait_ge(const_loaded, 32)

                def body(n, slot):
                    r = rows_of(n)
                    if not (isinstance(n, int) and n == NB):
                        low_x(n + 1, 1 - slot)
                    dve.wait_ge(z_stored[slot], (n - slot) * 8 + 16)
                    dve.wait_ge(bank_full[1], n + 1)
                    dve.tensor_scalar(z[:, slot, ZK:ZK + r], ps[:, 1, 0:r], 1.0 / SW, None, ALU.mult)
                    dve.tensor_scalar(z[:r, slot, ZKV:ZU], ps[:r, 1, P:P + 2 * KVW], 1.0 / SW, None, ALU.mult).then_inc(bank_read[1], 1)
                    dve.wait_ge(bank_full[3], n + 1)
                    layer_norm_stats(dve, [ps[:r, 3, :]], r, stats, mv, var_ready, rstd_ready, n + 1, EPS * SW * SW)
                    out = z[:r, slot, ZV:ZG]
                    dve.tensor_scalar(out, ps[:r, 3, :], mv[:r, 0:1], rstd[:r, :], ALU.subtract,
                                      ALU.mult).then_inc(bank_read[3], 1)
                    dve.drain()
                    dve.tensor_tensor(out, out, gain[:r, :], ALU.mult)
                    dve.drain()
                    dve.tensor_tensor(out, out, shift[:r, :], ALU.add)
                    dve.drain().then_inc(z_dve, 1)

                over_blocks(dve, body)


def mix_prompt_stage(nc, a):
    with ExitStack() as stack:
        s = Space(nc, stack, "mix")
        za = s.sb("za", [P, 2, ZG])
        prev = s.sb("prev", [P, 2, 3 * P])
        bias = s.sb("bias", [P, HEADS, 2 * P])
        sink = s.sb("sink", [P, HEADS])
        ident = s.sb("ident", [P, P])
        ws = s.sb("ws", [P, CG, P])
        tril = s.sb("tril", [P, P])
        bs = s.sb("bs", [P, CG])
        sc = s.sb("sc", [P, HEADS, 2 * P])
        m, negm, total, esink, dsink = (s.sb(x, [P, HEADS]) for x in ("m", "negm", "total", "esink", "dsink"))
        prT = s.sb("prT", [P, 2 * HEADS, P])
        yc = s.sb("yc", [P, CW])
        yt = s.sb("yt", [P, 2, 8, P])
        ps = s.psum("ps", [P, 8, 512])
        const_loaded, ws_ready = s.sem("const_loaded"), s.sem("ws_ready")
        loaded = s.sems("loaded", 2)
        left_loaded = s.sem("left_loaded")
        biased = s.sem("biased")
        scores_full = s.sem("scores_full")
        maxed = s.sem("maxed")
        exped = s.sem("exped")
        normed = s.sem("normed")
        gm_full, yc_ready, ycT_full, ycT_read = (s.sem(x) for x in ("gm_full", "yc_ready", "ycT_full", "ycT_read"))
        prT_full, prT_read = s.sems("prT_full", 4), s.sems("prT_read", 4)
        ya_full, ya_read = s.sem("ya_full"), s.sem("ya_read")
        y_stored = s.sems("y_stored", 2)

        with nc.Block() as block:

            def toeplitz(k0):
                return bass.AP(a.rev.tensor, k0 + P - 1, [[TOEP - 1, P], [P * TOEP, HEADS], [1, P]])

            @block.sync
            def _(sp):
                def load(n, slot):
                    sp.dma_start(za[:, slot], a.z[bass.ds(n + 1, 1), :, 0:ZG]).then_inc(loaded[slot], 16)
                    sp.dma_start(prev[:, slot, 0:3 * P], a.z[bass.ds(n, 1), :, ZK:ZK + 3 * P]).then_inc(loaded[slot], 16)

                load(0, 0)
                for dst, src in ((ident, a.c_ident), (ws, a.wsT), (tril, a.c_tril), (bs, a.bsT), (sink, a.sink_rows),
                                 (bias[:, :, P:2 * P], toeplitz(P))):
                    sp.dma_start(dst[:], src).then_inc(const_loaded, 16)
                with sp.Fori(0, NB // 2) as i:
                    for slot in range(2):
                        n = i * 2 + slot
                        if slot == 0:
                            sp.wait_ge(y_stored[1], i * 16 + 16)
                            load(n + 1, 1)
                        else:
                            sp.wait_ge(y_stored[0], i * 16 + 32)
                            load(n + 1, 0)
                        sp.wait_ge(biased, n + 1)
                        sp.dma_start(bias[:, :, 0:P], toeplitz(0)).then_inc(left_loaded, 16)
                        sp.wait_ge(ya_read, n + 2)
                        sp.wait_ge(ycT_read, n + 2)
                        sp.dma_start(a.yT[bass.ds(n, 1)], yt[:, slot]).then_inc(y_stored[slot], 16)
                sp.dma_start(a.k_prompt, a.z[NB, :, ZKV:ZKV + KVW]).then_inc(const_loaded, 16)
                sp.dma_start(a.v_prompt, a.z[NB, :, ZKV + KVW:ZU]).then_inc(const_loaded, 16)
                sp.wait_ge(const_loaded, 8 * 16)
                for slot in range(2):
                    sp.wait_ge(y_stored[slot], 16 * (NB // 2 + 1))
                sp.wait_ge(loaded[0], 32 * (NB // 2 + 1))
                sp.wait_ge(left_loaded, 16 * (NB + 1))

            @block.tensor
            def _(pe):
                pe.wait_ge(const_loaded, 6 * 16)

                def body(n, slot):
                    pe.wait_ge(loaded[slot], (n - slot) * 16 + 32)
                    pe.wait_ge(ya_read, n + 1)
                    for h in range(HEADS):
                        g, r = divmod(h, REP)
                        lo = g * HD
                        for half in range(2):
                            kT = prev[lo:lo + HD, slot, 0:P] if half == 0 else za[lo:lo + HD, slot, ZK:ZK + P]
                            mm = pe.matmul(ps[:, h // 2, (h % 2) * 256 + half * P:(h % 2) * 256 + half * P + P],
                                           za[lo:lo + HD, slot, r * P:(r + 1) * P], kT, start=True, stop=True)
                    mm.then_inc(scores_full, 1)
                    pe.wait_ge(ws_ready, 1)
                    pe.wait_ge(prT_read[0], n + 1)
                    for g in range(CG):
                        mm = pe.matmul(ps[:, 4, g * P:(g + 1) * P], ws[:, g, :],
                                       za[:, slot, ZV + g * P:ZV + (g + 1) * P], start=True, stop=True)
                    mm.then_inc(gm_full, 1)
                    pe.wait_ge(yc_ready, n + 1)
                    pe.wait_ge(prT_read[1], n + 1)
                    for g in range(CG):
                        mm = pe.transpose(ps[:, 5, g * P:(g + 1) * P], yc[:, g * P:(g + 1) * P], ident[:])
                    mm.then_inc(ycT_full, 1)
                    pe.wait_ge(normed, n + 1)
                    for q in range(4):
                        if q == 1:
                            pe.wait_ge(ycT_read, n + 2)
                        pe.wait_ge(prT_read[q], n + 1)
                        for j in range(4):
                            h, half = 2 * q + j // 2, j % 2
                            mm = pe.transpose(ps[:, 4 + q, j * P:(j + 1) * P], sc[:, h, half * P:(half + 1) * P], ident[:])
                        mm.then_inc(prT_full[q], 1)
                    for h in range(HEADS):
                        g, r = divmod(h, REP)
                        lo = g * HD
                        if h % 2 == 0:
                            pe.wait_ge(prT_read[h // 2], n + 2)
                        pe.matmul(ps[lo:lo + HD, 0, r * P:(r + 1) * P], prev[:, slot, 2 * P + lo:2 * P + lo + HD],
                                  prT[:, 2 * h, :], start=True, stop=False)
                        mm = pe.matmul(ps[lo:lo + HD, 0, r * P:(r + 1) * P],
                                       za[:, slot, ZKV + KVW + lo:ZKV + KVW + lo + HD],
                                       prT[:, 2 * h + 1, :], start=False, stop=True)
                    mm.then_inc(ya_full, 1)

                with pe.Fori(0, NB // 2) as i:
                    body(i * 2, 0)
                    body(i * 2 + 1, 1)

            @block.scalar
            def _(act):
                act.sem_inc(ya_read, 1)
                act.sem_inc(prT_read[0], 1)
                act.sem_inc(prT_read[1], 1)
                act.sem_inc(y_stored[0], 16)
                act.sem_inc(y_stored[1], 16)

                def body(n, slot):
                    act.wait_ge(maxed, n + 1)
                    for h in range(HEADS):
                        act.activation(sc[:, h, :], sc[:, h, :], ACT.Exp, bias=negm[:, h:h + 1],
                                       accum_out=total[:, h:h + 1])
                    act.activation(esink[:], dsink[:], ACT.Exp)
                    act.drain().then_inc(exped, 1)
                    act.wait_ge(y_stored[slot], (n - slot) * 8 + 16)
                    for q in (0, 1):
                        act.wait_ge(prT_full[q], n + 1)
                        act.activation(prT[:, 4 * q:4 * q + 4, :], ps[:, 4 + q, :].rearrange("p (j t) -> p j t", j=4),
                                       ACT.Copy).then_inc(prT_read[q], 1)
                    act.wait_ge(ya_full, n + 1)
                    act.activation(yt[:, slot, 0:4, :], ps[:, 0, :].rearrange("p (j t) -> p j t", j=4),
                                   ACT.Copy).then_inc(ya_read, 1)

                with act.Fori(0, NB // 2) as i:
                    body(i * 2, 0)
                    body(i * 2 + 1, 1)

            @block.gpsimd
            def _(pool):
                pool.memset(bias[:, :, 0:P], NEG)
                pool.drain()
                pool.sem_inc(left_loaded, 16)

            @block.vector
            def _(dve):
                dve.sem_inc(prT_read[2], 1)
                dve.sem_inc(prT_read[3], 1)
                dve.sem_inc(ycT_read, 1)
                dve.wait_ge(const_loaded, 6 * 16)
                for g in range(CG):
                    last = dve.tensor_tensor(ws[:, g, :], ws[:, g, :], tril[:], ALU.mult)
                last.then_inc(ws_ready, 1)

                def body(n, slot):
                    dve.wait_ge(left_loaded, n * 16 + 16)
                    dve.wait_ge(scores_full, n + 1)
                    for q in range(4):
                        dve.scalar_tensor_tensor(sc[:, 2 * q:2 * q + 2, :], ps[:, q, :].rearrange("p (h k) -> p h k", h=2),
                                                 HD ** -0.5, bias[:, 2 * q:2 * q + 2, :], ALU.mult, ALU.add)
                    dve.drain().then_inc(biased, 1)
                    dve.tensor_reduce(m[:], sc[:], X, ALU.max)
                    dve.drain()
                    dve.tensor_tensor(m[:], m[:], sink[:], ALU.max)
                    dve.drain()
                    dve.tensor_scalar(negm[:], m[:], -1.0, None, ALU.mult)
                    dve.tensor_tensor(dsink[:], sink[:], m[:], ALU.subtract)
                    dve.drain().then_inc(maxed, 1)
                    dve.wait_ge(gm_full, n + 1)
                    for g in range(CG):
                        cols = slice(g * P, (g + 1) * P)
                        dve.scalar_tensor_tensor(yc[:, cols], ps[:, 4, cols], bs[:, g:g + 1],
                                                 za[:, slot, ZU + g * P:ZU + (g + 1) * P], ALU.add, ALU.mult)
                    dve.drain().then_inc(yc_ready, 1)
                    dve.wait_ge(ycT_full, n + 1)
                    dve.wait_ge(y_stored[slot], (n - slot) * 8 + 16)
                    dve.tensor_copy(yt[:, slot, 4:8, :], ps[:, 5, :].rearrange("p (j t) -> p j t", j=4)).then_inc(ycT_read, 1)
                    dve.wait_ge(exped, n + 1)
                    dve.tensor_tensor(total[:], total[:], esink[:], ALU.add)
                    dve.drain()
                    dve.reciprocal(total[:], total[:])
                    dve.drain()
                    dve.tensor_tensor(sc[:], sc[:], total[:].unsqueeze(2).broadcast_to([P, HEADS, 2 * P]), ALU.mult)
                    dve.drain().then_inc(normed, 1)
                    for q in (2, 3):
                        dve.wait_ge(prT_full[q], n + 1)
                        dve.tensor_copy(prT[:, 4 * q:4 * q + 4, :],
                                        ps[:, 4 + q, :].rearrange("p (j t) -> p j t", j=4)).then_inc(prT_read[q], 1)

                with dve.Fori(0, NB // 2) as i:
                    body(i * 2, 0)
                    body(i * 2 + 1, 1)


def mix_sample_stage(nc, a):
    S4 = SEQS // 4
    KA = P + NEW
    with ExitStack() as stack:
        s = Space(nc, stack, "smix")
        za = s.sb("za", [P, ZG])
        qs = s.sb("qs", [P, SEQS, REP, NEW])
        ckT = s.sb("ckT", [P, SEQS, P])
        cv = s.sb("cv", [P, SEQS, P])
        vnew = s.sb("vnew", [NEW, SEQS, P])
        bias = s.sb("bias", [P, GROUPS, KA])
        sink = s.sb("sink", [P, S4, GROUPS])
        ident = s.sb("ident", [P, P])
        ws = s.sb("ws", [SAMPLE, CG, SAMPLE])
        tril = s.sb("tril", [P, P])
        bs = s.sb("bs", [SAMPLE, CG])
        sc = s.sb("sc", [P, S4, GROUPS, KA])
        m, negm, total, esink, dsink = (s.sb(x, [P, S4, GROUPS]) for x in ("m", "negm", "total", "esink", "dsink"))
        prT = s.sb("prT", [P, S4 * GROUPS, P])
        prN = s.sb("prN", [NEW, S4 * GROUPS, P])
        yc = s.sb("yc", [SAMPLE, CW])
        yt = s.sb("yt", [P, 8, P])
        ps = s.psum("ps", [P, 8, 512])
        loaded, ws_ready, outs, q_ready = (s.sem(x) for x in ("loaded", "ws_ready", "outs", "q_ready"))
        names = ("scores_full", "maxed", "exped", "normed", "gm_full", "yc_ready", "ycT_full", "prT_full", "prT_read",
                 "ya_full", "y_act", "y_dve")
        scores_full, maxed, exped, normed, gm_full, yc_ready, ycT_full, prT_full, prT_read, ya_full, y_act, y_dve = map(s.sem, names)
        with nc.Block() as block:

            @block.sync
            def _(sp):
                sp.dma_start(za[:], a.z[NB + 1, :, 0:ZG]).then_inc(loaded, 16)
                sp.dma_start(ckT[:], a.cache_kT).then_inc(loaded, 16)
                sp.dma_start(cv[:], a.cache_v).then_inc(loaded, 16)
                sp.dma_start(vnew[:], a.z[NB + 1, 0:SAMPLE, ZKV + KVW:ZU].rearrange("(s j) c -> j s c", j=NEW)).then_inc(loaded, 16)
                sp.dma_start(ident[:], a.c_ident).then_inc(loaded, 16)
                sp.dma_start(tril[:], a.c_tril).then_inc(loaded, 16)
                sp.dma_start(bs[:], a.bs_sample).then_inc(loaded, 16)
                sp.dma_start(sink[:], a.sink_sample).then_inc(loaded, 16)
                sp.dma_start(ws[:], a.ws_sample).then_inc(loaded, 16)
                for q in range(4):
                    for r in range(REP):
                        row = q * 32 + r * NEW
                        sp.dma_start(bias[row:row + NEW, :, :],
                                     bass.AP(a.rev.tensor, r * P * TOEP + P - 1,
                                             [[TOEP - 1, NEW], [REP * P * TOEP, GROUPS], [1, KA]])).then_inc(loaded, 16)
                for win, cache, c0 in ((a.k_sample, a.cache_k_rows, ZKV), (a.v_sample, a.cache_v_rows, ZKV + KVW)):
                    sp.dma_start(win[:, 0:P - NEW, :], cache[:, NEW:P, :]).then_inc(outs, 16)
                    sp.dma_start(win[:, P - NEW:P, :],
                                 a.z[NB + 1, 0:SAMPLE, c0:c0 + KVW].rearrange("(s j) c -> s j c", j=NEW)).then_inc(outs, 16)
                sp.dma_start(a.chunk_v, a.z[NB + 1, 0:SAMPLE, ZV:ZG]).then_inc(outs, 16)
                sp.wait_ge(y_act, 1)
                sp.wait_ge(y_dve, 2)
                sp.dma_start(a.yT[NB], yt[:]).then_inc(outs, 16)
                sp.wait_ge(outs, 6 * 16)

            n_loads = 9 + 16

            @block.tensor
            def _(pe):
                pe.wait_ge(loaded, 16 * n_loads)
                pe.wait_ge(q_ready, 1)
                for b in range(SEQS):
                    quad, hi = b % 4, b // 4
                    for g in range(GROUPS):
                        rows = slice(g * HD, (g + 1) * HD)
                        q = qs[rows, b].rearrange("p r j -> p (r j)")
                        out = ps[quad * 32:(quad + 1) * 32, hi * GROUPS + g, :]
                        pe.matmul(out[:, 0:P], q, ckT[rows, b, :], start=True, stop=True)
                        mm = pe.matmul(out[:, P:KA], q, za[rows, ZK + b * NEW:ZK + (b + 1) * NEW],
                                       start=True, stop=True)
                mm.then_inc(scores_full, 1)
                pe.wait_ge(ws_ready, 1)
                for g in range(CG):
                    mm = pe.matmul(ps[0:SAMPLE, 4, g * P:(g + 1) * P], ws[:, g, :],
                                   za[0:SAMPLE, ZV + g * P:ZV + (g + 1) * P], start=True, stop=True)
                mm.then_inc(gm_full, 1)
                pe.wait_ge(yc_ready, 1)
                for g in range(CG):
                    mm = pe.transpose(ps[:, 5, g * P:g * P + SAMPLE], yc[:, g * P:(g + 1) * P], ident[0:SAMPLE, 0:SAMPLE])
                mm.then_inc(ycT_full, 1)
                pe.wait_ge(normed, 1)
                for j in range(S4 * GROUPS):
                    pr = sc[:, j // GROUPS, j % GROUPS, :]
                    pe.transpose(ps[:, 6, j * P:(j + 1) * P], pr[:, 0:P], ident[:])
                    mm = pe.transpose(ps[0:NEW, 7, j * P:(j + 1) * P], pr[:, P:KA], ident[:])
                mm.then_inc(prT_full, 1)
                pe.wait_ge(prT_read, 1)
                for b in range(SEQS):
                    quad, hi = b % 4, b // 4
                    for g in range(GROUPS):
                        out = ps[g * HD:(g + 1) * HD, 0, 0:REP * SAMPLE].rearrange("p (r t) -> p r t", r=REP)[:, :, b * NEW:(b + 1) * NEW]
                        j = hi * GROUPS + g
                        cols = slice(quad * 32, quad * 32 + 32)
                        pe.matmul(out, cv[:, b, g * HD:(g + 1) * HD], prT[:, j, cols].rearrange("p (r t) -> p r t", r=REP), start=True, stop=False)
                        mm = pe.matmul(out, vnew[:, b, g * HD:(g + 1) * HD], prN[:, j, cols].rearrange("p (r t) -> p r t", r=REP), start=False, stop=True)
                mm.then_inc(ya_full, 1)

            @block.scalar
            def _(act):
                act.wait_ge(loaded, 16 * n_loads)
                for r in range(REP):
                    act.activation(qs[:, :, r, :], za[:, r * P:r * P + SAMPLE].rearrange("p (s j) -> p s j", j=NEW), ACT.Copy)
                act.drain().then_inc(q_ready, 1)
                act.wait_ge(maxed, 1)
                for b in range(S4):
                    for g in range(GROUPS):
                        act.activation(sc[:, b, g, :], sc[:, b, g, :], ACT.Exp, bias=negm[:, b, g:g + 1],
                                       accum_out=total[:, b, g:g + 1])
                act.activation(esink[:], dsink[:], ACT.Exp)
                act.drain().then_inc(exped, 1)
                act.wait_ge(prT_full, 1)
                act.activation(prT[:], ps[:, 6, :].rearrange("p (j t) -> p j t", j=4), ACT.Copy)
                act.activation(prN[:], ps[0:NEW, 7, :].rearrange("p (j t) -> p j t", j=4), ACT.Copy)
                act.drain().then_inc(prT_read, 1)
                act.wait_ge(y_dve, 1)
                act.wait_ge(ya_full, 1)
                act.activation(yt[:, 0:4, 0:SAMPLE], ps[:, 0, 0:REP * SAMPLE].rearrange("p (r t) -> p r t", r=REP),
                               ACT.Copy).then_inc(y_act, 1)

            @block.vector
            def _(dve):
                dve.memset(yt[:], 0.0)
                dve.drain().then_inc(y_dve, 1)
                dve.wait_ge(loaded, 16 * n_loads)
                for g in range(CG):
                    last = dve.tensor_tensor(ws[:, g, :], ws[:, g, :], tril[0:SAMPLE, 0:SAMPLE], ALU.mult)
                last.then_inc(ws_ready, 1)
                dve.wait_ge(scores_full, 1)
                for b in range(S4):
                    dve.scalar_tensor_tensor(sc[:, b], ps[:, GROUPS * b:GROUPS * b + GROUPS, 0:KA],
                                             HD ** -0.5, bias[:], ALU.mult, ALU.add)
                dve.drain()
                dve.tensor_reduce(m[:], sc[:], X, ALU.max)
                dve.drain()
                dve.tensor_tensor(m[:], m[:], sink[:], ALU.max)
                dve.drain()
                dve.tensor_scalar(negm[:], m[:], -1.0, None, ALU.mult)
                dve.tensor_tensor(dsink[:], sink[:], m[:], ALU.subtract)
                dve.drain().then_inc(maxed, 1)
                dve.wait_ge(gm_full, 1)
                for g in range(CG):
                    cols = slice(g * P, (g + 1) * P)
                    dve.scalar_tensor_tensor(yc[:, cols], ps[0:SAMPLE, 4, cols], bs[:, g:g + 1],
                                             za[0:SAMPLE, ZU + g * P:ZU + (g + 1) * P], ALU.add, ALU.mult)
                dve.drain().then_inc(yc_ready, 1)
                dve.wait_ge(exped, 1)
                dve.tensor_tensor(total[:], total[:], esink[:], ALU.add)
                dve.drain()
                dve.reciprocal(total[:], total[:])
                dve.drain()
                for b in range(S4):
                    for g in range(GROUPS):
                        dve.tensor_scalar(sc[:, b, g, :], sc[:, b, g, :], total[:, b, g:g + 1], None, ALU.mult)
                dve.drain().then_inc(normed, 1)
                dve.wait_ge(ycT_full, 1)
                dve.tensor_copy(yt[:, 4:8, 0:SAMPLE],
                                ps[:, 5, :].rearrange("p (j t) -> p j t", j=4)[:, :, 0:SAMPLE]).then_inc(y_dve, 1)


def merge_stage(nc, a):
    with ExitStack() as stack:
        s = Space(nc, stack, "merge")
        wa, wc = s.sb("wa", [P, 4, D]), s.sb("wc", [P, 4, D])
        wo, wpg, wpp = s.sb("wo", [P, KT, D]), s.sb("wpg", [P, KT, D]), s.sb("wpp", [P, 2, D])
        gain, shift, ident = s.sb("gain", [P, D]), s.sb("shift", [P, D]), s.sb("ident", [P, P])
        yt, gates = s.sb("yt", [P, 2, 8, P]), s.sb("gates", [P, 2, 2 * D])
        x, pt = s.sb("x", [P, 2, D]), s.sb("pt", [P, 2, 2, P])
        t1, t2, mt, x1 = s.sb("t1", [P, D]), s.sb("t2", [P, D]), s.sb("mt", [P, KT, P]), s.sb("x1", [P, D])
        x1t, xh, xl = s.sb("x1t", [P, KT, P]), s.sb("xh", [P, KT, P], F16), s.sb("xl", [P, KT, P], F16)
        pp, tg, base = s.sb("pp", [P, D]), s.sb("tg", [P, D]), s.sb("base", [P, D])
        stats, mv, rstd = s.sb("stats", [P, 2, 6]), s.sb("mv", [P, 2]), s.sb("rstd", [P, 1])
        power = s.sb("power", [P, 1])
        ps = s.psum("ps", [P, 8, 512])
        w_loaded = {k: s.sem(f"w_loaded_{k}") for k in ("wa", "wc", "wo", "wpg", "wpp", "const")}
        loaded = s.sems("loaded", 2)
        (ac_full, ac_read, mix_ready, mixT_full, mixT_read, o_full, o_read, x_scaled, x1_ready, x1T_full, x1T_read,
         xl_ready, gate_full, gate_act, base_ready, pp_full, pp_read) = (s.sem(k) for k in (
             "ac_full", "ac_read", "mix_ready", "mixT_full", "mixT_read", "o_full", "o_read", "x_scaled", "x1_ready",
             "x1T_full", "x1T_read", "xl_ready", "gate_full", "gate_act", "base_ready", "pp_full", "pp_read"))
        stored = s.sem("stored")
        var_ready, rstd_ready = s.sem("var_ready"), s.sem("rstd_ready")

        with nc.Block() as block:

            @block.sync
            def _(sp):
                def load(n, slot):
                    for dst, src in ((yt, a.yT[bass.ds(n, 1)]), (gates, a.z[bass.ds(n + 1, 1), :, ZG:ZW]),
                                     (x, a.x_blocks[bass.ds(n, 1)]), (pt, a.pt_blocks[bass.ds(n, 1)])):
                        sp.dma_start(dst[:, slot], src).then_inc(loaded[slot], 16)

                sp.dma_start(wa[:], a.wa).then_inc(w_loaded["wa"], 16)
                load(0, 0)
                for k, dst, src in (("wc", wc, a.wc), ("const", ident, a.c_ident), ("wo", wo, a.wo),
                                    ("const", gain, a.ln1_g), ("const", shift, a.ln1_b), ("wpg", wpg, a.wpg), ("wpp", wpp, a.wpp)):
                    sp.dma_start(dst[:], src).then_inc(w_loaded[k], 16)

                def store(n):
                    sp.wait_ge(x1T_read, n + 1)
                    sp.wait_ge(xl_ready, n + 1)
                    cols = bass.ds(n * P, P)
                    sp.dma_start(a.x1T[bass.ds(n, 1)], x1t[:]).then_inc(stored, 16)
                    sp.dma_start(a.xh[:, :, cols], xh[:]).then_inc(stored, 16)
                    sp.dma_start(a.xl[:, :, cols], xl[:]).then_inc(stored, 16)
                    sp.wait_ge(base_ready, n + 2)
                    sp.dma_start(a.base[bass.ds(n, 1)], base[:]).then_inc(stored, 16)

                with sp.Fori(0, NB // 2) as i:
                    for slot in range(2):
                        n = i * 2 + slot
                        sp.wait_ge(base_ready, n + 1)
                        load(n + 1, 1 - slot)
                        store(n)
                store(NB)
                sp.dma_start(a.x1_sample, x1[0:SAMPLE, :]).then_inc(stored, 16)
                sp.wait_ge(stored, (NB + 2) * 64 + 16)

            @block.tensor
            def _(pe):
                def product(bank, lhs, w, kt):
                    for c in range(2):
                        for k in range(kt):
                            mm = pe.matmul(ps[:, bank + c, :], lhs[:, k, :], w[:, k, c * 512:(c + 1) * 512],
                                           start=k == 0, stop=k == kt - 1)
                    return mm

                def transposes(bank, src):
                    for k in range(KT):
                        mm = pe.transpose(ps[:, bank + k // 4, (k % 4) * P:(k % 4 + 1) * P], src[:, k * P:(k + 1) * P], ident[:])
                    return mm

                def branches(n, slot):
                    pe.wait_ge(loaded[slot], (n - slot) * 32 + 64)
                    product(0, yt[:, slot, 0:4], wa, 4)
                    product(2, yt[:, slot, 4:8], wc, 4).then_inc(ac_full, 1)

                for k in ("wa", "wc"):
                    pe.wait_ge(w_loaded[k], 16)
                branches(0, 0)
                pe.wait_ge(w_loaded["const"], 48)

                def body(n, slot):
                    pe.wait_ge(mix_ready, n + 1)
                    transposes(4, t1).then_inc(mixT_full, 1)
                    pe.wait_ge(gate_act, n + 1)
                    pe.wait_ge(mixT_read, n + 1)
                    pe.wait_ge(w_loaded["wo"], 16)
                    product(6, mt, wo, KT).then_inc(o_full, 1)
                    for k in ("wpg", "wpp"):
                        pe.wait_ge(w_loaded[k], 16)
                    product(4, pt[:, slot], wpp, 2).then_inc(pp_full, 1)
                    if not (isinstance(n, int) and n == NB):
                        branches(n + 1, 1 - slot)
                    pe.wait_ge(pp_read, n + 1)
                    pe.wait_ge(x1_ready, n + 1)
                    transposes(4, x1).then_inc(x1T_full, 1)
                    pe.wait_ge(x1T_read, n + 1)
                    product(6, x1t, wpg, KT).then_inc(gate_full, 1)

                over_blocks(pe, body)

            def two(bank):
                return ps[:, bank:bank + 2, :]

            def halves(t):
                return t.rearrange("p (c n) -> p c n", c=2)

            @block.scalar
            def _(act):
                act.sem_inc(stored, 64)
                act.sem_inc(gate_act, 1)

                def body(n, slot):
                    act.wait_ge(loaded[slot], (n - slot) * 32 + 64)
                    act.activation(x[:, slot], x[:, slot], ACT.Copy, scale=ALPHA).then_inc(x_scaled, 1)
                    act.wait_ge(mixT_full, n + 1)
                    act.activation(mt[:].rearrange("p (c k) t -> p c (k t)", c=2), two(4), ACT.Copy).then_inc(mixT_read, 1)
                    act.wait_ge(base_ready, n + 1)
                    act.wait_ge(pp_full, n + 1)
                    act.activation(halves(pp[:]), two(4), ACT.Copy).then_inc(pp_read, 1)
                    act.wait_ge(x1T_full, n + 1)
                    act.wait_ge(stored, n * 64 + 64)
                    act.activation(x1t[:].rearrange("p (c k) t -> p c (k t)", c=2), two(4), ACT.Copy)
                    act.activation(xh[:].rearrange("p (c k) t -> p c (k t)", c=2), two(4), ACT.Copy)
                    act.drain().then_inc(x1T_read, 1)
                    act.wait_ge(gate_full, n + 1)
                    act.activation(halves(tg[:]), two(6), ACT.Tanh, scale=0.5).then_inc(gate_act, 1)

                over_blocks(act, body)

            @block.gpsimd
            def _(pool):
                pool.memset(power[:], -0.5)
                pool.drain()
                over_blocks(pool, lambda n, slot: inverse_deviation(pool, P, mv, power, rstd, var_ready, rstd_ready, n + 1))

            @block.vector
            def _(dve):
                def mix(n, slot):
                    dve.wait_ge(loaded[slot], (n - slot) * 32 + 64)
                    dve.wait_ge(ac_full, n + 1)
                    dve.scalar_tensor_tensor(halves(t1[:]), halves(gates[:, slot, 0:D]), 1.0, two(0), ALU.add, ALU.mult)
                    dve.scalar_tensor_tensor(halves(t2[:]), halves(gates[:, slot, D:2 * D]), 1.0, two(2), ALU.add, ALU.mult)
                    dve.drain()
                    dve.tensor_tensor(t1[:], t1[:], t2[:], ALU.add)
                    dve.drain().then_inc(mix_ready, 1)

                def body(n, slot):
                    dve.wait_ge(x_scaled, n + 1)
                    dve.wait_ge(o_full, n + 1)
                    dve.scalar_tensor_tensor(halves(x1[:]), two(6), 0.5, halves(x[:, slot]), ALU.mult, ALU.add)
                    dve.drain()
                    layer_norm_stats(dve, [x1[:, 0:512], x1[:, 512:1024]], P, stats, mv, var_ready, rstd_ready, n + 1)
                    dve.tensor_scalar(x1[:], x1[:], mv[:, 0:1], rstd[:, :], ALU.subtract, ALU.mult)
                    dve.drain()
                    dve.tensor_tensor(x1[:], x1[:], gain[:], ALU.mult)
                    dve.drain()
                    dve.tensor_tensor(x1[:], x1[:], shift[:], ALU.add)
                    dve.drain().then_inc(x1_ready, 1)
                    if not (isinstance(n, int) and n == NB):
                        mix(n + 1, 1 - slot)
                    dve.wait_ge(x1T_read, n + 1)
                    dve.tensor_tensor(xl[:], x1t[:], xh[:], ALU.subtract).then_inc(xl_ready, 1)
                    dve.wait_ge(gate_act, n + 2)
                    dve.scalar_tensor_tensor(t2[:], tg[:], 1.0, pp[:], ALU.add, ALU.mult)
                    dve.wait_ge(stored, n * 64 + 64)
                    dve.tensor_scalar(base[:], x1[:], ALPHA, None, ALU.mult)
                    dve.drain()
                    dve.scalar_tensor_tensor(base[:], t2[:], 0.5, base[:], ALU.mult, ALU.add)
                    dve.drain().then_inc(base_ready, 1)

                dve.sem_inc(base_ready, 1)
                mix(0, 0)
                dve.wait_ge(w_loaded["const"], 48)
                over_blocks(dve, body)


def route_stage(nc, a):
    with ExitStack() as stack:
        s = Space(nc, stack, "route")
        wq, sub = s.sb("wq", [P, KT, 2 * PH * P]), s.sb("sub", [P, 2 * PH, KEYS])
        ident, iota, iota16 = s.sb("ident", [P, P]), s.sb("iota", [P, KEYS, BT], F16), s.sb("iota16", [P, TOPK])
        x1t, qt = s.sb("x1t", [P, KT, P]), s.sb("qt", [P, 2 * PH, P])
        sc = s.sb("sc", [P, 2 * PH, KEYS])
        rest = s.sb("rest", [P, 2 * PH * KEYS])
        pair = s.sb("pair", [P, PH, TOPK * TOPK])
        sv, si = s.sb("sv", [P, 2 * PH, TOPK]), s.sb("si", [P, 2 * PH, TOPK], U32)
        sif = s.sb("sif", [P, PH, 2, TOPK])
        fv, fi = s.sb("fv", [P, PH, TOPK]), s.sb("fi", [P, PH, TOPK], U32)
        half_u = s.sb("half_u", [P, 2, PH, TOPK], U32)
        half_f = s.sb("half_f", [P, 2, PH, TOPK])
        pick = s.sb("pick", [P, 3, PH, TOPK])
        gsum = s.sb("gsum", [P, PH])
        col = s.sb("col", [P, 2, P], F16)
        gt, gh, gl = s.sb("gt", [P, P]), s.sb("gh", [P, P], F16), s.sb("gl", [P, P], F16)
        hot_r, hot_c = s.sb("hot_r", [P, 2, KEYS, BT], F16), s.sb("hot_c", [P, 2, KEYS, BT], F16)
        hot_h, hot_l = s.sb("hot_h", [P, 2, KEYS, BT], F16), s.sb("hot_l", [P, 2, KEYS, BT], F16)
        one, scrap = s.sb("one", [P, 1]), s.sb("scrap", [P, 1])
        place_f = s.sb("place_f", [P, 2, SAMPLE])
        place, gate = s.sb("place", [P, SAMPLE], U32), s.sb("gate", [P, SAMPLE])
        gbuf = s.sb("gbuf", [P, KEYS, P])
        ps = s.psum("ps", [P, 8, 512])
        w_loaded = s.sems("w_loaded", 4)
        const_loaded, x_loaded = s.sem("const_loaded"), s.sem("x_loaded")
        q_full, q_read, s_full, s_read = (s.sem(k) for k in ("q_full", "q_read", "s_full", "s_read"))
        sc_used, exp_in, exp_out, picked = (s.sem(k) for k in ("sc_used", "exp_in", "exp_out", "picked"))
        pickT_full = s.sem("pickT_full")
        rows_ready, lows_ready = s.sem("rows_ready"), s.sem("lows_ready")
        hots_ready, places_ready, places_stored = s.sem("hots_ready"), s.sem("places_ready"), s.sem("places_stored")
        g_full, g_read, g_stored = s.sem("g_full"), s.sem("g_read"), s.sem("g_stored")
        block_done = s.sem("block_done")
        batches = P // BT

        def over_batches(eng, n, body):
            if isinstance(n, int) and n == NB:
                return
            with eng.Fori(0, batches // 2) as j:
                body(j * 2, 0)
                body(j * 2 + 1, 1)

        def spread(values):
            return values.unsqueeze(1).broadcast_to([P, KEYS, BT])

        with nc.Block() as block:

            @block.sync
            def _(sp):
                sp.dma_start(x1t[:], a.x1T[0]).then_inc(x_loaded, 16)
                for j in range(4):
                    cols = slice(j * 4 * P, (j + 1) * 4 * P)
                    sp.dma_start(wq[:, :, cols], a.wq[:, :, cols]).then_inc(w_loaded[j], 16)
                for dst, src in ((sub, a.subT), (ident, a.c_ident), (iota, a.c_iota), (iota16, a.c_iota16)):
                    sp.dma_start(dst[:], src).then_inc(const_loaded, 16)

                def load_x(n):
                    sp.wait_ge(q_full, n * 4)
                    sp.dma_start(x1t[:], a.x1T[bass.ds(n, 1)]).then_inc(x_loaded, 16)

                def store_g(n):
                    sp.wait_ge(block_done, n + 1)
                    sp.dma_start(a.g[:, :, bass.ds(n * P, P)].rearrange("i p t -> p i t"), gbuf[:]).then_inc(g_stored, 16)

                load_x(1)
                with sp.Fori(0, NB - 1) as n:
                    load_x(n + 2)
                    store_g(n)
                store_g(NB - 1)
                sp.wait_ge(places_ready, 1)
                sp.dma_start(a.place, place[:]).then_inc(places_stored, 16)
                sp.dma_start(a.gate, gate[:]).then_inc(places_stored, 16)
                sp.wait_ge(places_stored, 32)
                sp.wait_ge(g_stored, 16 * (NB + 1))

            @block.tensor
            def _(pe):
                pe.sem_inc(g_full, 4)

                def queries(n):
                    pe.wait_ge(x_loaded, n * 16 + 16)
                    for j in range(4):
                        pe.wait_ge(q_read, n * 4 + j + 1)
                        pe.wait_ge(w_loaded[j], 16)
                        for t in range(4):
                            c = (4 * j + t) * P
                            for k in range(KT):
                                mm = pe.matmul(ps[:, j % 2, t * P:(t + 1) * P], wq[:, k, c:c + P], x1t[:, k, :],
                                               start=k == 0, stop=k == KT - 1)
                        mm.then_inc(q_full, 1)

                def scores(n):
                    for j in range(4):
                        pe.wait_ge(q_read, n * 4 + j + 3)
                        pe.wait_ge(s_read, n * 4 + j + 1)
                        for t in range(4):
                            hc = 4 * j + t
                            mm = pe.matmul(ps[:, 2, t * P:(t + 1) * P], qt[:, hc, :], sub[:, hc, :], start=True, stop=True)
                        mm.then_inc(s_full, 1)

                queries(0)
                pe.wait_ge(const_loaded, 64)
                scores(0)

                def body(n, slot):
                    if not (isinstance(n, int) and n == NB):
                        queries(n + 1)
                    pe.wait_ge(picked, n + 1)
                    for j in range(3):
                        mm = pe.transpose(ps[:, 3, j * P:(j + 1) * P], pick[:, j].rearrange("p h k -> p (h k)"), ident[:])
                    mm.then_inc(pickT_full, 1)
                    if not (isinstance(n, int) and n == NB):
                        scores(n + 1)

                    def batch(b, half):
                        pe.wait_ge(hots_ready, n * batches + b + 1)
                        pe.wait_ge(lows_ready, n * batches + b + 3)
                        for q in range(BT // 4):
                            pe.wait_ge(g_read, (n * batches + b) * 2 + q + 1)
                            for t in range(4):
                                o = ps[:, 4 + 2 * half + q, t * P:(t + 1) * P]
                                tt = 4 * q + t
                                pe.matmul(o, hot_c[:, half, :, tt], hot_h[:, half, :, tt], start=True, stop=False)
                                mm = pe.matmul(o, hot_c[:, half, :, tt], hot_l[:, half, :, tt], start=False, stop=True)
                            mm.then_inc(g_full, 1)
                    over_batches(pe, n, batch)

                over_blocks(pe, body)

            @block.scalar
            def _(act):
                act.sem_inc(q_read, 2)
                act.sem_inc(s_read, 1)
                act.sem_inc(g_read, 4)
                act.sem_inc(g_stored, 16)
                act.sem_inc(sc_used, 1)

                def queries(n):
                    for j in range(4):
                        act.wait_ge(q_full, n * 4 + j + 1)
                        act.activation(qt[:, 4 * j:4 * j + 4, :], ps[:, j % 2, :].rearrange("p (t n) -> p t n", t=4),
                                       ACT.Copy).then_inc(q_read, 1)

                def scores(n):
                    act.wait_ge(sc_used, n + 1)
                    for j in range(4):
                        act.wait_ge(s_full, n * 4 + j + 1)
                        act.activation(sc[:, 4 * j:4 * j + 4, :], ps[:, 2, :].rearrange("p (t n) -> p t n", t=4),
                                       ACT.Copy).then_inc(s_read, 1)

                queries(0)
                scores(0)

                def body(n, slot):
                    if not (isinstance(n, int) and n == NB):
                        queries(n + 1)
                    act.wait_ge(exp_in, n + 1)
                    act.activation(pick[:, 2], pick[:, 2], ACT.Exp).then_inc(exp_out, 1)
                    if not (isinstance(n, int) and n == NB):
                        scores(n + 1)
                    if isinstance(n, int) and n == NB:
                        return
                    act.wait_ge(g_stored, n * 16 + 16)

                    def batch(b, half):
                        for q in range(BT // 4):
                            act.wait_ge(g_full, (n * batches + b) * 2 + q + 5)
                            act.wait_ge(const_loaded, 64)
                            act.activation(gbuf[:, :, bass.ds(b * BT + 4 * q, 4)],
                                           ps[:, 4 + 2 * half + q, :].rearrange("p (t i) -> p i t", t=4),
                                           ACT.Copy).then_inc(g_read, 1)
                    over_batches(act, n, batch)
                    act.drain().then_inc(block_done, 1)

                over_blocks(act, body)

            @block.gpsimd
            def _(pool):
                pool.memset(one[:], 1.0)
                pool.drain()
                pool.sem_inc(lows_ready, 2)

                def body(n, slot):
                    def batch(b, half):
                        pool.wait_ge(g_full, (n * batches + b) * 2 + 2)
                        pool.wait_ge(rows_ready, n * batches + b + 1)
                        pool.tensor_tensor(scrap[:], one[:], one[:], ALU.mult)
                        pool.tensor_tensor(hot_l[:, half], hot_r[:, half], spread(gl[:, bass.ds(b * BT, BT)]), ALU.mult)
                        pool.drain().then_inc(lows_ready, 1)
                    over_batches(pool, n, batch)

                over_blocks(pool, body)

            @block.vector
            def _(dve):
                dve.wait_ge(const_loaded, 64)

                def top16(scores, rest, values, indices):
                    n = len(scores)
                    for j in range(n):
                        dve.max(values[j][:, 0:8], scores[j])
                    dve.drain()
                    for j in range(n):
                        dve.max_index(indices[j][:, 0:8], values[j][:, 0:8], scores[j])
                        dve.match_replace(rest[j], values[j][:, 0:8], scores[j], LOWEST)
                    dve.drain()
                    for j in range(n):
                        dve.max(values[j][:, 8:16], rest[j])
                    dve.drain()
                    for j in range(n):
                        dve.max_index(indices[j][:, 8:16], values[j][:, 8:16], rest[j])

                def body(n, slot):
                    dve.wait_ge(s_read, n * 4 + 5)
                    dve.memset(gsum[:], 0.0)
                    hc = range(2 * PH)
                    top16([sc[:, j, :] for j in hc], [rest[:, j * KEYS:(j + 1) * KEYS] for j in hc],
                          [sv[:, j, :] for j in hc], [si[:, j, :] for j in hc])
                    dve.drain().then_inc(sc_used, 1)
                    half = sv[:].rearrange("p (h c) k -> p h c k", c=2)
                    pairs = pair[:].rearrange("p h (i j) -> p h i j", i=TOPK)
                    dve.tensor_tensor(pairs, half[:, :, 0].unsqueeze(3).broadcast_to([P, PH, TOPK, TOPK]),
                                      half[:, :, 1].unsqueeze(2).broadcast_to([P, PH, TOPK, TOPK]), ALU.add)
                    dve.tensor_copy(sif[:].rearrange("p h c k -> p (h c k)"), si[:].rearrange("p h k -> p (h k)"))
                    dve.drain()
                    top16([pair[:, h, :] for h in range(PH)], [rest[:, h * 256:(h + 1) * 256] for h in range(PH)],
                          [fv[:, h, :] for h in range(PH)], [fi[:, h, :] for h in range(PH)])
                    dve.drain()
                    dve.tensor_tensor(pick[:, 2], fv[:], fv[:, :, 0:1].broadcast_to([P, PH, TOPK]), ALU.subtract)
                    dve.tensor_scalar(half_u[:, 0], fi[:], 4, None, ALU.logical_shift_right)
                    dve.tensor_scalar(half_u[:, 1], fi[:], TOPK - 1, None, ALU.bitwise_and)
                    dve.drain().then_inc(exp_in, 1)
                    dve.tensor_copy(half_f[:].rearrange("p c h k -> p (c h k)"), half_u[:].rearrange("p c h k -> p (c h k)"))
                    dve.drain()
                    for c in range(2):
                        dve.tensor_tensor(pairs, half_f[:, c].unsqueeze(3).broadcast_to([P, PH, TOPK, TOPK]),
                                          iota16[:].unsqueeze(1).unsqueeze(1).broadcast_to([P, PH, TOPK, TOPK]), ALU.is_equal)
                        dve.drain()
                        dve.tensor_tensor(pairs, pairs, sif[:, :, c].unsqueeze(2).broadcast_to([P, PH, TOPK, TOPK]), ALU.mult)
                        dve.drain()
                        dve.tensor_reduce(pick[:, c], pairs, X, ALU.add)
                        dve.drain()
                    dve.wait_ge(exp_out, n + 1)
                    dve.tensor_reduce(gsum[:], pick[:, 2], X, ALU.add)
                    dve.drain()
                    dve.reciprocal(gsum[:], gsum[:])
                    dve.drain()
                    dve.tensor_tensor(pick[:, 2], pick[:, 2], gsum[:].unsqueeze(2).broadcast_to([P, PH, TOPK]), ALU.mult)
                    dve.drain().then_inc(picked, 1)
                    dve.wait_ge(pickT_full, n + 1)
                    choice = ps[:, 3, 0:2 * P].rearrange("p (c t) -> p c t", c=2)
                    if isinstance(n, int) and n == NB:
                        dve.tensor_copy(place_f[:], choice[:, :, 0:SAMPLE])
                        dve.tensor_copy(gate[:], ps[:, 3, 2 * P:2 * P + SAMPLE])
                        dve.drain()
                        dve.scalar_tensor_tensor(place_f[:, 0], place_f[:, 0], float(KEYS), place_f[:, 1], ALU.mult, ALU.add)
                        dve.drain()
                        dve.tensor_copy(place[:], place_f[:, 0])
                        dve.drain().then_inc(places_ready, 1)
                        return
                    dve.wait_ge(lows_ready, n * batches + 2)
                    dve.wait_ge(const_loaded, 64)
                    dve.tensor_copy(col[:], choice)
                    dve.tensor_scalar(gt[:], ps[:, 3, 2 * P:3 * P], SG, None, ALU.mult)
                    dve.drain()
                    dve.tensor_copy(gh[:], gt[:])
                    dve.drain()
                    dve.tensor_tensor(gl[:], gt[:], gh[:], ALU.subtract)
                    dve.drain()

                    def batch(b, half):
                        dve.wait_ge(lows_ready, n * batches + b + 1)
                        dve.wait_ge(g_full, (n * batches + b) * 2 + 2)
                        now = bass.ds(b * BT, BT)
                        dve.tensor_tensor(hot_r[:, half], iota[:], spread(col[:, 0, now]), ALU.is_equal)
                        dve.drain().then_inc(rows_ready, 1)
                        dve.tensor_tensor(hot_c[:, half], iota[:], spread(col[:, 1, now]), ALU.is_equal)
                        dve.tensor_tensor(hot_h[:, half], hot_r[:, half], spread(gh[:, now]), ALU.mult)
                        dve.drain().then_inc(hots_ready, 1)
                    over_batches(dve, n, batch)

                over_blocks(dve, body)


def experts_stage(nc, a):
    ROWS = 4
    TURNS = KEYS // ROWS
    HALF = TURNS // 2
    assert HALF * ROWS == SAMPLE
    W = 512
    NC = PROMPT // W
    YB = 3
    with ExitStack() as stack:
        s = Space(nc, stack, "experts")
        xh, xl = s.sb("xh", [P, KT, PROMPT], F16), s.sb("xl", [P, KT, PROMPT], F16)
        y = s.sb("y", [P, NB + 1, D])
        ut, uh, ul = s.sb("ut", [P, 2, D]), s.sb("uh", [P, 2, KT, P], F16), s.sb("ul", [P, 2, KT, P], F16)
        vt = s.sb("vt", [P, 2, D])
        vh, vl = s.sb("vh", [P, ROWS, D], F16), s.sb("vl", [P, ROWS, D], F16)
        g = s.sb("g", [P, 2, PROMPT])
        act_a, hf = s.sb("act_a", [P, NC, W]), s.sb("hf", [P, W])
        hh, hl = s.sb("hh", [P, ROWS, PROMPT], F16), s.sb("hl", [P, ROWS, PROMPT], F16)
        gain, shift = s.sb("gain", [P, D]), s.sb("shift", [P, D])
        stats, mv, rstd = s.sb("stats", [P, 2, 6]), s.sb("mv", [P, 2]), s.sb("rstd", [P, 1])
        power, scrap = s.sb("power", [P, 1]), s.sb("scrap", [P, 1])
        place, gate = s.sb("place", [P, SAMPLE], U32), s.sb("gate", [P, SAMPLE])
        now_place = s.sb("now_place", [P, 2], U32)
        fetched, xb, prod = s.sb("fetched", [P, 2, D]), s.sb("xb", [P, 2, D]), s.sb("prod", [P, D])
        dot, av, hs = s.sb("dot", [P, ROWS]), s.sb("av", [P, SAMPLE]), s.sb("hs", [P, SAMPLE])
        yst, ident = s.sb("yst", [P, KT, SAMPLE]), s.sb("ident", [P, P])
        ps = s.psum("ps", [P, 8, 512])
        x_loaded, y_loaded, place_loaded = s.sem("x_loaded"), s.sem("y_loaded"), s.sem("place_loaded")
        u_loaded, v_loaded, g_loaded = s.sems("u_loaded", 2), s.sems("v_loaded", 2), s.sems("g_loaded", 2)
        xb_loaded, gathered = s.sems("xb_loaded", 2), s.sems("gathered", 2)
        u_high, u_ready, v_high, v_ready = (s.sem(k) for k in ("u_high", "u_ready", "v_high", "v_ready"))
        a_full, a_read, h_temp, h_ready = (s.sem(k) for k in ("a_full", "a_read", "h_temp", "h_ready"))
        y_full, y_read, turn_done = s.sem("y_full"), s.sem("y_read"), s.sem("turn_done")
        fetched_used, av_ready, av_act, hs_ready = (s.sem(k) for k in ("fetched_used", "av_ready", "av_act", "hs_ready"))
        yst_full, yst_read, ys_full = s.sem("yst_full"), s.sem("yst_read"), s.sem("ys_full")
        y_ready, y_stored = s.sem("y_ready"), s.sem("y_stored")
        var_ready, rstd_ready = s.sem("var_ready"), s.sem("rstd_ready")

        def over_turns(eng, body, between=lambda: None):
            with eng.Fori(0, HALF) as i:
                body(i, True, False)
            between()
            with eng.Fori(HALF, TURNS - 1) as i:
                body(i, False, False)
            body(TURNS - 1, False, True)

        with nc.Block() as block:

            @block.sync
            def _(sp):
                def load_u(e, slot):
                    sp.dma_start(ut[:, slot], a.uT[bass.ds(e, 1)]).then_inc(u_loaded[slot], 16)

                def load_vg(e, slot):
                    sp.dma_start(g[:, slot], a.g[bass.ds(e, 1)]).then_inc(g_loaded[slot], 16)
                    sp.dma_start(vt[:, slot], a.v[bass.ds(e, 1)]).then_inc(v_loaded[slot], 16)

                load_u(0, 0)
                sp.dma_start(xh[:], a.xh[:, :, 0:PROMPT]).then_inc(x_loaded, 16)
                sp.dma_start(xl[:], a.xl[:, :, 0:PROMPT]).then_inc(x_loaded, 16)
                load_u(1, 1)
                load_vg(0, 0)
                load_vg(1, 1)
                for dst, src in ((place, a.place), (gate, a.gate)):
                    sp.dma_start(dst[:], src).then_inc(place_loaded, 16)
                for dst, src in ((y, a.base.rearrange("b p d -> p b d")), (gain, a.ln2_g), (shift, a.ln2_b), (ident, a.c_ident)):
                    sp.dma_start(dst[:], src).then_inc(y_loaded, 16)

                def body(i, from_u, last):
                    for m in range(ROWS):
                        e, slot = i * ROWS + m, m % 2
                        if from_u:
                            sp.wait_ge(fetched_used, e + 1)
                            sp.dma_start(xb[:, slot], a.x1_sample[bass.ds(e, 1), :].broadcast_to([P, D])).then_inc(xb_loaded[slot], 16)
                        if last and m >= ROWS - 2:
                            continue
                        sp.wait_ge(u_ready, e + 1)
                        load_u(e + 2, slot)
                        sp.wait_ge(v_ready, e + 1)
                        sp.wait_ge(h_temp, e * NC + 2 * NC)
                        load_vg(e + 2, slot)

                over_turns(sp, body)
                sp.wait_ge(y_ready, 1)
                sp.dma_start(a.y_sample, y[0:SAMPLE, NB, :]).then_inc(y_stored, 16)
                for b in range(NB):
                    sp.wait_ge(y_ready, b + 2)
                    sp.dma_start(a.y_prompt[b * P:(b + 1) * P, :], y[:, b, :]).then_inc(y_stored, 16)
                sp.wait_ge(y_stored, 16 * (NB + 1))

            @block.tensor
            def _(pe):
                pe.sem_inc(turn_done, 1)
                pe.wait_ge(x_loaded, 32)

                def body(i, from_u, last):
                    for m in range(ROWS):
                        e, slot = i * ROWS + m, m % 2
                        pe.wait_ge(u_ready, e + 1)
                        for c in range(NC):
                            bank = (m * NC + c) % 4
                            pe.wait_ge(a_read, e * NC + c + 1)
                            for k in range(KT):
                                for j, (w, x) in enumerate(((uh, xh), (uh, xl), (ul, xh))):
                                    mm = pe.matmul(ps[:, bank, :], w[:, slot, k, :], x[:, k, c * W:(c + 1) * W],
                                                   start=k == 0 and j == 0, stop=k == KT - 1 and j == 2)
                            mm.then_inc(a_full, 1)
                        if not from_u:
                            if m == 0:
                                pe.wait_ge(yst_read, (i - HALF) + 1)
                            pe.wait_ge(gathered[slot], (i * 2 + m // 2) * 16 + 16)
                            for d in range(KT):
                                mm = pe.matmul(ps[:, 7, m * KT + d:m * KT + d + 1], fetched[:, slot, d * P:(d + 1) * P],
                                               hs[:, bass.ds(e - SAMPLE, 1)], start=True, stop=True)
                            mm.then_inc(fetched_used, 1)
                    if not from_u:
                        pe.drain().then_inc(yst_full, 1)
                    if last:
                        pe.wait_ge(yst_read, HALF + 1)
                        pe.wait_ge(a_read, KEYS * NC + 4)
                        for d in range(KT):
                            mm = pe.transpose(ps[0:SAMPLE, d // 4, (d % 4) * P:(d % 4 + 1) * P], yst[:, d, :], ident[:])
                        mm.then_inc(ys_full, 1)
                    pe.wait_ge(v_ready, i * ROWS + ROWS)
                    for b in range(NB):
                        if b * P % W == 0:
                            pe.wait_ge(h_ready, i * (ROWS * NC) + (ROWS - 1) * NC + b * P // W + 1)
                        for d in range(2):
                            q = b * 2 + d
                            pe.wait_ge(y_read, i * (2 * NB) + q + 1)
                            for m in range(ROWS):
                                for j, (h, v) in enumerate(((hh, vh), (hh, vl), (hl, vh))):
                                    mm = pe.matmul(ps[:, 4 + q % YB, :], h[:, m, b * P:(b + 1) * P], v[:, m, d * 512:(d + 1) * 512],
                                                   start=m == 0 and j == 0, stop=m == ROWS - 1 and j == 2)
                            mm.then_inc(y_full, 1)
                    pe.drain().then_inc(turn_done, 1)

                def between():
                    pe.wait_ge(hs_ready, 1)
                    pe.wait_ge(y_loaded, 64)

                over_turns(pe, body, between)

            @block.scalar
            def _(act):
                act.sem_inc(a_read, 4)

                def high_u(e, slot, count):
                    act.wait_ge(u_loaded[slot], count)
                    act.activation(uh[:, slot].rearrange("p k t -> p (k t)"), ut[:, slot], ACT.Copy, scale=SU).then_inc(u_high, 1)

                high_u(0, 0, 16)
                high_u(1, 1, 16)

                def body(i, from_u, last):
                    for m in range(ROWS):
                        e, slot = i * ROWS + m, m % 2
                        if m == 0:
                            act.wait_ge(turn_done, i + 1)
                        act.wait_ge(v_loaded[slot], (i * 2 + m // 2) * 16 + 16)
                        act.activation(vh[:, m], vt[:, slot], ACT.Copy, scale=SV).then_inc(v_high, 1)
                        for c in range(NC):
                            act.wait_ge(h_temp, e * NC + c + 1)
                            act.wait_ge(a_full, e * NC + c + 1)
                            act.activation(act_a[:, c, :], ps[:, (m * NC + c) % 4, :],
                                           ACT.Gelu_apprx_tanh, scale=1.0 / SU).then_inc(a_read, 1)
                        if not (last and m >= ROWS - 2):
                            high_u(e + 2, slot, (i * 2 + m // 2) * 16 + 32)

                def between():
                    act.wait_ge(av_ready, 1)
                    act.activation(hs[:], av[:], ACT.Gelu_apprx_tanh).then_inc(av_act, 1)

                over_turns(act, body, between)

            @block.gpsimd
            def _(pool):
                pool.memset(power[:], -0.5)
                pool.wait_ge(place_loaded, 32)
                pool.drain()

                def body(i, from_u, last):
                    for m in range(ROWS):
                        t, slot = i * ROWS + m, m % 2
                        pool.wait_ge(fetched_used, t + 1)
                        pool.tensor_tensor(scrap[:], power[:], power[:], ALU.mult)
                        token = t if from_u else t - SAMPLE
                        pool.tensor_copy(now_place[:, slot:slot + 1], place[:, bass.ds(token, 1)])
                        pool.drain()
                        rows = a.u_rows if from_u else a.v.rearrange("r e d -> (r e) d")
                        pool.indirect_dma_start(fetched[:, slot], None, rows,
                                                bass.IndirectOffsetOnAxis(ap=now_place[:, slot:slot + 1], axis=0)).then_inc(gathered[slot], 16)

                over_turns(pool, body)
                inverse_deviation(pool, SAMPLE, mv, power, rstd, var_ready, rstd_ready, 1)
                for b in range(NB):
                    inverse_deviation(pool, P, mv, power, rstd, var_ready, rstd_ready, b + 2)

            @block.vector
            def _(dve):
                dve.sem_inc(h_temp, NC)
                dve.sem_inc(y_read, YB)
                dve.sem_inc(fetched_used, 2)
                dve.sem_inc(yst_read, 1)

                def low_u(e, slot):
                    dve.wait_ge(u_high, e + 1)
                    dve.scalar_tensor_tensor(ul[:, slot].rearrange("p k t -> p (k t)"), ut[:, slot], SU,
                                             uh[:, slot].rearrange("p k t -> p (k t)"), ALU.mult, ALU.subtract).then_inc(u_ready, 1)

                def normalised(rows, b, count):
                    row = y[0:rows, b, :]
                    dve.drain()
                    layer_norm_stats(dve, [row[:, 0:512], row[:, 512:1024]], rows, stats, mv, var_ready, rstd_ready, count)
                    dve.tensor_scalar(row, row, mv[:rows, 0:1], rstd[:rows, :], ALU.subtract, ALU.mult)
                    dve.drain()
                    dve.tensor_tensor(row, row, gain[:rows, :], ALU.mult)
                    dve.drain()
                    dve.tensor_tensor(row, row, shift[:rows, :], ALU.add)
                    dve.drain().then_inc(y_ready, 1)

                dve.memset(mv[:], 0.0)
                low_u(0, 0)
                low_u(1, 1)

                def body(i, from_u, last):
                    dve.wait_ge(turn_done, i + 1)
                    for m in range(ROWS):
                        e, slot = i * ROWS + m, m % 2
                        dve.wait_ge(v_high, e + 1)
                        dve.scalar_tensor_tensor(vl[:, m], vt[:, slot], SV, vh[:, m], ALU.mult, ALU.subtract).then_inc(v_ready, 1)
                        dve.wait_ge(g_loaded[slot], (i * 2 + m // 2) * 16 + 16)
                        for c in range(NC):
                            cols = slice(c * W, (c + 1) * W)
                            dve.wait_ge(a_read, e * NC + c + 5)
                            dve.scalar_tensor_tensor(hf[:], g[:, slot, cols], SH / SG, act_a[:, c, :], ALU.mult, ALU.mult)
                            dve.drain().then_inc(h_temp, 1)
                            dve.tensor_copy(hh[:, m, cols], hf[:])
                            dve.drain()
                            dve.tensor_tensor(hl[:, m, cols], hf[:], hh[:, m, cols], ALU.subtract)
                            dve.drain().then_inc(h_ready, 1)
                        if not (last and m >= ROWS - 2):
                            low_u(e + 2, slot)
                        if from_u:
                            dve.wait_ge(gathered[slot], (i * 2 + m // 2) * 16 + 16)
                            dve.wait_ge(xb_loaded[slot], (i * 2 + m // 2) * 16 + 16)
                            dve.tensor_tensor_reduce(prod[:], fetched[:, slot], xb[:, slot], 1.0, 0.0, ALU.mult, ALU.add, dot[:, m:m + 1])
                            dve.drain().then_inc(fetched_used, 1)
                    if from_u:
                        dve.tensor_copy(av[:, bass.ds(i * ROWS, ROWS)], dot[:])
                        dve.drain()
                    else:
                        dve.wait_ge(yst_full, (i - HALF) + 1)
                        dve.wait_ge(y_loaded, 64)
                        dve.tensor_copy(yst[:, :, bass.ds(i * ROWS - SAMPLE, ROWS)],
                                        ps[:, 7, 0:ROWS * KT].rearrange("p (m d) -> p d m", m=ROWS)).then_inc(yst_read, 1)
                    if last:
                        dve.wait_ge(ys_full, 1)
                        row = y[0:SAMPLE, NB, :].rearrange("p (c n) -> p c n", c=2)
                        dve.tensor_tensor(row, ps[0:SAMPLE, 0:2, :], row, ALU.add)
                        normalised(SAMPLE, NB, 1)
                    dve.wait_ge(y_loaded, 64)
                    dve.wait_ge(place_loaded, 32)
                    for b in range(NB):
                        for d in range(2):
                            q = b * 2 + d
                            dve.wait_ge(y_full, i * (2 * NB) + q + 1)
                            part = y[:, b, d * 512:(d + 1) * 512]
                            dve.scalar_tensor_tensor(part, ps[:, 4 + q % YB, :], 1.0 / (SH * SV), part, ALU.mult,
                                                     ALU.add).then_inc(y_read, 1)
                        if last:
                            normalised(P, b, b + 2)

                def between():
                    dve.drain().then_inc(av_ready, 1)
                    dve.wait_ge(av_act, 1)
                    dve.tensor_tensor(hs[:], hs[:], gate[:], ALU.mult).then_inc(hs_ready, 1)

                over_turns(dve, body, between)


def build(nc, a):
    bias_stage(nc, a)
    project_stage(nc, a)
    mix_prompt_stage(nc, a)
    mix_sample_stage(nc, a)
    merge_stage(nc, a)
    route_stage(nc, a)
    experts_stage(nc, a)


class Arrays:
    pass


def shape_constants():
    dist = 2 * P - 1 - np.arange(TOEP)
    inside = (dist >= 0) & (dist < P)
    n = np.maximum(dist, 0)
    exact = BUCKETS // 2
    large = exact + (np.log(np.maximum(n, 1) / exact) / math.log(MAX_DISTANCE / exact) * (BUCKETS - exact)).astype(np.int32)
    bucket = np.where(n < exact, n, np.minimum(large, BUCKETS - 1))
    onehot = ((np.arange(BUCKETS)[:, None] == bucket[None]) & inside[None]).astype(np.float32)
    outside = np.broadcast_to(np.where(inside, 0.0, NEG).astype(np.float32), (HEADS, TOEP))
    return {
        "c_bucket": onehot,
        "c_outside": np.ascontiguousarray(outside),
        "c_ident": np.eye(P, dtype=np.float32),
        "c_tril": np.triu(np.ones((P, P), np.float32)),
        "c_iota": np.broadcast_to(np.arange(KEYS, dtype=np.float16)[None, :, None], (P, KEYS, BT)).copy(),
        "c_iota16": np.broadcast_to(np.arange(TOPK, dtype=np.float32), (P, TOPK)).copy(),
    }


def laid_out(x_prompt, x_sample, cache_k_win, cache_v_win, p_prompt, p_sample, rel_bias_table, w_in, attn_sinks,
             w_att_out, c_ln_g, c_ln_b, c_ws, c_bs, w_chunk_out, w_o, ln1_g, ln1_b, peer_wq, peer_subkeys, peer_u,
             peer_v, w_ple_gate, w_ple_proj, ln2_g, ln2_b):
    def blocks(prompt, sample):
        w = prompt.shape[-1]
        rows = np.zeros(((NB + 1) * P, w), np.float32)
        rows[:PROMPT] = prompt.reshape(PROMPT, w)
        rows[PROMPT:T] = sample.reshape(SAMPLE, w)
        return rows.reshape(NB + 1, P, w)

    def by_feature(b):
        return b.reshape(NB + 1, P, -1, P).transpose(0, 3, 2, 1)

    def k_tiles(w):
        return w.reshape(-1, P, w.shape[-1]).transpose(1, 0, 2)

    def rows(v):
        return np.broadcast_to(v.reshape(1, -1), (P, v.size))

    heads = [g * REP + r for r in range(REP) for g in range(GROUPS)]
    q_cols = np.concatenate([np.arange(h * HD, (h + 1) * HD) for h in heads])
    w = w_in[0]
    x = blocks(x_prompt, x_sample)
    ws_sample = np.zeros((SAMPLE, CG, SAMPLE), np.float32)
    for b in range(SEQS):
        seq = slice(b * NEW, (b + 1) * NEW)
        ws_sample[seq, :, seq] = c_ws[0][:, :NEW, :NEW].transpose(2, 0, 1)
    sinks = attn_sinks[0].reshape(1, GROUPS, REP, 1, 1).transpose(0, 2, 3, 4, 1)
    sink_sample = np.broadcast_to(sinks, (4, REP, NEW, SEQS // 4, GROUPS)).reshape(P, SEQS // 4, GROUPS)
    return {
        "ws_sample": ws_sample,
        "sink_sample": sink_sample,
        "bs_sample": np.tile(c_bs[0][:, :NEW].T, (SEQS, 1)),
        "x_blocks": x,
        "xt_blocks": by_feature(x),
        "pt_blocks": by_feature(blocks(p_prompt[0], p_sample[0])),
        "rel_bias_table": rel_bias_table,
        "w_in": k_tiles(np.concatenate([w[:, q_cols], w[:, QW:]], axis=1)),
        "sink_rows": rows(attn_sinks),
        "wa": k_tiles(w_att_out[0][q_cols]),
        "wc": k_tiles(w_chunk_out[0]),
        "wo": k_tiles(w_o[0]),
        "wpg": k_tiles(w_ple_gate[0]),
        "wpp": k_tiles(w_ple_proj[0]),
        "wq": k_tiles(peer_wq[0]),
        "subT": peer_subkeys[0].reshape(2 * PH, KEYS, P).transpose(2, 0, 1),
        "uT": peer_u[0].reshape(KEYS, KEYS, KT, P).transpose(0, 3, 2, 1),
        "u_rows": peer_u[0],
        "v": peer_v[0].reshape(KEYS, KEYS, D),
        "c_ln_g": rows(c_ln_g), "c_ln_b": rows(c_ln_b),
        "ln1_g": rows(ln1_g), "ln1_b": rows(ln1_b), "ln2_g": rows(ln2_g), "ln2_b": rows(ln2_b),
        "wsT": c_ws[0].transpose(2, 0, 1),
        "bsT": c_bs[0].T,
        "cache_kT": cache_k_win[0].transpose(2, 3, 0, 1).reshape(KVW, SEQS, P),
        "cache_v": cache_v_win[0].reshape(SEQS, P, KVW).transpose(1, 0, 2),
        "cache_k_rows": cache_k_win[0].reshape(SEQS, P, KVW),
        "cache_v_rows": cache_v_win[0].reshape(SEQS, P, KVW),
    }


OUTPUTS = {
    "y_prompt": (PROMPT, D), "y_sample": (SAMPLE, D), "k_prompt": (P, KVW), "v_prompt": (P, KVW),
    "k_sample": (SEQS, P, KVW), "v_sample": (SEQS, P, KVW), "chunk_v": (SAMPLE, CW),
}
SCRATCH = {
    "rev": ((HEADS, P, TOEP), F32),
    "z": ((NB + 2, P, ZW), F32),
    "yT": ((NB + 1, P, 8, P), F32),
    "x1T": ((NB + 1, P, KT, P), F32),
    "xh": ((P, KT, (NB + 1) * P), F16), "xl": ((P, KT, (NB + 1) * P), F16),
    "base": ((NB + 1, P, D), F32), "x1_sample": ((SAMPLE, D), F32),
    "g": ((KEYS, KEYS, PROMPT), F32),
    "place": ((P, SAMPLE), U32), "gate": ((P, SAMPLE), F32),
}
SHAPES = {
    "y_prompt": (1, PROMPT, D), "y_sample": (SEQS, NEW, D),
    "k_prompt": (1, 1, P, GROUPS, HD), "v_prompt": (1, 1, P, GROUPS, HD),
    "k_sample": (1, SEQS, P, GROUPS, HD), "v_sample": (1, SEQS, P, GROUPS, HD),
    "chunk_v": (1, SEQS, NEW, CW),
}


def kernel(**inputs):
    import concourse.bacc as bacc
    from concourse.bass_utils import run_bass_kernel_spmd

    nc = bacc.Bacc("TRN2", target_bir_lowering=False, num_devices=1)
    arrays = {**shape_constants(), **laid_out(**{k: np.asarray(v) for k, v in inputs.items()})}
    arrays = {f"in_{k}": np.ascontiguousarray(v) for k, v in arrays.items()}
    a = Arrays()
    for k, v in arrays.items():
        a.__dict__[k[3:]] = nc.dram_tensor(k, v.shape, mybir.dt.from_np(v.dtype), kind="ExternalInput").ap()
    for k, shape in OUTPUTS.items():
        a.__dict__[k] = nc.dram_tensor(f"out_{k}", shape, F32, kind="ExternalOutput").ap()
    for k, (shape, dt) in SCRATCH.items():
        a.__dict__[k] = nc.dram_tensor(f"scratch_{k}", shape, dt, kind="Internal").ap()
    build(nc, a)
    r = run_bass_kernel_spmd(nc, [arrays], core_ids=[0])
    return tuple(r.results[0][f"out_{k}"].reshape(SHAPES[k]) for k in OUTPUTS)
```

```python
import math
from contextlib import ExitStack

import numpy as np

import concourse.bass as bass
from concourse import mybir

F32 = mybir.dt.float32
F16 = mybir.dt.float16
U32 = mybir.dt.uint32
ALU = mybir.AluOpType
ACT = mybir.ActivationFunctionType
X = mybir.AxisListType.X

P = 128
D = 1024
KT = D // P
PROMPT, SAMPLE = 1024, 64
T = PROMPT + SAMPLE
NB = PROMPT // P
SEQS, NEW = 8, 8
HEADS, GROUPS, REP, HD = 8, 2, 4, 64
QW, KVW, CW = 512, 128, 512
CG = 4
IN_W = QW + 2 * KVW + 2 * CW + 2 * D
PLE = 256
PH, HALVES, KEYS, TOPK = 8, 2, 128, 16
HK = PH * TOPK
BT, QT = 8, 4
NEG = -1e30
LOWEST = -3.0e38
ALPHA = 2.0 ** 0.25
EPS = 1e-5
BUCKETS, MAX_DISTANCE = 32, 128
TOEP = 384
ZK, ZKV, ZU, ZV, ZG, ZW = 512, 640, 896, 1408, 1920, 3968

SW, SU, SV, SH, SG = 64.0, 64.0, 16.0, 64.0, 32768.0


def over_blocks(eng, body):
    with eng.Fori(0, NB // 2) as i:
        body(i * 2, 0)
        body(i * 2 + 1, 1)
    body(NB, 0)


def rows_of(n):
    return SAMPLE if isinstance(n, int) and n == NB else P


class Space:

    def __init__(self, nc, stack, stage):
        self.nc, self.stack, self.stage = nc, stack, stage
        self.taken = []
        stack.callback(self.clear)

    def sb(self, name, shape, dt=F32):
        return self.stack.enter_context(self.nc.sbuf_tensor(f"{self.stage}_{name}", shape, dt))

    def psum(self, name, shape, dt=F32):
        return self.stack.enter_context(self.nc.psum_tensor(f"{self.stage}_{name}", shape, dt))

    def sem(self, name):
        self.taken.append(self.nc.alloc_semaphore(f"{self.stage}_{name}"))
        return self.taken[-1]

    def sems(self, name, n):
        return [self.sem(f"{name}{i}") for i in range(n)]

    def clear(self):
        self.nc.all_engine_barrier()
        self.nc.clear_and_free_semaphores(self.taken)
        self.nc.all_engine_barrier()


def layer_norm_stats(dve, src, rows, stats, mv, var_ready, rstd_ready, count, eps=EPS):
    for c, part in enumerate(src):
        dve.bn_stats(stats[:rows, c, :], part)
    dve.drain()
    dve.bn_aggr(mv[:rows, :], stats[:rows, 0:len(src), :])
    dve.drain()
    dve.tensor_scalar(mv[:rows, 1:2], mv[:rows, 1:2], eps, None, ALU.add).then_inc(var_ready, 1)
    dve.wait_ge(rstd_ready, count)


def inverse_deviation(pool, rows, mv, power, rstd, var_ready, rstd_ready, count):
    pool.wait_ge(var_ready, count)
    pool.tensor_tensor(rstd[:rows, :], mv[:rows, 1:2], power[:rows, :], ALU.pow).then_inc(rstd_ready, 1)


def project_stage(nc, a):
    PIECE = 256
    PIECES = IN_W // PIECE
    with ExitStack() as stack:
        s = Space(nc, stack, "project")
        table, onehot = s.sb("table", [BUCKETS, HEADS]), s.sb("onehot", [BUCKETS, TOEP])
        outside, rev = s.sb("outside", [HEADS, TOEP]), s.sb("rev", [HEADS, TOEP])
        piece = s.sb("piece", [P, 2, KT, PIECE])
        wh, wl = s.sb("wh", [P, KT, IN_W], F16), s.sb("wl", [P, KT, IN_W], F16)
        xt = s.sb("xt", [P, 2, KT, P])
        xh, xl = s.sb("xh", [P, 2, KT, P], F16), s.sb("xl", [P, 2, KT, P], F16)
        z = s.sb("z", [P, 2, ZW])
        gain = s.sb("gain", [P, CW])
        shift = s.sb("shift", [P, CW])
        stats, mv, rstd = s.sb("stats", [P, 1, 6]), s.sb("mv", [P, 2]), s.sb("rstd", [P, 1])
        power = s.sb("power", [P, 1])
        ps = s.psum("ps", [P, 8, 512])
        w_cols = [(0, 512), (512, 768), (768, 1280), (1280, 1792)] + [(1792 + 512 * j, 2304 + 512 * j) for j in range(4)]
        bias_loaded, bias_full, bias_made, bias_stored = (s.sem(k) for k in ("bias_loaded", "bias_full", "bias_made", "bias_stored"))
        zeroed = s.sem("zeroed")
        w_loaded = s.sems("w_loaded", 2)
        w_high, w_ready = s.sem("w_high"), s.sem("w_ready")
        x_high, x_ready = s.sem("x_high"), s.sem("x_ready")
        const_loaded = s.sem("const_loaded")
        x_loaded = s.sems("x_loaded", 2)
        bank_full = s.sems("bank_full", 8)
        bank_read = s.sems("bank_read", 8)
        z_act, z_dve = s.sem("z_act"), s.sem("z_dve")
        z_stored = s.sems("z_stored", 2)
        var_ready, rstd_ready = s.sem("var_ready"), s.sem("rstd_ready")
        with nc.Block() as block:

            @block.sync
            def _(sp):
                sp.dma_start(xt[:, 0], a.xt_blocks[0]).then_inc(x_loaded[0], 16)
                for j in range(PIECES):
                    if j > 1:
                        sp.wait_ge(w_ready, j - 1)
                    sp.dma_start(piece[:, j % 2], a.w_in[:, :, j * PIECE:(j + 1) * PIECE]).then_inc(w_loaded[j % 2], 16)
                    if j == 1:
                        for dst, src in ((table, a.rel_bias_table), (onehot, a.c_bucket), (outside, a.c_outside)):
                            sp.dma_start(dst[:], src).then_inc(bias_loaded, 16)
                sp.dma_start(gain[:], a.c_ln_g).then_inc(const_loaded, 16)
                sp.dma_start(shift[:], a.c_ln_b).then_inc(const_loaded, 16)

                sp.wait_ge(bias_made, 1)
                sp.dma_start(a.rev, rev[:].unsqueeze(1).broadcast_to([HEADS, P, TOEP])).then_inc(bias_stored, 16)
                sp.wait_ge(zeroed, 1)
                sp.dma_start(a.z[0], z[:, 0]).then_inc(z_stored[0], 16)

                def load(n, slot):
                    sp.dma_start(xt[:, slot], a.xt_blocks[bass.ds(n, 1)]).then_inc(x_loaded[slot], 16)

                def store(n, slot):
                    sp.wait_ge(z_act, n + 1)
                    sp.wait_ge(z_dve, n + 1)
                    sp.dma_start(a.z[bass.ds(n + 1, 1)], z[:, slot]).then_inc(z_stored[slot], 16)

                with sp.Fori(0, NB // 2) as i:
                    for slot in range(2):
                        n = i * 2 + slot
                        sp.wait_ge(bank_full[7], n + 1)
                        load(n + 1, 1 - slot)
                        store(n, slot)
                store(NB, 0)
                sp.wait_ge(z_stored[0], 16 * (NB // 2 + 2))
                sp.wait_ge(z_stored[1], 16 * (NB // 2 + 1))
                sp.wait_ge(bias_stored, 16)

            @block.tensor
            def _(pe):
                pe.sem_inc(bank_full[7], 1)
                pe.wait_ge(bias_loaded, 48)
                pe.matmul(ps[0:HEADS, 7, 0:TOEP], table[:], onehot[:], start=True, stop=True).then_inc(bias_full, 1)

                def body(n, slot):
                    r = rows_of(n)
                    pe.wait_ge(x_ready, n + 1)
                    for bank in range(8):
                        pe.wait_ge(bank_read[bank], n + 1)
                        pe.wait_ge(w_ready, w_cols[bank][1] // PIECE)
                        q_tiles = [(j * P, j * P) for j in range(4)]
                        for o, c in (q_tiles, [(0, QW)])[bank] if bank < 2 else ():
                            for k in range(KT):
                                for j, (w, x) in enumerate(((wh, xh), (wh, xl), (wl, xh))):
                                    mm = pe.matmul(ps[:, bank, o:o + r], w[:, k, c:c + P], x[:, slot, k, :r],
                                                   start=k == 0 and j == 0, stop=k == KT - 1 and j == 2)
                        c0, c1 = w_cols[bank]
                        o = 0 if bank > 1 else P
                        if bank:
                            for k in range(KT):
                                for j, (x, w) in enumerate(((xh, wh), (xh, wl), (xl, wh))):
                                    mm = pe.matmul(ps[:r, bank, o:o + c1 - c0], x[:, slot, k, :r], w[:, k, c0:c1],
                                                   start=k == 0 and j == 0, stop=k == KT - 1 and j == 2)
                        mm.then_inc(bank_full[bank], 1)

                over_blocks(pe, body)

            @block.scalar
            def _(act):
                for bank in (0, 2, 4, 5, 6):
                    act.sem_inc(bank_read[bank], 1)

                def high_x(n, slot):
                    act.wait_ge(x_loaded[slot], (n - slot) * 8 + 16)
                    act.activation(xh[:, slot], xt[:, slot], ACT.Copy).then_inc(x_high, 1)

                high_x(0, 0)
                for j in range(PIECES):
                    act.wait_ge(w_loaded[j % 2], 16 * (j // 2 + 1))
                    act.activation(wh[:, :, j * PIECE:(j + 1) * PIECE], piece[:, j % 2], ACT.Copy, scale=SW).then_inc(w_high, 1)

                def body(n, slot):
                    r = rows_of(n)
                    if not (isinstance(n, int) and n == NB):
                        high_x(n + 1, 1 - slot)
                    act.wait_ge(z_stored[slot], (n - slot) * 8 + 16)
                    act.wait_ge(bank_full[0], n + 1)
                    act.activation(z[:, slot, 0:QW].rearrange("p (j t) -> p j t", j=4)[:, :, :r],
                                   ps[:, 0, :].rearrange("p (j t) -> p j t", j=4)[:, :, :r],
                                   ACT.Copy, scale=1.0 / SW).then_inc(bank_read[0], 1)
                    act.wait_ge(bank_full[2], n + 1)
                    act.activation(z[:r, slot, ZU:ZV], ps[:r, 2, :], ACT.Copy, scale=1.0 / SW).then_inc(bank_read[2], 1)
                    for j in range(4):
                        if j == 3:
                            act.wait_ge(bank_full[7], n + 2)
                        else:
                            act.wait_ge(bank_full[4 + j], n + 1)
                        act.activation(z[:r, slot, ZG + 512 * j:ZG + 512 * j + 512], ps[:r, 4 + j, :],
                                       ACT.Tanh, scale=0.5 / SW).then_inc(bank_read[4 + j], 1)
                    act.drain().then_inc(z_act, 1)

                over_blocks(act, body)

            @block.gpsimd
            def _(pool):
                pool.memset(power[:], -0.5)
                pool.memset(z[:], 0.0)
                pool.drain().then_inc(zeroed, 1)
                pool.sem_inc(z_stored[1], 16)
                over_blocks(pool, lambda n, slot: inverse_deviation(pool, rows_of(n), mv, power, rstd, var_ready, rstd_ready, n + 1))

            @block.vector
            def _(dve):
                for bank in (1, 3):
                    dve.sem_inc(bank_read[bank], 1)

                def low_x(n, slot):
                    dve.wait_ge(x_high, n + 1)
                    dve.tensor_tensor(xl[:, slot], xt[:, slot], xh[:, slot], ALU.subtract).then_inc(x_ready, 1)

                low_x(0, 0)
                dve.wait_ge(bias_loaded, 48)
                dve.wait_ge(bias_full, 1)
                dve.tensor_tensor(rev[:], ps[0:HEADS, 7, 0:TOEP], outside[:], ALU.add).then_inc(bias_made, 1)
                dve.drain().then_inc(bank_read[7], 1)
                for j in range(PIECES):
                    cols = slice(j * PIECE, (j + 1) * PIECE)
                    dve.wait_ge(w_high, j + 1)
                    dve.scalar_tensor_tensor(wl[:, :, cols], piece[:, j % 2], SW, wh[:, :, cols], ALU.mult,
                                             ALU.subtract).then_inc(w_ready, 1)
                dve.wait_ge(const_loaded, 32)

                def body(n, slot):
                    r = rows_of(n)
                    if not (isinstance(n, int) and n == NB):
                        low_x(n + 1, 1 - slot)
                    dve.wait_ge(z_stored[slot], (n - slot) * 8 + 16)
                    dve.wait_ge(bank_full[1], n + 1)
                    dve.tensor_scalar(z[:, slot, ZK:ZK + r], ps[:, 1, 0:r], 1.0 / SW, None, ALU.mult)
                    dve.tensor_scalar(z[:r, slot, ZKV:ZU], ps[:r, 1, P:P + 2 * KVW], 1.0 / SW, None, ALU.mult).then_inc(bank_read[1], 1)
                    dve.wait_ge(bank_full[3], n + 1)
                    layer_norm_stats(dve, [ps[:r, 3, :]], r, stats, mv, var_ready, rstd_ready, n + 1, EPS * SW * SW)
                    out = z[:r, slot, ZV:ZG]
                    dve.tensor_scalar(out, ps[:r, 3, :], mv[:r, 0:1], rstd[:r, :], ALU.subtract,
                                      ALU.mult).then_inc(bank_read[3], 1)
                    dve.drain()
                    dve.tensor_tensor(out, out, gain[:r, :], ALU.mult)
                    dve.drain()
                    dve.tensor_tensor(out, out, shift[:r, :], ALU.add)
                    dve.drain().then_inc(z_dve, 1)

                over_blocks(dve, body)


def mix_prompt_stage(nc, a):
    RING = 4
    with ExitStack() as stack:
        s = Space(nc, stack, "mix")
        za = s.sb("za", [P, RING, ZG])
        bias = s.sb("bias", [P, HEADS, 2 * P])
        sink = s.sb("sink", [P, HEADS])
        ident = s.sb("ident", [P, P])
        ws = s.sb("ws", [P, CG, P])
        tril = s.sb("tril", [P, P])
        bs = s.sb("bs", [P, CG])
        sc = s.sb("sc", [P, 2, HEADS, 2 * P])
        m, negm, total, esink, dsink = (s.sb(x, [P, HEADS]) for x in ("m", "negm", "total", "esink", "dsink"))
        prT = s.sb("prT", [P, 2 * HEADS, P])
        yc = s.sb("yc", [P, CW])
        yt = s.sb("yt", [P, 2, 8, P])
        ps = s.psum("ps", [P, 8, 512])
        const_loaded, ws_ready = s.sem("const_loaded"), s.sem("ws_ready")
        loaded = s.sems("loaded", RING)
        left_clear, left_loaded = s.sem("left_clear"), s.sem("left_loaded")
        scores_full, biased, maxed, exped, normed = (s.sem(x) for x in ("scores_full", "biased", "maxed", "exped", "normed"))
        gm_full, yc_ready, ycT_full, ycT_read = (s.sem(x) for x in ("gm_full", "yc_ready", "ycT_full", "ycT_read"))
        prT_full, prT_read = s.sems("prT_full", 4), s.sems("prT_read", 4)
        ya_full, ya_read = s.sem("ya_full"), s.sem("ya_read")
        y_stored = s.sems("y_stored", 2)

        def over_ring(eng, body):
            with eng.Fori(0, NB // RING) as i:
                for r in range(RING):
                    body(i * RING + r, r)

        def z_ready(eng, n, ring):
            eng.wait_ge(loaded[ring], (n - ring) * (16 // RING) + (32 if ring == RING - 1 else 16))

        def four(bank):
            return ps[:, bank, :].rearrange("p (j t) -> p j t", j=4)

        with nc.Block() as block:

            def toeplitz(k0):
                return bass.AP(a.rev.tensor, k0 + P - 1, [[TOEP - 1, P], [P * TOEP, HEADS], [1, P]])

            @block.sync
            def _(sp):
                def load(n):
                    sp.dma_start(za[:, n % RING], a.z[n + 1, :, 0:ZG]).then_inc(loaded[n % RING], 16)

                load(0)
                load(-1)
                for dst, src in ((ident, a.c_ident), (ws, a.wsT), (tril, a.c_tril), (bs, a.bsT), (sink, a.sink_rows),
                                 (bias[:, :, P:2 * P], toeplitz(P))):
                    sp.dma_start(dst[:], src).then_inc(const_loaded, 16)
                load(1)
                load(2)
                sp.wait_ge(biased, 1)
                sp.dma_start(bias[:, :, 0:P], toeplitz(0)).then_inc(left_loaded, 16)
                for n in range(NB):
                    sp.wait_ge(ya_full, n + 1)
                    if n + 3 <= NB:
                        load(n + 3)
                    sp.wait_ge(ya_read, n + 2)
                    sp.wait_ge(ycT_read, n + 1)
                    sp.dma_start(a.yT[n], yt[:, n % 2]).then_inc(y_stored[n % 2], 16)
                sp.dma_start(a.k_prompt, a.z[NB, :, ZKV:ZKV + KVW]).then_inc(const_loaded, 16)
                sp.dma_start(a.v_prompt, a.z[NB, :, ZKV + KVW:ZU]).then_inc(const_loaded, 16)
                sp.wait_ge(const_loaded, 8 * 16)
                for slot in range(2):
                    sp.wait_ge(y_stored[slot], 16 * (NB // 2 + 1))

            @block.tensor
            def _(pe):
                def scores(n, ring):
                    z_ready(pe, n, ring)
                    for h in range(HEADS):
                        g, r = divmod(h, REP)
                        lo = g * HD
                        for half, keys in enumerate(((ring - 1) % RING, ring)):
                            mm = pe.matmul(ps[:, h // 2, (h % 2) * 256 + half * P:(h % 2) * 256 + half * P + P],
                                           za[lo:lo + HD, ring, r * P:(r + 1) * P], za[lo:lo + HD, keys, ZK:ZK + P],
                                           start=True, stop=True)
                    mm.then_inc(scores_full, 1)

                def gmlp(n, ring):
                    for g in range(CG):
                        mm = pe.matmul(ps[:, 5, g * P:(g + 1) * P], ws[:, g, :],
                                       za[:, ring, ZV + g * P:ZV + (g + 1) * P], start=True, stop=True)
                    mm.then_inc(gm_full, 1)
                    pe.wait_ge(yc_ready, n + 1)
                    for g in range(CG):
                        mm = pe.transpose(ps[:, 6, g * P:(g + 1) * P], yc[:, g * P:(g + 1) * P], ident[:])
                    mm.then_inc(ycT_full, 1)

                pe.wait_ge(const_loaded, 6 * 16)
                pe.wait_ge(loaded[RING - 1], 16)
                scores(0, 0)
                pe.wait_ge(ws_ready, 1)
                gmlp(0, 0)

                def body(n, ring):
                    pe.wait_ge(biased, n + 1)
                    scores(n + 1, (ring + 1) % RING)
                    pe.wait_ge(ya_read, n + 1)
                    pe.wait_ge(normed, n + 1)
                    for q in range(4):
                        if q == 2:
                            pe.wait_ge(ycT_read, n + 1)
                        for j in range(4):
                            h, half = 2 * q + j // 2, j % 2
                            mm = pe.transpose(ps[:, 4 + q, j * P:(j + 1) * P], sc[:, ring % 2, h, half * P:(half + 1) * P], ident[:])
                        mm.then_inc(prT_full[q], 1)
                    for h in range(HEADS):
                        g, r = divmod(h, REP)
                        lo = g * HD
                        v = ZKV + KVW + lo
                        if h % 2 == 0:
                            pe.wait_ge(prT_read[h // 2], n + 1)
                        pe.matmul(ps[lo:lo + HD, 4, r * P:(r + 1) * P], za[:, (ring - 1) % RING, v:v + HD],
                                  prT[:, 2 * h, :], start=True, stop=False)
                        mm = pe.matmul(ps[lo:lo + HD, 4, r * P:(r + 1) * P], za[:, ring, v:v + HD],
                                       prT[:, 2 * h + 1, :], start=False, stop=True)
                    mm.then_inc(ya_full, 1)
                    gmlp(n + 1, (ring + 1) % RING)

                over_ring(pe, body)

            @block.scalar
            def _(act):
                act.sem_inc(ya_read, 1)
                act.sem_inc(y_stored[0], 16)
                act.sem_inc(y_stored[1], 16)

                def exponentials(n, slot):
                    act.wait_ge(maxed, n + 1)
                    for h in range(HEADS):
                        act.activation(sc[:, slot, h, :], sc[:, slot, h, :], ACT.Exp, bias=negm[:, h:h + 1],
                                       accum_out=total[:, h:h + 1])
                    act.activation(esink[:], dsink[:], ACT.Exp)
                    act.drain().then_inc(exped, 1)

                exponentials(0, 0)

                def body(n, ring):
                    slot = ring % 2
                    for q in (0, 1):
                        act.wait_ge(prT_full[q], n + 1)
                        act.activation(prT[:, 4 * q:4 * q + 4, :], four(4 + q), ACT.Copy).then_inc(prT_read[q], 1)
                    exponentials(n + 1, 1 - slot)
                    act.wait_ge(y_stored[slot], (n - slot) * 8 + 16)
                    act.wait_ge(ya_full, n + 1)
                    act.activation(yt[:, slot, 0:4, :], four(4), ACT.Copy).then_inc(ya_read, 1)

                over_ring(act, body)

            @block.gpsimd
            def _(pool):
                pool.memset(bias[:, :, 0:P], NEG).then_inc(left_clear, 1)

            @block.vector
            def _(dve):
                dve.wait_ge(const_loaded, 6 * 16)
                for g in range(CG):
                    last = dve.tensor_tensor(ws[:, g, :], ws[:, g, :], tril[:], ALU.mult)
                last.then_inc(ws_ready, 1)

                def maxima(n, slot):
                    dve.wait_ge(scores_full, n + 1)
                    for q in range(4):
                        dve.scalar_tensor_tensor(sc[:, slot, 2 * q:2 * q + 2, :], ps[:, q, :].rearrange("p (h k) -> p h k", h=2),
                                                 HD ** -0.5, bias[:, 2 * q:2 * q + 2, :], ALU.mult, ALU.add)
                    dve.drain().then_inc(biased, 1)
                    dve.tensor_reduce(m[:], sc[:, slot], X, ALU.max)
                    dve.drain()
                    dve.tensor_tensor(m[:], m[:], sink[:], ALU.max)
                    dve.drain()
                    dve.tensor_scalar(negm[:], m[:], -1.0, None, ALU.mult)
                    dve.tensor_tensor(dsink[:], sink[:], m[:], ALU.subtract)
                    dve.drain().then_inc(maxed, 1)

                def gmlp_and_softmax(n, ring, slot):
                    dve.wait_ge(gm_full, n + 1)
                    for g in range(CG):
                        cols = slice(g * P, (g + 1) * P)
                        dve.scalar_tensor_tensor(yc[:, cols], ps[:, 5, cols], bs[:, g:g + 1],
                                                 za[:, ring, ZU + g * P:ZU + (g + 1) * P], ALU.add, ALU.mult)
                    dve.drain().then_inc(yc_ready, 1)
                    dve.wait_ge(ycT_full, n + 1)
                    dve.wait_ge(y_stored[slot], (n - slot) * 8 + 16)
                    dve.tensor_copy(yt[:, slot, 4:8, :], four(6)).then_inc(ycT_read, 1)
                    dve.wait_ge(exped, n + 1)
                    dve.tensor_tensor(total[:], total[:], esink[:], ALU.add)
                    dve.drain()
                    dve.reciprocal(total[:], total[:])
                    dve.drain()
                    dve.tensor_tensor(sc[:, slot], sc[:, slot], total[:].unsqueeze(2).broadcast_to([P, HEADS, 2 * P]), ALU.mult)
                    dve.drain().then_inc(normed, 1)

                dve.wait_ge(left_clear, 1)
                maxima(0, 0)
                gmlp_and_softmax(0, 0, 0)
                dve.wait_ge(left_loaded, 16)

                def body(n, ring):
                    slot = ring % 2
                    maxima(n + 1, 1 - slot)
                    for q in (2, 3):
                        dve.wait_ge(prT_full[q], n + 1)
                        dve.tensor_copy(prT[:, 4 * q:4 * q + 4, :], four(4 + q)).then_inc(prT_read[q], 1)
                    gmlp_and_softmax(n + 1, (ring + 1) % RING, 1 - slot)

                over_ring(dve, body)


class MergeWeights:
    WA, WC, WO, WPP, WPG, TILES = 0, 4, 8, 16, 18, 26
    PIECE, EARLY = 2, 6
    PIECES = TILES // PIECE

    def __init__(self, nc, stack, a):
        s = Space(nc, stack, "merge_w")
        self.source = a.w_merge
        self.piece = s.sb("piece", [P, 2, self.PIECE, D])
        self.high, self.low = s.sb("high", [P, self.TILES, D], F16), s.sb("low", [P, self.TILES, D], F16)
        self.loaded = s.sems("loaded", 2)
        self.high_ready, self.ready = s.sem("high_ready"), s.sem("ready")

    def part(self, j):
        return slice(j * self.PIECE, (j + 1) * self.PIECE)

    def load(self, sp, j):
        if j > 1:
            sp.wait_ge(self.ready, j - 1)
        sp.dma_start(self.piece[:, j % 2], self.source[:, self.part(j), :]).then_inc(self.loaded[j % 2], 16)

    def split_high(self, act, j):
        act.wait_ge(self.loaded[j % 2], 16 * (j // 2 + 1))
        act.activation(self.high[:, self.part(j), :], self.piece[:, j % 2], ACT.Copy, scale=SW).then_inc(self.high_ready, 1)

    def split_low(self, dve, j):
        dve.wait_ge(self.high_ready, j + 1)
        dve.scalar_tensor_tensor(self.low[:, self.part(j), :], self.piece[:, j % 2], SW, self.high[:, self.part(j), :],
                                 ALU.mult, ALU.subtract).then_inc(self.ready, 1)


def mix_sample_stage(nc, a, weights):
    S4 = SEQS // 4
    KA = P + NEW
    with ExitStack() as stack:
        s = Space(nc, stack, "smix")
        za = s.sb("za", [P, ZG])
        qs = s.sb("qs", [P, SEQS, REP, NEW])
        ckT = s.sb("ckT", [P, SEQS, P])
        cv = s.sb("cv", [P, SEQS, P])
        vnew = s.sb("vnew", [NEW, SEQS, P])
        bias = s.sb("bias", [P, GROUPS, KA])
        sink = s.sb("sink", [P, S4, GROUPS])
        ident = s.sb("ident", [P, P])
        ws = s.sb("ws", [SAMPLE, CG, SAMPLE])
        tril = s.sb("tril", [P, P])
        bs = s.sb("bs", [SAMPLE, CG])
        sc = s.sb("sc", [P, S4, GROUPS, KA])
        m, negm, total, esink, dsink = (s.sb(x, [P, S4, GROUPS]) for x in ("m", "negm", "total", "esink", "dsink"))
        prT = s.sb("prT", [P, S4 * GROUPS, P])
        prN = s.sb("prN", [NEW, S4 * GROUPS, P])
        yc = s.sb("yc", [SAMPLE, CW])
        yt = s.sb("yt", [P, 8, P])
        ps = s.psum("ps", [P, 8, 512])
        loaded, ws_ready, outs, q_ready = (s.sem(x) for x in ("loaded", "ws_ready", "outs", "q_ready"))
        names = ("scores_full", "maxed", "exped", "normed", "gm_full", "yc_ready", "ycT_full", "prT_full", "prT_read",
                 "ya_full", "y_act", "y_dve")
        scores_full, maxed, exped, normed, gm_full, yc_ready, ycT_full, prT_full, prT_read, ya_full, y_act, y_dve = map(s.sem, names)
        with nc.Block() as block:

            @block.sync
            def _(sp):
                sp.dma_start(za[:], a.z[NB + 1, :, 0:ZG]).then_inc(loaded, 16)
                weights.load(sp, 0)
                weights.load(sp, 1)
                sp.dma_start(ckT[:], a.cache_kT).then_inc(loaded, 16)
                sp.dma_start(cv[:], a.cache_v).then_inc(loaded, 16)
                sp.dma_start(vnew[:], a.z[NB + 1, 0:SAMPLE, ZKV + KVW:ZU].rearrange("(s j) c -> j s c", j=NEW)).then_inc(loaded, 16)
                sp.dma_start(ident[:], a.c_ident).then_inc(loaded, 16)
                sp.dma_start(tril[:], a.c_tril).then_inc(loaded, 16)
                sp.dma_start(bs[:], a.bs_sample).then_inc(loaded, 16)
                sp.dma_start(sink[:], a.sink_sample).then_inc(loaded, 16)
                sp.dma_start(ws[:], a.ws_sample).then_inc(loaded, 16)
                for q in range(4):
                    for r in range(REP):
                        row = q * 32 + r * NEW
                        sp.dma_start(bias[row:row + NEW, :, :],
                                     bass.AP(a.rev.tensor, r * P * TOEP + P - 1,
                                             [[TOEP - 1, NEW], [REP * P * TOEP, GROUPS], [1, KA]])).then_inc(loaded, 16)
                for win, cache, c0 in ((a.k_sample, a.cache_k_rows, ZKV), (a.v_sample, a.cache_v_rows, ZKV + KVW)):
                    sp.dma_start(win[:, 0:P - NEW, :], cache[:, NEW:P, :]).then_inc(outs, 16)
                    sp.dma_start(win[:, P - NEW:P, :],
                                 a.z[NB + 1, 0:SAMPLE, c0:c0 + KVW].rearrange("(s j) c -> s j c", j=NEW)).then_inc(outs, 16)
                sp.dma_start(a.chunk_v, a.z[NB + 1, 0:SAMPLE, ZV:ZG]).then_inc(outs, 16)
                for j in range(2, weights.EARLY):
                    weights.load(sp, j)
                sp.wait_ge(y_act, 1)
                sp.wait_ge(y_dve, 2)
                sp.dma_start(a.yT[NB], yt[:]).then_inc(outs, 16)
                sp.wait_ge(outs, 6 * 16)

            n_loads = 9 + 16

            @block.tensor
            def _(pe):
                pe.wait_ge(loaded, 16 * n_loads)
                pe.wait_ge(q_ready, 1)
                for b in range(SEQS):
                    quad, hi = b % 4, b // 4
                    for g in range(GROUPS):
                        rows = slice(g * HD, (g + 1) * HD)
                        q = qs[rows, b].rearrange("p r j -> p (r j)")
                        out = ps[quad * 32:(quad + 1) * 32, hi * GROUPS + g, :]
                        pe.matmul(out[:, 0:P], q, ckT[rows, b, :], start=True, stop=True)
                        mm = pe.matmul(out[:, P:KA], q, za[rows, ZK + b * NEW:ZK + (b + 1) * NEW],
                                       start=True, stop=True)
                mm.then_inc(scores_full, 1)
                pe.wait_ge(ws_ready, 1)
                for g in range(CG):
                    mm = pe.matmul(ps[0:SAMPLE, 4, g * P:(g + 1) * P], ws[:, g, :],
                                   za[0:SAMPLE, ZV + g * P:ZV + (g + 1) * P], start=True, stop=True)
                mm.then_inc(gm_full, 1)
                pe.wait_ge(yc_ready, 1)
                for g in range(CG):
                    mm = pe.transpose(ps[:, 5, g * P:g * P + SAMPLE], yc[:, g * P:(g + 1) * P], ident[0:SAMPLE, 0:SAMPLE])
                mm.then_inc(ycT_full, 1)
                pe.wait_ge(normed, 1)
                for j in range(S4 * GROUPS):
                    pr = sc[:, j // GROUPS, j % GROUPS, :]
                    pe.transpose(ps[:, 6, j * P:(j + 1) * P], pr[:, 0:P], ident[:])
                    mm = pe.transpose(ps[0:NEW, 7, j * P:(j + 1) * P], pr[:, P:KA], ident[:])
                mm.then_inc(prT_full, 1)
                pe.wait_ge(prT_read, 1)
                for b in range(SEQS):
                    quad, hi = b % 4, b // 4
                    for g in range(GROUPS):
                        out = ps[g * HD:(g + 1) * HD, 0, 0:REP * SAMPLE].rearrange("p (r t) -> p r t", r=REP)[:, :, b * NEW:(b + 1) * NEW]
                        j = hi * GROUPS + g
                        cols = slice(quad * 32, quad * 32 + 32)
                        pe.matmul(out, cv[:, b, g * HD:(g + 1) * HD], prT[:, j, cols].rearrange("p (r t) -> p r t", r=REP), start=True, stop=False)
                        mm = pe.matmul(out, vnew[:, b, g * HD:(g + 1) * HD], prN[:, j, cols].rearrange("p (r t) -> p r t", r=REP), start=False, stop=True)
                mm.then_inc(ya_full, 1)

            @block.scalar
            def _(act):
                weights.split_high(act, 0)
                weights.split_high(act, 1)
                act.wait_ge(loaded, 16 * n_loads)
                for r in range(REP):
                    act.activation(qs[:, :, r, :], za[:, r * P:r * P + SAMPLE].rearrange("p (s j) -> p s j", j=NEW), ACT.Copy)
                act.drain().then_inc(q_ready, 1)
                weights.split_high(act, 2)
                act.wait_ge(maxed, 1)
                for b in range(S4):
                    for g in range(GROUPS):
                        act.activation(sc[:, b, g, :], sc[:, b, g, :], ACT.Exp, bias=negm[:, b, g:g + 1],
                                       accum_out=total[:, b, g:g + 1])
                act.activation(esink[:], dsink[:], ACT.Exp)
                act.drain().then_inc(exped, 1)
                weights.split_high(act, 3)
                act.wait_ge(prT_full, 1)
                act.activation(prT[:], ps[:, 6, :].rearrange("p (j t) -> p j t", j=4), ACT.Copy)
                act.activation(prN[:], ps[0:NEW, 7, :].rearrange("p (j t) -> p j t", j=4), ACT.Copy)
                act.drain().then_inc(prT_read, 1)
                weights.split_high(act, 4)
                act.wait_ge(y_dve, 1)
                act.wait_ge(ya_full, 1)
                act.activation(yt[:, 0:4, 0:SAMPLE], ps[:, 0, 0:REP * SAMPLE].rearrange("p (r t) -> p r t", r=REP),
                               ACT.Copy).then_inc(y_act, 1)
                weights.split_high(act, 5)

            @block.vector
            def _(dve):
                dve.memset(yt[:], 0.0)
                dve.drain().then_inc(y_dve, 1)
                weights.split_low(dve, 0)
                weights.split_low(dve, 1)
                dve.wait_ge(loaded, 16 * n_loads)
                for g in range(CG):
                    last = dve.tensor_tensor(ws[:, g, :], ws[:, g, :], tril[0:SAMPLE, 0:SAMPLE], ALU.mult)
                last.then_inc(ws_ready, 1)
                weights.split_low(dve, 2)
                dve.wait_ge(scores_full, 1)
                for b in range(S4):
                    dve.scalar_tensor_tensor(sc[:, b], ps[:, GROUPS * b:GROUPS * b + GROUPS, 0:KA],
                                             HD ** -0.5, bias[:], ALU.mult, ALU.add)
                dve.drain()
                dve.tensor_reduce(m[:], sc[:], X, ALU.max)
                dve.drain()
                dve.tensor_tensor(m[:], m[:], sink[:], ALU.max)
                dve.drain()
                dve.tensor_scalar(negm[:], m[:], -1.0, None, ALU.mult)
                dve.tensor_tensor(dsink[:], sink[:], m[:], ALU.subtract)
                dve.drain().then_inc(maxed, 1)
                dve.wait_ge(gm_full, 1)
                for g in range(CG):
                    cols = slice(g * P, (g + 1) * P)
                    dve.scalar_tensor_tensor(yc[:, cols], ps[0:SAMPLE, 4, cols], bs[:, g:g + 1],
                                             za[0:SAMPLE, ZU + g * P:ZU + (g + 1) * P], ALU.add, ALU.mult)
                dve.drain().then_inc(yc_ready, 1)
                dve.wait_ge(exped, 1)
                dve.tensor_tensor(total[:], total[:], esink[:], ALU.add)
                dve.drain()
                dve.reciprocal(total[:], total[:])
                dve.drain()
                for b in range(S4):
                    for g in range(GROUPS):
                        dve.tensor_scalar(sc[:, b, g, :], sc[:, b, g, :], total[:, b, g:g + 1], None, ALU.mult)
                dve.drain().then_inc(normed, 1)
                weights.split_low(dve, 3)
                dve.wait_ge(ycT_full, 1)
                dve.tensor_copy(yt[:, 4:8, 0:SAMPLE],
                                ps[:, 5, :].rearrange("p (j t) -> p j t", j=4)[:, :, 0:SAMPLE]).then_inc(y_dve, 1)
                weights.split_low(dve, 4)
                weights.split_low(dve, 5)


def merge_stage(nc, a, weights):
    PIECE = weights.PIECE
    with ExitStack() as stack:
        s = Space(nc, stack, "merge")
        wh, wl = weights.high, weights.low
        gain, shift, ident = s.sb("gain", [P, D]), s.sb("shift", [P, D]), s.sb("ident", [P, P])
        yt, gates = s.sb("yt", [P, 2, 8, P]), s.sb("gates", [P, 2, 2 * D])
        x, pt = s.sb("x", [P, 2, D]), s.sb("pt", [P, 2, 2, P])
        yh, yl = s.sb("yh", [P, 8, P], F16), s.sb("yl", [P, 8, P], F16)
        ph, pl = s.sb("ph", [P, 2, P], F16), s.sb("pl", [P, 2, P], F16)
        mh, ml = s.sb("mh", [P, KT, P], F16), s.sb("ml", [P, KT, P], F16)
        t1, t2, x1 = s.sb("t1", [P, D]), s.sb("t2", [P, D]), s.sb("x1", [P, D])
        x1t, xh, xl = s.sb("x1t", [P, KT, P]), s.sb("xh", [P, KT, P], F16), s.sb("xl", [P, KT, P], F16)
        pp, tg, base = s.sb("pp", [P, D]), s.sb("tg", [P, D]), s.sb("base", [P, D])
        stats, mv, rstd = s.sb("stats", [P, 2, 6]), s.sb("mv", [P, 2]), s.sb("rstd", [P, 1])
        power = s.sb("power", [P, 1])
        ps = s.psum("ps", [P, 8, 512])
        const_loaded = s.sem("const_loaded")
        y_high, y_ready, p_high, p_ready = (s.sem(k) for k in ("y_high", "y_ready", "p_high", "p_ready"))
        ml_ready = s.sem("ml_ready")
        loaded = s.sems("loaded", 2)
        (ac_full, mix_ready, mixT_full, mixT_read, o_full, x_scaled, x1_ready, x1T_full, x1T_read,
         xl_ready, gate_full, gate_act, base_ready, pp_full, pp_read) = (s.sem(k) for k in (
             "ac_full", "mix_ready", "mixT_full", "mixT_read", "o_full", "x_scaled", "x1_ready",
             "x1T_full", "x1T_read", "xl_ready", "gate_full", "gate_act", "base_ready", "pp_full", "pp_read"))
        stored = s.sem("stored")
        var_ready, rstd_ready = s.sem("var_ready"), s.sem("rstd_ready")

        with nc.Block() as block:

            @block.sync
            def _(sp):
                def load(n, slot):
                    for dst, src in ((yt, a.yT[bass.ds(n, 1)]), (gates, a.z[bass.ds(n + 1, 1), :, ZG:ZW]),
                                     (x, a.x_blocks[bass.ds(n, 1)]), (pt, a.pt_blocks[bass.ds(n, 1)])):
                        sp.dma_start(dst[:, slot], src).then_inc(loaded[slot], 16)

                load(0, 0)
                for dst, src in ((ident, a.c_ident), (gain, a.ln1_g), (shift, a.ln1_b)):
                    sp.dma_start(dst[:], src).then_inc(const_loaded, 16)
                for j in range(weights.EARLY, weights.PIECES):
                    weights.load(sp, j)

                def store(n):
                    sp.wait_ge(x1T_read, n + 1)
                    sp.wait_ge(xl_ready, n + 1)
                    cols = bass.ds(n * P, P)
                    sp.dma_start(a.x1T[bass.ds(n, 1)], x1t[:]).then_inc(stored, 16)
                    sp.dma_start(a.xh[:, :, cols], xh[:]).then_inc(stored, 16)
                    sp.dma_start(a.xl[:, :, cols], xl[:]).then_inc(stored, 16)
                    sp.wait_ge(base_ready, n + 2)
                    sp.dma_start(a.base[bass.ds(n, 1)], base[:]).then_inc(stored, 16)

                with sp.Fori(0, NB // 2) as i:
                    for slot in range(2):
                        n = i * 2 + slot
                        sp.wait_ge(base_ready, n + 1)
                        load(n + 1, 1 - slot)
                        store(n)
                store(NB)
                sp.dma_start(a.x1_sample, x1[0:SAMPLE, :]).then_inc(stored, 16)
                sp.wait_ge(stored, (NB + 2) * 64 + 16)

            @block.tensor
            def _(pe):
                def product(bank, high, low, k0, kt, low_ready=lambda: None):
                    for c in range(2):
                        for j, (x, w) in enumerate(((high, wh), (high, wl), (low, wh))):
                            if j == 2 and c == 0:
                                low_ready()
                            for k in range(kt):
                                mm = pe.matmul(ps[:, bank + c, :], x[:, k, :], w[:, k0 + k, c * 512:(c + 1) * 512],
                                               start=j == 0 and k == 0, stop=j == 2 and k == kt - 1)
                    return mm

                def transposes(bank, src):
                    for k in range(KT):
                        mm = pe.transpose(ps[:, bank + k // 4, (k % 4) * P:(k % 4 + 1) * P], src[:, k * P:(k + 1) * P], ident[:])
                    return mm

                def branches(n, slot):
                    pe.wait_ge(y_ready, n + 1)
                    product(0, yh[:, 0:4], yl[:, 0:4], weights.WA, 4)
                    product(2, yh[:, 4:8], yl[:, 4:8], weights.WC, 4).then_inc(ac_full, 1)

                pe.wait_ge(weights.ready, weights.WO // PIECE)
                branches(0, 0)
                pe.wait_ge(const_loaded, 48)

                def body(n, slot):
                    pe.wait_ge(mix_ready, n + 1)
                    transposes(4, t1).then_inc(mixT_full, 1)
                    pe.wait_ge(gate_act, n + 1)
                    pe.wait_ge(mixT_read, n + 1)
                    pe.wait_ge(weights.ready, weights.WPP // PIECE)
                    product(6, mh, ml, weights.WO, KT, lambda: pe.wait_ge(ml_ready, n + 1)).then_inc(o_full, 1)
                    pe.wait_ge(weights.ready, weights.PIECES)
                    pe.wait_ge(p_ready, n + 1)
                    product(4, ph, pl, weights.WPP, 2).then_inc(pp_full, 1)
                    if not (isinstance(n, int) and n == NB):
                        branches(n + 1, 1 - slot)
                    pe.wait_ge(pp_read, n + 1)
                    pe.wait_ge(x1_ready, n + 1)
                    transposes(4, x1).then_inc(x1T_full, 1)
                    pe.wait_ge(x1T_read, n + 1)
                    product(6, xh, xl, weights.WPG, KT, lambda: pe.wait_ge(xl_ready, n + 1)).then_inc(gate_full, 1)

                over_blocks(pe, body)

            def two(bank):
                return ps[:, bank:bank + 2, :]

            def halves(t):
                return t.rearrange("p (c n) -> p c n", c=2)

            @block.scalar
            def _(act):
                act.sem_inc(stored, 64)
                act.sem_inc(gate_act, 1)

                def high_y(n, slot):
                    act.wait_ge(loaded[slot], (n - slot) * 32 + 64)
                    act.activation(yh[:], yt[:, slot], ACT.Copy).then_inc(y_high, 1)

                def high_p(slot):
                    act.activation(ph[:], pt[:, slot], ACT.Copy).then_inc(p_high, 1)

                high_y(0, 0)
                high_p(0)
                for j in range(weights.EARLY, weights.PIECES):
                    weights.split_high(act, j)

                def body(n, slot):
                    act.activation(x[:, slot], x[:, slot], ACT.Copy, scale=ALPHA).then_inc(x_scaled, 1)
                    act.wait_ge(mixT_full, n + 1)
                    act.activation(mh[:].rearrange("p (c k) t -> p c (k t)", c=2), two(4), ACT.Copy,
                                   scale=1.0 / SW).then_inc(mixT_read, 1)
                    if not (isinstance(n, int) and n == NB):
                        high_y(n + 1, 1 - slot)
                    act.wait_ge(base_ready, n + 1)
                    act.wait_ge(pp_full, n + 1)
                    act.activation(halves(pp[:]), two(4), ACT.Copy, scale=1.0 / SW).then_inc(pp_read, 1)
                    if not (isinstance(n, int) and n == NB):
                        high_p(1 - slot)
                    act.wait_ge(x1T_full, n + 1)
                    act.wait_ge(stored, n * 64 + 64)
                    act.activation(x1t[:].rearrange("p (c k) t -> p c (k t)", c=2), two(4), ACT.Copy)
                    act.activation(xh[:].rearrange("p (c k) t -> p c (k t)", c=2), two(4), ACT.Copy)
                    act.drain().then_inc(x1T_read, 1)
                    act.wait_ge(gate_full, n + 1)
                    act.activation(halves(tg[:]), two(6), ACT.Tanh, scale=0.5 / SW).then_inc(gate_act, 1)

                over_blocks(act, body)

            @block.gpsimd
            def _(pool):
                pool.memset(power[:], -0.5)
                pool.drain()
                over_blocks(pool, lambda n, slot: inverse_deviation(pool, P, mv, power, rstd, var_ready, rstd_ready, n + 1))

            @block.vector
            def _(dve):
                def low_y(n, slot):
                    dve.wait_ge(y_high, n + 1)
                    dve.tensor_tensor(yl[:], yt[:, slot], yh[:], ALU.subtract).then_inc(y_ready, 1)

                def low_p(n, slot):
                    dve.wait_ge(p_high, n + 1)
                    dve.tensor_tensor(pl[:], pt[:, slot], ph[:], ALU.subtract).then_inc(p_ready, 1)

                def mix(n, slot):
                    dve.wait_ge(loaded[slot], (n - slot) * 32 + 64)
                    dve.wait_ge(ac_full, n + 1)
                    dve.scalar_tensor_tensor(halves(t1[:]), halves(gates[:, slot, 0:D]), 1.0, two(0), ALU.add, ALU.mult)
                    dve.scalar_tensor_tensor(halves(t2[:]), halves(gates[:, slot, D:2 * D]), 1.0, two(2), ALU.add, ALU.mult)
                    dve.drain()
                    dve.tensor_tensor(t1[:], t1[:], t2[:], ALU.add)
                    dve.drain().then_inc(mix_ready, 1)

                def body(n, slot):
                    dve.wait_ge(mixT_read, n + 1)
                    dve.scalar_tensor_tensor(ml[:].rearrange("p (c k) t -> p c (k t)", c=2), two(4), 1.0 / SW,
                                             mh[:].rearrange("p (c k) t -> p c (k t)", c=2), ALU.mult,
                                             ALU.subtract).then_inc(ml_ready, 1)
                    if not (isinstance(n, int) and n == NB):
                        low_y(n + 1, 1 - slot)
                    dve.wait_ge(x_scaled, n + 1)
                    dve.wait_ge(o_full, n + 1)
                    dve.scalar_tensor_tensor(halves(x1[:]), two(6), 0.5 / SW, halves(x[:, slot]), ALU.mult, ALU.add)
                    dve.drain()
                    layer_norm_stats(dve, [x1[:, 0:512], x1[:, 512:1024]], P, stats, mv, var_ready, rstd_ready, n + 1)
                    dve.tensor_scalar(x1[:], x1[:], mv[:, 0:1], rstd[:, :], ALU.subtract, ALU.mult)
                    dve.drain()
                    dve.tensor_tensor(x1[:], x1[:], gain[:], ALU.mult)
                    dve.drain()
                    dve.tensor_tensor(x1[:], x1[:], shift[:], ALU.add)
                    dve.drain().then_inc(x1_ready, 1)
                    if not (isinstance(n, int) and n == NB):
                        mix(n + 1, 1 - slot)
                        low_p(n + 1, 1 - slot)
                    dve.wait_ge(x1T_read, n + 1)
                    dve.tensor_tensor(xl[:], x1t[:], xh[:], ALU.subtract).then_inc(xl_ready, 1)
                    dve.wait_ge(gate_act, n + 2)
                    dve.scalar_tensor_tensor(t2[:], tg[:], 1.0, pp[:], ALU.add, ALU.mult)
                    dve.wait_ge(stored, n * 64 + 64)
                    dve.tensor_scalar(base[:], x1[:], ALPHA, None, ALU.mult)
                    dve.drain()
                    dve.scalar_tensor_tensor(base[:], t2[:], 0.5, base[:], ALU.mult, ALU.add)
                    dve.drain().then_inc(base_ready, 1)

                dve.sem_inc(base_ready, 1)
                low_y(0, 0)
                low_p(0, 0)
                weights.split_low(dve, weights.EARLY)
                weights.split_low(dve, weights.EARLY + 1)
                mix(0, 0)
                for j in range(weights.EARLY + 2, weights.PIECES):
                    weights.split_low(dve, j)
                dve.wait_ge(const_loaded, 48)
                over_blocks(dve, body)


def route_stage(nc, a):
    OCTETS = 10
    G = BT // QT
    with ExitStack() as stack:
        s = Space(nc, stack, "route")
        wq, sub = s.sb("wq", [P, KT, 2 * PH * P]), s.sb("sub", [P, 2 * PH, KEYS])
        ident, iota, iota16 = s.sb("ident", [P, P]), s.sb("iota", [P, KEYS, QT], F16), s.sb("iota16", [P, TOPK])
        x1t, qt = s.sb("x1t", [P, KT, P]), s.sb("qt", [P, 2 * PH, P])
        sc = s.sb("sc", [P, 2 * PH, KEYS])
        rest = s.sb("rest", [P, 2 * PH * KEYS])
        pair = s.sb("pair", [P, PH, OCTETS * 8])
        match = s.sb("match", [P, PH, TOPK, TOPK], F16)
        sv, si = s.sb("sv", [P, 2 * PH, TOPK]), s.sb("si", [P, 2 * PH, TOPK], U32)
        sif = s.sb("sif", [P, PH, 2, TOPK], F16)
        fv, fi = s.sb("fv", [P, PH, TOPK]), s.sb("fi", [P, PH, TOPK], U32)
        half_u = s.sb("half_u", [P, 2, PH, TOPK], U32)
        half_f = s.sb("half_f", [P, 2, PH, TOPK])
        place_j = s.sb("place_j", [P, PH, TOPK])
        last_octet = s.sb("last_octet", [P, PH, TOPK])
        pick = s.sb("pick", [P, 3, PH, TOPK])
        gsum = s.sb("gsum", [P, PH])
        col = s.sb("col", [P, 2, P], F16)
        gt, gh, gl = s.sb("gt", [P, P]), s.sb("gh", [P, P], F16), s.sb("gl", [P, P], F16)
        hot_r, hot_c = s.sb("hot_r", [P, 2, G, KEYS, QT], F16), s.sb("hot_c", [P, 2, G, KEYS, QT], F16)
        hot_h, hot_l = s.sb("hot_h", [P, 2, G, KEYS, QT], F16), s.sb("hot_l", [P, 2, G, KEYS, QT], F16)
        one, scrap = s.sb("one", [P, 1]), s.sb("scrap", [P, 1])
        place_f = s.sb("place_f", [P, 2, SAMPLE])
        place, gate = s.sb("place", [P, SAMPLE], U32), s.sb("gate", [P, SAMPLE])
        gbuf = s.sb("gbuf", [P, KEYS, P])
        ps = s.psum("ps", [P, 8, 512])
        w_loaded = s.sems("w_loaded", 4)
        const_loaded, x_loaded = s.sem("const_loaded"), s.sem("x_loaded")
        q_full, q_read, s_full, s_read = (s.sem(k) for k in ("q_full", "q_read", "s_full", "s_read"))
        sc_used, exp_in, exp_out, picked = (s.sem(k) for k in ("sc_used", "exp_in", "exp_out", "picked"))
        pickT_full = s.sem("pickT_full")
        rows_ready, lows_ready = s.sem("rows_ready"), s.sem("lows_ready")
        hots_ready, places_ready, places_stored = s.sem("hots_ready"), s.sem("places_ready"), s.sem("places_stored")
        g_full, g_read, g_stored = s.sem("g_full"), s.sem("g_read"), s.sem("g_stored")
        block_done = s.sem("block_done")
        batches = P // BT

        def over_batches(eng, n, body):
            if isinstance(n, int) and n == NB:
                return
            with eng.Fori(0, batches // 4) as j:
                for k in range(4):
                    body(j * 4 + k, k % 2)

        def spread(values):
            return values.rearrange("p (g t) -> p g t", t=QT).unsqueeze(2).broadcast_to([P, G, KEYS, QT])

        numbers = iota[:].unsqueeze(1).broadcast_to([P, G, KEYS, QT])

        with nc.Block() as block:

            @block.sync
            def _(sp):
                sp.dma_start(x1t[:], a.x1T[0]).then_inc(x_loaded, 16)
                for j in range(4):
                    cols = slice(j * 4 * P, (j + 1) * 4 * P)
                    sp.dma_start(wq[:, :, cols], a.wq[:, :, cols]).then_inc(w_loaded[j], 16)
                for dst, src in ((sub, a.subT), (ident, a.c_ident), (iota, a.c_iota), (iota16, a.c_iota16)):
                    sp.dma_start(dst[:], src).then_inc(const_loaded, 16)

                def load_x(n):
                    sp.wait_ge(q_full, n * 4)
                    sp.dma_start(x1t[:], a.x1T[bass.ds(n, 1)]).then_inc(x_loaded, 16)

                def store_g(n):
                    sp.wait_ge(block_done, n + 1)
                    sp.dma_start(a.g[:, :, bass.ds(n * P, P)].rearrange("i p t -> p i t"), gbuf[:]).then_inc(g_stored, 16)

                load_x(1)
                with sp.Fori(0, NB - 1) as n:
                    load_x(n + 2)
                    store_g(n)
                store_g(NB - 1)
                sp.wait_ge(places_ready, 1)
                sp.dma_start(a.place, place[:]).then_inc(places_stored, 16)
                sp.dma_start(a.gate, gate[:]).then_inc(places_stored, 16)
                sp.wait_ge(places_stored, 32)
                sp.wait_ge(g_stored, 16 * (NB + 1))

            @block.tensor
            def _(pe):
                pe.sem_inc(g_full, 4)

                def queries(n):
                    pe.wait_ge(x_loaded, n * 16 + 16)
                    for j in range(4):
                        pe.wait_ge(q_read, n * 4 + j + 1)
                        pe.wait_ge(w_loaded[j], 16)
                        for t in range(4):
                            c = (4 * j + t) * P
                            for k in range(KT):
                                mm = pe.matmul(ps[:, j % 2, t * P:(t + 1) * P], wq[:, k, c:c + P], x1t[:, k, :],
                                               start=k == 0, stop=k == KT - 1)
                        mm.then_inc(q_full, 1)

                def scores(n):
                    for j in range(4):
                        pe.wait_ge(q_read, n * 4 + j + 3)
                        pe.wait_ge(s_read, n * 4 + j + 1)
                        for t in range(4):
                            hc = 4 * j + t
                            mm = pe.matmul(ps[:, 2, t * P:(t + 1) * P], qt[:, hc, :], sub[:, hc, :], start=True, stop=True)
                        mm.then_inc(s_full, 1)

                queries(0)
                pe.wait_ge(const_loaded, 64)
                scores(0)

                def body(n, slot):
                    if not (isinstance(n, int) and n == NB):
                        queries(n + 1)
                    pe.wait_ge(picked, n + 1)
                    for j in range(3):
                        mm = pe.transpose(ps[:, 3, j * P:(j + 1) * P], pick[:, j].rearrange("p h k -> p (h k)"), ident[:])
                    mm.then_inc(pickT_full, 1)
                    if not (isinstance(n, int) and n == NB):
                        scores(n + 1)

                    def batch(b, half):
                        pe.wait_ge(hots_ready, n * batches + b + 1)
                        pe.wait_ge(lows_ready, n * batches + b + 3)
                        for q in range(G):
                            pe.wait_ge(g_read, (n * batches + b) * 2 + q + 1)
                            for t in range(4):
                                o = ps[:, 4 + 2 * half + q, t * P:(t + 1) * P]
                                pe.matmul(o, hot_c[:, half, q, :, t], hot_h[:, half, q, :, t], start=True, stop=False)
                                mm = pe.matmul(o, hot_c[:, half, q, :, t], hot_l[:, half, q, :, t], start=False, stop=True)
                            mm.then_inc(g_full, 1)
                    over_batches(pe, n, batch)

                over_blocks(pe, body)

            @block.scalar
            def _(act):
                act.sem_inc(q_read, 2)
                act.sem_inc(s_read, 1)
                act.sem_inc(g_read, 4)
                act.sem_inc(g_stored, 16)
                act.sem_inc(sc_used, 1)

                def queries(n):
                    for j in range(4):
                        act.wait_ge(q_full, n * 4 + j + 1)
                        act.activation(qt[:, 4 * j:4 * j + 4, :], ps[:, j % 2, :].rearrange("p (t n) -> p t n", t=4),
                                       ACT.Copy).then_inc(q_read, 1)

                def scores(n):
                    act.wait_ge(sc_used, n + 1)
                    for j in range(4):
                        act.wait_ge(s_full, n * 4 + j + 1)
                        act.activation(sc[:, 4 * j:4 * j + 4, :], ps[:, 2, :].rearrange("p (t n) -> p t n", t=4),
                                       ACT.Copy).then_inc(s_read, 1)

                queries(0)
                scores(0)

                def body(n, slot):
                    if not (isinstance(n, int) and n == NB):
                        queries(n + 1)
                    act.wait_ge(exp_in, n + 1)
                    act.activation(pick[:, 2], pick[:, 2], ACT.Exp).then_inc(exp_out, 1)
                    if not (isinstance(n, int) and n == NB):
                        scores(n + 1)
                    if isinstance(n, int) and n == NB:
                        return
                    act.wait_ge(g_stored, n * 16 + 16)

                    def batch(b, half):
                        for q in range(G):
                            act.wait_ge(g_full, (n * batches + b) * 2 + q + 5)
                            act.wait_ge(const_loaded, 64)
                            act.activation(gbuf[:, :, bass.ds(b * BT + 4 * q, 4)],
                                           ps[:, 4 + 2 * half + q, :].rearrange("p (t i) -> p i t", t=4),
                                           ACT.Copy).then_inc(g_read, 1)
                    over_batches(act, n, batch)
                    act.drain().then_inc(block_done, 1)

                over_blocks(act, body)

            @block.gpsimd
            def _(pool):
                pool.memset(one[:], 1.0)
                pool.drain()
                pool.sem_inc(lows_ready, 2)

                def body(n, slot):
                    def batch(b, half):
                        pool.wait_ge(rows_ready, n * batches + b + 1)
                        pool.tensor_tensor(scrap[:], one[:], one[:], ALU.mult)
                        pool.tensor_tensor(hot_l[:, half], hot_r[:, half], spread(gl[:, bass.ds(b * BT, BT)]), ALU.mult)
                        pool.drain().then_inc(lows_ready, 1)
                    over_batches(pool, n, batch)

                over_blocks(pool, body)

            @block.vector
            def _(dve):
                dve.wait_ge(const_loaded, 64)

                def top16(scores, rest, values, indices):
                    n = len(scores)
                    for j in range(n):
                        dve.max(values[j][:, 0:8], scores[j])
                    dve.drain()
                    for j in range(n):
                        dve.max_index(indices[j][:, 0:8], values[j][:, 0:8], scores[j])
                        dve.match_replace(rest[j], values[j][:, 0:8], scores[j], LOWEST)
                    dve.drain()
                    for j in range(n):
                        dve.max(values[j][:, 8:16], rest[j])
                    dve.drain()
                    for j in range(n):
                        dve.max_index(indices[j][:, 8:16], values[j][:, 8:16], rest[j])

                def body(n, slot):
                    dve.wait_ge(s_read, n * 4 + 5)
                    dve.memset(gsum[:], 0.0)
                    hc = range(2 * PH)
                    top16([sc[:, j, :] for j in hc], [rest[:, j * KEYS:(j + 1) * KEYS] for j in hc],
                          [sv[:, j, :] for j in hc], [si[:, j, :] for j in hc])
                    dve.drain().then_inc(sc_used, 1)
                    half = sv[:].rearrange("p (h c) k -> p h c k", c=2)
                    first, second = half[:, :, 0], half[:, :, 1]
                    dve.tensor_tensor(pair[:, :, 0:16], first[:, :, 0:1].broadcast_to([P, PH, 16]), second, ALU.add)
                    dve.tensor_tensor(pair[:, :, 16:72].rearrange("p h (i j) -> p h i j", j=8),
                                      first[:, :, 1:8].unsqueeze(3).broadcast_to([P, PH, 7, 8]),
                                      second[:, :, 0:8].unsqueeze(2).broadcast_to([P, PH, 7, 8]), ALU.add)
                    dve.tensor_tensor(pair[:, :, 72:80], first[:, :, 8:16], second[:, :, 0:1].broadcast_to([P, PH, 8]), ALU.add)
                    dve.tensor_copy(sif[:].rearrange("p h c k -> p (h c k)"), si[:].rearrange("p h k -> p (h k)"))
                    dve.drain()
                    top16([pair[:, h, :] for h in range(PH)], [rest[:, h * KEYS:h * KEYS + OCTETS * 8] for h in range(PH)],
                          [fv[:, h, :] for h in range(PH)], [fi[:, h, :] for h in range(PH)])
                    dve.drain()
                    dve.tensor_tensor(pick[:, 2], fv[:], fv[:, :, 0:1].broadcast_to([P, PH, TOPK]), ALU.subtract)
                    dve.tensor_scalar(half_u[:, 0], fi[:], 3, None, ALU.logical_shift_right)
                    dve.tensor_scalar(half_u[:, 1], fi[:], 7, None, ALU.bitwise_and)
                    dve.drain().then_inc(exp_in, 1)
                    dve.tensor_copy(half_f[:].rearrange("p c h k -> p (c h k)"), half_u[:].rearrange("p c h k -> p (c h k)"))
                    dve.drain()
                    octet, within = half_f[:, 0], half_f[:, 1]
                    dve.scalar_tensor_tensor(last_octet[:], octet, float(OCTETS - 1), within, ALU.is_equal, ALU.mult)
                    dve.tensor_scalar(place_j[:], octet, 1.0, 8.0, ALU.is_equal, ALU.mult)
                    dve.drain()
                    dve.tensor_tensor(within, within, last_octet[:], ALU.subtract)
                    dve.tensor_scalar(octet, octet, -1.0, 0.0, ALU.add, ALU.max)
                    dve.drain()
                    dve.tensor_tensor(within, within, place_j[:], ALU.add)
                    dve.tensor_tensor(octet, octet, last_octet[:], ALU.add)
                    dve.drain()
                    for c in range(2):
                        dve.tensor_tensor(match[:], half_f[:, c].unsqueeze(3).broadcast_to([P, PH, TOPK, TOPK]),
                                          iota16[:].unsqueeze(1).unsqueeze(1).broadcast_to([P, PH, TOPK, TOPK]), ALU.is_equal)
                        dve.drain()
                        dve.tensor_tensor(match[:], match[:], sif[:, :, c].unsqueeze(2).broadcast_to([P, PH, TOPK, TOPK]), ALU.mult)
                        dve.drain()
                        dve.tensor_reduce(pick[:, c], match[:], X, ALU.add)
                        dve.drain()
                    dve.wait_ge(exp_out, n + 1)
                    dve.tensor_reduce(gsum[:], pick[:, 2], X, ALU.add)
                    dve.drain()
                    dve.reciprocal(gsum[:], gsum[:])
                    dve.drain()
                    dve.tensor_tensor(pick[:, 2], pick[:, 2], gsum[:].unsqueeze(2).broadcast_to([P, PH, TOPK]), ALU.mult)
                    dve.drain().then_inc(picked, 1)
                    dve.wait_ge(pickT_full, n + 1)
                    choice = ps[:, 3, 0:2 * P].rearrange("p (c t) -> p c t", c=2)
                    if isinstance(n, int) and n == NB:
                        dve.tensor_copy(place_f[:], choice[:, :, 0:SAMPLE])
                        dve.tensor_copy(gate[:], ps[:, 3, 2 * P:2 * P + SAMPLE])
                        dve.drain()
                        dve.scalar_tensor_tensor(place_f[:, 0], place_f[:, 0], float(KEYS), place_f[:, 1], ALU.mult, ALU.add)
                        dve.drain()
                        dve.tensor_copy(place[:], place_f[:, 0])
                        dve.drain().then_inc(places_ready, 1)
                        return
                    dve.wait_ge(lows_ready, n * batches + 2)
                    dve.wait_ge(const_loaded, 64)
                    dve.tensor_copy(col[:], choice)
                    dve.tensor_scalar(gt[:], ps[:, 3, 2 * P:3 * P], SG, None, ALU.mult)
                    dve.drain()
                    dve.tensor_copy(gh[:], gt[:])
                    dve.drain()
                    dve.tensor_tensor(gl[:], gt[:], gh[:], ALU.subtract)
                    dve.drain()

                    def batch(b, half):
                        dve.wait_ge(g_full, (n * batches + b) * 2 + 2)
                        dve.wait_ge(const_loaded, 64)
                        now = bass.ds(b * BT, BT)
                        dve.tensor_tensor(hot_r[:, half], numbers, spread(col[:, 0, now]), ALU.is_equal)
                        dve.drain().then_inc(rows_ready, 1)
                        dve.tensor_tensor(hot_c[:, half], numbers, spread(col[:, 1, now]), ALU.is_equal)
                        dve.tensor_tensor(hot_h[:, half], hot_r[:, half], spread(gh[:, now]), ALU.mult)
                        dve.drain().then_inc(hots_ready, 1)
                    over_batches(dve, n, batch)

                over_blocks(dve, body)


def experts_stage(nc, a):
    ROWS = 4
    TURNS = KEYS // ROWS
    HALF = TURNS // 2
    assert HALF * ROWS == SAMPLE
    W = 512
    NC = PROMPT // W
    YB = 2
    with ExitStack() as stack:
        s = Space(nc, stack, "experts")
        xh, xl = s.sb("xh", [P, KT, PROMPT], F16), s.sb("xl", [P, KT, PROMPT], F16)
        y = s.sb("y", [P, NB + 1, D])
        ut, uh, ul = s.sb("ut", [P, 2, D]), s.sb("uh", [P, 2, KT, P], F16), s.sb("ul", [P, 2, KT, P], F16)
        vt = s.sb("vt", [P, 2, D])
        vh, vl = s.sb("vh", [P, ROWS, D], F16), s.sb("vl", [P, ROWS, D], F16)
        g = s.sb("g", [P, 2, PROMPT])
        act_a, hf = s.sb("act_a", [P, NC, W]), s.sb("hf", [P, W])
        hh, hl = s.sb("hh", [P, ROWS, PROMPT], F16), s.sb("hl", [P, ROWS, PROMPT], F16)
        gain, shift = s.sb("gain", [P, D]), s.sb("shift", [P, D])
        stats, mv, rstd = s.sb("stats", [P, 2, 6]), s.sb("mv", [P, 2]), s.sb("rstd", [P, 2])
        center = s.sb("center", [P, 2])
        power, scrap = s.sb("power", [P, 1]), s.sb("scrap", [P, 1])
        place, gate = s.sb("place", [P, SAMPLE], U32), s.sb("gate", [P, SAMPLE])
        now_place = s.sb("now_place", [P, 2], U32)
        fetched, xb, prod = s.sb("fetched", [P, 2, D]), s.sb("xb", [P, 2, D]), s.sb("prod", [P, D])
        dot, av, hs = s.sb("dot", [P, ROWS]), s.sb("av", [P, SAMPLE]), s.sb("hs", [P, SAMPLE])
        hs_high, sel = s.sb("hs_high", [P, SAMPLE], F16), s.sb("sel", [P, SAMPLE * P], F16)
        fh, fl = s.sb("fh", [P, 2, D], F16), s.sb("fl", [P, 2, D], F16)
        acc, fold = s.sb("acc", [P, D]), s.sb("fold", [P, SAMPLE])
        ps = s.psum("ps", [P, 8, 512])
        x_loaded, y_loaded, place_loaded = s.sem("x_loaded"), s.sem("y_loaded"), s.sem("place_loaded")
        u_loaded, v_loaded, g_loaded = s.sems("u_loaded", 2), s.sems("v_loaded", 2), s.sems("g_loaded", 2)
        xb_loaded, gathered = s.sems("xb_loaded", 2), s.sems("gathered", 2)
        u_high, u_ready, v_high, v_ready = (s.sem(k) for k in ("u_high", "u_ready", "v_high", "v_ready"))
        a_full, a_read, h_temp, h_ready = (s.sem(k) for k in ("a_full", "a_read", "h_temp", "h_ready"))
        y_full, y_read, turn_done = s.sem("y_full"), s.sem("y_read"), s.sem("turn_done")
        fetched_used, av_ready, av_act, hs_ready = (s.sem(k) for k in ("fetched_used", "av_ready", "av_act", "hs_ready"))
        fh_ready, fl_ready, f_used, sel_clear = (s.sem(k) for k in ("fh_ready", "fl_ready", "f_used", "sel_clear"))
        acc_full, acc_read, ys_full = s.sem("acc_full"), s.sem("acc_read"), s.sem("ys_full")
        center_ready, standard, gained = s.sem("center_ready"), s.sem("standard"), s.sem("gained")
        y_ready, y_stored = s.sem("y_ready"), s.sem("y_stored")
        var_ready, rstd_ready = s.sem("var_ready"), s.sem("rstd_ready")

        def over_turns(eng, body, between=lambda: None):
            with eng.Fori(0, HALF) as i:
                body(i, True, False)
            between()
            with eng.Fori(HALF, TURNS - 1) as i:
                body(i, False, False)
            body(TURNS - 1, False, True)

        with nc.Block() as block:

            @block.sync
            def _(sp):
                def load_u(e, slot):
                    sp.dma_start(ut[:, slot], a.uT[bass.ds(e, 1)]).then_inc(u_loaded[slot], 16)

                def load_vg(e, slot):
                    sp.dma_start(g[:, slot], a.g[bass.ds(e, 1)]).then_inc(g_loaded[slot], 16)
                    sp.dma_start(vt[:, slot], a.v[bass.ds(e, 1)]).then_inc(v_loaded[slot], 16)

                load_u(0, 0)
                sp.dma_start(xh[:], a.xh[:, :, 0:PROMPT]).then_inc(x_loaded, 16)
                sp.dma_start(xl[:], a.xl[:, :, 0:PROMPT]).then_inc(x_loaded, 16)
                load_u(1, 1)
                load_vg(0, 0)
                load_vg(1, 1)
                for dst, src in ((place, a.place), (gate, a.gate)):
                    sp.dma_start(dst[:], src).then_inc(place_loaded, 16)
                for dst, src in ((y, a.base.rearrange("b p d -> p b d")), (gain, a.ln2_g), (shift, a.ln2_b), (fold, a.c_fold)):
                    sp.dma_start(dst[:], src).then_inc(y_loaded, 16)

                def body(i, from_u, last):
                    for m in range(ROWS):
                        e, slot = i * ROWS + m, m % 2
                        if from_u:
                            sp.wait_ge(fetched_used, e + 1)
                            sp.dma_start(xb[:, slot], a.x1_sample[bass.ds(e, 1), :].broadcast_to([P, D])).then_inc(xb_loaded[slot], 16)
                        if last and m >= ROWS - 2:
                            continue
                        sp.wait_ge(u_ready, e + 1)
                        load_u(e + 2, slot)
                        sp.wait_ge(v_ready, e + 1)
                        sp.wait_ge(h_temp, e * NC + 2 * NC)
                        load_vg(e + 2, slot)

                over_turns(sp, body)
                sp.wait_ge(y_ready, 1)
                sp.dma_start(a.y_sample, y[0:SAMPLE, NB, :]).then_inc(y_stored, 16)
                for b in range(NB):
                    sp.wait_ge(y_ready, b + 2)
                    sp.dma_start(a.y_prompt[b * P:(b + 1) * P, :], y[:, b, :]).then_inc(y_stored, 16)
                sp.wait_ge(y_stored, 16 * (NB + 1))

            @block.tensor
            def _(pe):
                pe.sem_inc(turn_done, 1)
                pe.wait_ge(x_loaded, 32)

                def body(i, from_u, last):
                    for m in range(ROWS):
                        e, slot = i * ROWS + m, m % 2
                        pe.wait_ge(u_ready, e + 1)
                        for c in range(NC):
                            bank = (m * NC + c) % 4
                            pe.wait_ge(a_read, e * NC + c + 1)
                            for k in range(KT):
                                for j, (w, x) in enumerate(((uh, xh), (uh, xl), (ul, xh))):
                                    mm = pe.matmul(ps[:, bank, :], w[:, slot, k, :], x[:, k, c * W:(c + 1) * W],
                                                   start=k == 0 and j == 0, stop=k == KT - 1 and j == 2)
                            mm.then_inc(a_full, 1)
                        if not from_u:
                            if m == 0:
                                pe.wait_ge(acc_read, (i - HALF) + 1)
                            pe.wait_ge(fl_ready, (e - SAMPLE) + 1)
                            for c in range(2):
                                for j, part in enumerate((fh, fl)):
                                    mm = pe.matmul(ps[:, 6 + c, :], sel[:, bass.ds((e - SAMPLE) * P, P)],
                                                   part[:, slot, c * 512:(c + 1) * 512],
                                                   start=m == 0 and j == 0, stop=m == ROWS - 1 and j == 1)
                            mm.then_inc(f_used, 1)
                    if not from_u:
                        pe.drain().then_inc(acc_full, 1)
                    if last:
                        pe.wait_ge(acc_read, HALF + 1)
                        pe.wait_ge(a_read, KEYS * NC + 4)
                        for c in range(2):
                            mm = pe.matmul(ps[0:SAMPLE, c, :], fold[:], acc[:, c * 512:(c + 1) * 512], start=True, stop=True)
                        mm.then_inc(ys_full, 1)
                    pe.wait_ge(v_ready, i * ROWS + ROWS)
                    for b in range(NB):
                        if b * P % W == 0:
                            pe.wait_ge(h_ready, i * (ROWS * NC) + (ROWS - 1) * NC + b * P // W + 1)
                        for d in range(2):
                            q = b * 2 + d
                            pe.wait_ge(y_read, i * (2 * NB) + q + 1)
                            for m in range(ROWS):
                                for j, (h, v) in enumerate(((hh, vh), (hh, vl), (hl, vh))):
                                    mm = pe.matmul(ps[:, 4 + q % YB, :], h[:, m, b * P:(b + 1) * P], v[:, m, d * 512:(d + 1) * 512],
                                                   start=m == 0 and j == 0, stop=m == ROWS - 1 and j == 2)
                            mm.then_inc(y_full, 1)
                    pe.drain().then_inc(turn_done, 1)

                def between():
                    pe.wait_ge(hs_ready, 1)
                    pe.wait_ge(y_loaded, 64)

                over_turns(pe, body, between)

            @block.scalar
            def _(act):
                act.sem_inc(a_read, 4)
                act.sem_inc(f_used, 2)

                def high_u(e, slot, count):
                    act.wait_ge(u_loaded[slot], count)
                    act.activation(uh[:, slot].rearrange("p k t -> p (k t)"), ut[:, slot], ACT.Copy, scale=SU).then_inc(u_high, 1)

                high_u(0, 0, 16)
                high_u(1, 1, 16)

                def body(i, from_u, last):
                    for m in range(ROWS):
                        e, slot = i * ROWS + m, m % 2
                        if m == 0:
                            act.wait_ge(turn_done, i + 1)
                        act.wait_ge(v_loaded[slot], (i * 2 + m // 2) * 16 + 16)
                        act.activation(vh[:, m], vt[:, slot], ACT.Copy, scale=SV).then_inc(v_high, 1)
                        if not from_u:
                            act.wait_ge(f_used, (e - SAMPLE) + 1)
                            act.wait_ge(gathered[slot], (i * 2 + m // 2) * 16 + 16)
                            act.activation(fh[:, slot], fetched[:, slot], ACT.Copy, scale=SV).then_inc(fh_ready, 1)
                        for c in range(NC):
                            act.wait_ge(h_temp, e * NC + c + 1)
                            act.wait_ge(a_full, e * NC + c + 1)
                            act.activation(act_a[:, c, :], ps[:, (m * NC + c) % 4, :],
                                           ACT.Gelu_apprx_tanh, scale=1.0 / SU).then_inc(a_read, 1)
                        if not (last and m >= ROWS - 2):
                            high_u(e + 2, slot, (i * 2 + m // 2) * 16 + 32)

                def between():
                    act.wait_ge(av_ready, 1)
                    act.activation(hs[:], av[:], ACT.Gelu_apprx_tanh).then_inc(av_act, 1)

                over_turns(act, body, between)
                for k in range(NB + 1):
                    rows, b = (SAMPLE, NB) if k == 0 else (P, k - 1)
                    act.wait_ge(center_ready, k + 1)
                    act.activation(y[0:rows, b, :], y[0:rows, b, :], ACT.Identity, bias=center[:rows, k % 2:k % 2 + 1],
                                   scale=rstd[:rows, k % 2:k % 2 + 1]).then_inc(standard, 1)

            @block.gpsimd
            def _(pool):
                pool.memset(power[:], -0.5)
                pool.memset(sel[:], 0.0).then_inc(sel_clear, 1)
                pool.wait_ge(place_loaded, 32)
                pool.drain()

                def body(i, from_u, last):
                    for m in range(ROWS):
                        t, slot = i * ROWS + m, m % 2
                        pool.wait_ge(fetched_used, t + 1)
                        pool.tensor_tensor(scrap[:], power[:], power[:], ALU.mult)
                        token = t if from_u else t - SAMPLE
                        pool.tensor_copy(now_place[:, slot:slot + 1], place[:, bass.ds(token, 1)])
                        pool.drain()
                        rows = a.u_rows if from_u else a.v.rearrange("r e d -> (r e) d")
                        pool.indirect_dma_start(fetched[:, slot], None, rows,
                                                bass.IndirectOffsetOnAxis(ap=now_place[:, slot:slot + 1], axis=0)).then_inc(gathered[slot], 16)

                def shifted(k):
                    rows, b = (SAMPLE, NB) if k == 0 else (P, k - 1)
                    pool.wait_ge(gained, k + 1)
                    pool.tensor_tensor(y[0:rows, b, :], y[0:rows, b, :], shift[:rows, :], ALU.add).then_inc(y_ready, 1)

                over_turns(pool, body)

                for k in range(NB + 1):
                    rows = SAMPLE if k == 0 else P
                    inverse_deviation(pool, rows, mv, power, rstd[:, k % 2:k % 2 + 1], var_ready, rstd_ready, k + 1)
                    if k > 0:
                        shifted(k - 1)
                shifted(NB)

            @block.vector
            def _(dve):
                dve.sem_inc(h_temp, NC)
                dve.sem_inc(y_read, YB)
                dve.sem_inc(fetched_used, 2)
                dve.sem_inc(acc_read, 1)
                dve.memset(acc[:], 0.0)

                def low_u(e, slot):
                    dve.wait_ge(u_high, e + 1)
                    dve.scalar_tensor_tensor(ul[:, slot].rearrange("p k t -> p (k t)"), ut[:, slot], SU,
                                             uh[:, slot].rearrange("p k t -> p (k t)"), ALU.mult, ALU.subtract).then_inc(u_ready, 1)

                def statistics(rows, b, k):
                    row = y[0:rows, b, :]
                    if k >= 2:
                        dve.wait_ge(standard, k - 1)
                    dve.drain()
                    layer_norm_stats(dve, [row[:, 0:512], row[:, 512:1024]], rows, stats, mv, var_ready, rstd_ready, k + 1)
                    dve.scalar_tensor_tensor(center[:rows, k % 2:k % 2 + 1], mv[:rows, 0:1], -1.0,
                                             rstd[:rows, k % 2:k % 2 + 1], ALU.mult, ALU.mult)
                    dve.drain().then_inc(center_ready, 1)

                def gain_of(rows, b, k):
                    dve.wait_ge(standard, k + 1)
                    dve.tensor_tensor(y[0:rows, b, :], y[0:rows, b, :], gain[:rows, :], ALU.mult).then_inc(gained, 1)

                low_u(0, 0)
                low_u(1, 1)

                def body(i, from_u, last):
                    dve.wait_ge(turn_done, i + 1)
                    for m in range(ROWS):
                        e, slot = i * ROWS + m, m % 2
                        dve.wait_ge(v_high, e + 1)
                        dve.scalar_tensor_tensor(vl[:, m], vt[:, slot], SV, vh[:, m], ALU.mult, ALU.subtract).then_inc(v_ready, 1)
                        if not from_u:
                            dve.wait_ge(fh_ready, (e - SAMPLE) + 1)
                            dve.scalar_tensor_tensor(fl[:, slot], fetched[:, slot], SV, fh[:, slot], ALU.mult, ALU.subtract).then_inc(fl_ready, 1)
                            dve.drain().then_inc(fetched_used, 1)
                        dve.wait_ge(g_loaded[slot], (i * 2 + m // 2) * 16 + 16)
                        for c in range(NC):
                            cols = slice(c * W, (c + 1) * W)
                            dve.wait_ge(a_read, e * NC + c + 5)
                            dve.scalar_tensor_tensor(hf[:], g[:, slot, cols], SH / SG, act_a[:, c, :], ALU.mult, ALU.mult)
                            dve.drain().then_inc(h_temp, 1)
                            dve.tensor_copy(hh[:, m, cols], hf[:])
                            dve.drain()
                            dve.tensor_tensor(hl[:, m, cols], hf[:], hh[:, m, cols], ALU.subtract)
                            dve.drain().then_inc(h_ready, 1)
                        if not (last and m >= ROWS - 2):
                            low_u(e + 2, slot)
                        if from_u:
                            dve.wait_ge(gathered[slot], (i * 2 + m // 2) * 16 + 16)
                            dve.wait_ge(xb_loaded[slot], (i * 2 + m // 2) * 16 + 16)
                            dve.tensor_tensor_reduce(prod[:], fetched[:, slot], xb[:, slot], 1.0, 0.0, ALU.mult, ALU.add, dot[:, m:m + 1])
                            dve.drain().then_inc(fetched_used, 1)
                    if from_u:
                        dve.tensor_copy(av[:, bass.ds(i * ROWS, ROWS)], dot[:])
                        dve.drain()
                    else:
                        dve.wait_ge(acc_full, (i - HALF) + 1)
                        sums = acc[:].rearrange("p (c n) -> p c n", c=2)
                        dve.tensor_tensor(sums, ps[:, 6:8, :], sums, ALU.add)
                        dve.drain().then_inc(acc_read, 1)
                    if last:
                        dve.wait_ge(ys_full, 1)
                        row = y[0:SAMPLE, NB, :].rearrange("p (c n) -> p c n", c=2)
                        dve.scalar_tensor_tensor(row, ps[0:SAMPLE, 0:2, :], 1.0 / (SH * SV), row, ALU.mult, ALU.add)
                        statistics(SAMPLE, NB, 0)
                    dve.wait_ge(y_loaded, 64)
                    dve.wait_ge(place_loaded, 32)
                    for b in range(NB):
                        for d in range(2):
                            q = b * 2 + d
                            dve.wait_ge(y_full, i * (2 * NB) + q + 1)
                            part = y[:, b, d * 512:(d + 1) * 512]
                            dve.scalar_tensor_tensor(part, ps[:, 4 + q % YB, :], 1.0 / (SH * SV), part, ALU.mult,
                                                     ALU.add).then_inc(y_read, 1)
                        if last:
                            statistics(P, b, b + 1)
                            gain_of(SAMPLE if b == 0 else P, NB if b == 0 else b - 1, b)
                    if last:
                        gain_of(P, NB - 1, NB)

                def between():
                    dve.drain().then_inc(av_ready, 1)
                    dve.wait_ge(av_act, 1)
                    dve.scalar_tensor_tensor(hs[:], hs[:], SH, gate[:], ALU.mult, ALU.mult)
                    dve.drain()
                    dve.tensor_copy(hs_high[:], hs[:])
                    dve.wait_ge(sel_clear, 1)
                    dve.tensor_copy(sel[:, 0:(SAMPLE - 1) * (P + 1) + 1:P + 1], hs[:])
                    dve.drain()
                    dve.tensor_tensor(sel[:, SAMPLE:SAMPLE + (SAMPLE - 1) * (P + 1) + 1:P + 1], hs[:], hs_high[:], ALU.subtract)
                    dve.drain().then_inc(hs_ready, 1)

                over_turns(dve, body, between)


def build(nc, a):
    project_stage(nc, a)
    mix_prompt_stage(nc, a)
    with ExitStack() as stack:
        weights = MergeWeights(nc, stack, a)
        mix_sample_stage(nc, a, weights)
        merge_stage(nc, a, weights)
    route_stage(nc, a)
    experts_stage(nc, a)


class Arrays:
    pass


def shape_constants():
    dist = 2 * P - 1 - np.arange(TOEP)
    inside = (dist >= 0) & (dist < P)
    n = np.maximum(dist, 0)
    exact = BUCKETS // 2
    large = exact + (np.log(np.maximum(n, 1) / exact) / math.log(MAX_DISTANCE / exact) * (BUCKETS - exact)).astype(np.int32)
    bucket = np.where(n < exact, n, np.minimum(large, BUCKETS - 1))
    onehot = ((np.arange(BUCKETS)[:, None] == bucket[None]) & inside[None]).astype(np.float32)
    outside = np.broadcast_to(np.where(inside, 0.0, NEG).astype(np.float32), (HEADS, TOEP))
    return {
        "c_bucket": onehot,
        "c_outside": np.ascontiguousarray(outside),
        "c_ident": np.eye(P, dtype=np.float32),
        "c_fold": np.tile(np.eye(SAMPLE, dtype=np.float32), (2, 1)),
        "c_tril": np.triu(np.ones((P, P), np.float32)),
        "c_iota": np.broadcast_to(np.arange(KEYS, dtype=np.float16)[None, :, None], (P, KEYS, QT)).copy(),
        "c_iota16": np.broadcast_to(np.arange(TOPK, dtype=np.float32), (P, TOPK)).copy(),
    }


def laid_out(x_prompt, x_sample, cache_k_win, cache_v_win, p_prompt, p_sample, rel_bias_table, w_in, attn_sinks,
             w_att_out, c_ln_g, c_ln_b, c_ws, c_bs, w_chunk_out, w_o, ln1_g, ln1_b, peer_wq, peer_subkeys, peer_u,
             peer_v, w_ple_gate, w_ple_proj, ln2_g, ln2_b):
    def blocks(prompt, sample):
        w = prompt.shape[-1]
        rows = np.zeros(((NB + 1) * P, w), np.float32)
        rows[:PROMPT] = prompt.reshape(PROMPT, w)
        rows[PROMPT:T] = sample.reshape(SAMPLE, w)
        return rows.reshape(NB + 1, P, w)

    def by_feature(b):
        return b.reshape(NB + 1, P, -1, P).transpose(0, 3, 2, 1)

    def k_tiles(w):
        return w.reshape(-1, P, w.shape[-1]).transpose(1, 0, 2)

    def rows(v):
        return np.broadcast_to(v.reshape(1, -1), (P, v.size))

    heads = [g * REP + r for r in range(REP) for g in range(GROUPS)]
    q_cols = np.concatenate([np.arange(h * HD, (h + 1) * HD) for h in heads])
    w = w_in[0]
    x = blocks(x_prompt, x_sample)
    ws_sample = np.zeros((SAMPLE, CG, SAMPLE), np.float32)
    for b in range(SEQS):
        seq = slice(b * NEW, (b + 1) * NEW)
        ws_sample[seq, :, seq] = c_ws[0][:, :NEW, :NEW].transpose(2, 0, 1)
    sinks = attn_sinks[0].reshape(1, GROUPS, REP, 1, 1).transpose(0, 2, 3, 4, 1)
    sink_sample = np.broadcast_to(sinks, (4, REP, NEW, SEQS // 4, GROUPS)).reshape(P, SEQS // 4, GROUPS)
    return {
        "ws_sample": ws_sample,
        "sink_sample": sink_sample,
        "bs_sample": np.tile(c_bs[0][:, :NEW].T, (SEQS, 1)),
        "x_blocks": x,
        "xt_blocks": by_feature(x),
        "pt_blocks": by_feature(blocks(p_prompt[0], p_sample[0])),
        "rel_bias_table": rel_bias_table,
        "w_in": k_tiles(np.concatenate([w[:, q_cols], w[:, QW:]], axis=1)),
        "sink_rows": rows(attn_sinks),
        "w_merge": np.concatenate([k_tiles(v) for v in (w_att_out[0][q_cols], w_chunk_out[0], w_o[0], w_ple_proj[0],
                                                        w_ple_gate[0])], axis=1),
        "wq": k_tiles(peer_wq[0]),
        "subT": peer_subkeys[0].reshape(2 * PH, KEYS, P).transpose(2, 0, 1),
        "uT": peer_u[0].reshape(KEYS, KEYS, KT, P).transpose(0, 3, 2, 1),
        "u_rows": peer_u[0],
        "v": peer_v[0].reshape(KEYS, KEYS, D),
        "c_ln_g": rows(c_ln_g), "c_ln_b": rows(c_ln_b),
        "ln1_g": rows(ln1_g), "ln1_b": rows(ln1_b), "ln2_g": rows(ln2_g), "ln2_b": rows(ln2_b),
        "wsT": c_ws[0].transpose(2, 0, 1),
        "bsT": c_bs[0].T,
        "cache_kT": cache_k_win[0].transpose(2, 3, 0, 1).reshape(KVW, SEQS, P),
        "cache_v": cache_v_win[0].reshape(SEQS, P, KVW).transpose(1, 0, 2),
        "cache_k_rows": cache_k_win[0].reshape(SEQS, P, KVW),
        "cache_v_rows": cache_v_win[0].reshape(SEQS, P, KVW),
    }


OUTPUTS = {
    "y_prompt": (PROMPT, D), "y_sample": (SAMPLE, D), "k_prompt": (P, KVW), "v_prompt": (P, KVW),
    "k_sample": (SEQS, P, KVW), "v_sample": (SEQS, P, KVW), "chunk_v": (SAMPLE, CW),
}
SCRATCH = {
    "rev": ((HEADS, P, TOEP), F32),
    "z": ((NB + 2, P, ZW), F32),
    "yT": ((NB + 1, P, 8, P), F32),
    "x1T": ((NB + 1, P, KT, P), F32),
    "xh": ((P, KT, (NB + 1) * P), F16), "xl": ((P, KT, (NB + 1) * P), F16),
    "base": ((NB + 1, P, D), F32), "x1_sample": ((SAMPLE, D), F32),
    "g": ((KEYS, KEYS, PROMPT), F32),
    "place": ((P, SAMPLE), U32), "gate": ((P, SAMPLE), F32),
}
SHAPES = {
    "y_prompt": (1, PROMPT, D), "y_sample": (SEQS, NEW, D),
    "k_prompt": (1, 1, P, GROUPS, HD), "v_prompt": (1, 1, P, GROUPS, HD),
    "k_sample": (1, SEQS, P, GROUPS, HD), "v_sample": (1, SEQS, P, GROUPS, HD),
    "chunk_v": (1, SEQS, NEW, CW),
}


def kernel(**inputs):
    import concourse.bacc as bacc
    from concourse.bass_utils import run_bass_kernel_spmd

    nc = bacc.Bacc("TRN2", target_bir_lowering=False, num_devices=1)
    arrays = {**shape_constants(), **laid_out(**{k: np.asarray(v) for k, v in inputs.items()})}
    arrays = {f"in_{k}": np.ascontiguousarray(v) for k, v in arrays.items()}
    a = Arrays()
    for k, v in arrays.items():
        a.__dict__[k[3:]] = nc.dram_tensor(k, v.shape, mybir.dt.from_np(v.dtype), kind="ExternalInput").ap()
    for k, shape in OUTPUTS.items():
        a.__dict__[k] = nc.dram_tensor(f"out_{k}", shape, F32, kind="ExternalOutput").ap()
    for k, (shape, dt) in SCRATCH.items():
        a.__dict__[k] = nc.dram_tensor(f"scratch_{k}", shape, dt, kind="Internal").ap()
    build(nc, a)
    r = run_bass_kernel_spmd(nc, [arrays], core_ids=[0])
    return tuple(r.results[0][f"out_{k}"].reshape(SHAPES[k]) for k in OUTPUTS)
```
